# Optimizing a Trainium2 kernel written in Bass

```python
import jax
import jax.numpy as jnp
from jax import lax
import numpy as np

D_MODEL = 2048
BATCH = 1
SEQ = 512
DEPTH = 1
DEC_BATCH = 8
DEC_SEQ = 1
PAST_LEN = 512
PAGE_SIZE = 128

N_BRANCH = 3
BRANCH_W = 1024
RET_HEADS = 4
RET_DK = 128
RET_DV = 256
RET_CHUNK = 128
RET_THETA = 10000.0
NSA_HEADS = 8
NSA_KV_HEADS = 2
HEAD_DIM = 128
CMP_BLOCK = 32
SEL_BLOCK = 64
SEL_TOPK = 4
WINDOW = 256
Q_BLOCK = 128
ROPE_THETA = 500000.0
ROPE_DIMS = HEAD_DIM // 4
N_MEM = 256
MEM_HEADS = 4
MEM_HEAD_DIM = 256
PEER_HEADS = 8
PEER_KEYS = 128
PEER_N = PEER_KEYS * PEER_KEYS
PEER_DKEY = 128
PEER_TOPK = 16
TOK_BLOCK = 128

EPS = 1e-6
NEG_INF = -1e30
FORCE = 1e4

RET_QK_W = RET_HEADS * RET_DK
RET_V_W = RET_HEADS * RET_DV
NSA_Q_W = NSA_HEADS * HEAD_DIM
NSA_KV_W = NSA_KV_HEADS * HEAD_DIM
MEM_W = MEM_HEADS * MEM_HEAD_DIM
IN_SIZES = (RET_QK_W, RET_QK_W, RET_V_W, RET_V_W, NSA_Q_W,
            NSA_KV_W, NSA_KV_W, NSA_KV_W, NSA_KV_W, NSA_KV_W, NSA_KV_W,
            NSA_HEADS * 3, MEM_W, N_BRANCH * D_MODEL)
IN_WIDTH = sum(IN_SIZES)

kernel_name = 'hybrid_retention_nsa_peer_step'

def rms_norm(x, g):
    xf = x.astype(jnp.float32)
    y = xf * lax.rsqrt(jnp.mean(xf * xf, axis=-1, keepdims=True) + EPS)
    return (y * g.astype(jnp.float32)).astype(x.dtype)

def rotary(x, pos, rot_dims, theta):
    half = rot_dims // 2
    inv = theta ** (-jnp.arange(half, dtype=jnp.float32) * 2.0 / rot_dims)
    ang = pos.astype(jnp.float32)[:, None] * inv[None, :]
    cos = jnp.cos(ang)[:, None, :]
    sin = jnp.sin(ang)[:, None, :]
    xf = x.astype(jnp.float32)
    x1 = xf[..., :half]
    x2 = xf[..., half:rot_dims]
    out = jnp.concatenate([x1 * cos - x2 * sin, x2 * cos + x1 * sin, xf[..., rot_dims:]], axis=-1)
    return out.astype(x.dtype)

def masked_softmax(s, mask):
    s = jnp.where(mask, s.astype(jnp.float32), NEG_INF)
    return jax.nn.softmax(s, axis=-1) * mask

def split_in(z):
    offs = np.cumsum(IN_SIZES)[:-1].tolist()
    return jnp.split(z, offs, axis=-1)

def retention_chunk(state, q, k, v, log_gamma):
    c = q.shape[1]
    i = jnp.arange(c, dtype=jnp.float32)
    rel = i[:, None] - i[None, :]
    decay = jnp.where(rel >= 0, jnp.exp(jnp.maximum(rel, 0.0)[None] * log_gamma[:, None, None]), 0.0)
    qf, kf, vf = q.astype(jnp.float32), k.astype(jnp.float32), v.astype(jnp.float32)
    inner = jnp.einsum('bihd,bjhd->bhij', qf, kf) * decay
    o = jnp.einsum('bhij,bjhe->bihe', inner, vf)
    cross_decay = jnp.exp((i[:, None] + 1.0) * log_gamma[None, :])[None, :, :, None]
    o = o + jnp.einsum('bihd,bhde->bihe', qf, state) * cross_decay
    k_dec = kf * jnp.exp((c - 1.0 - i)[:, None] * log_gamma[None, :])[None, :, :, None]
    new_state = jnp.exp(c * log_gamma)[None, :, None, None] * state + jnp.einsum('bjhd,bjhe->bhde', k_dec, vf)
    return new_state, o

def retention_branch(q, k, v, gate, pos, state0, gn):
    B, T = q.shape[:2]
    log_gamma = jnp.log1p(-(2.0 ** (-5.0 - jnp.arange(RET_HEADS, dtype=jnp.float32))))
    q = rotary(q, pos, RET_DK, RET_THETA)
    k = rotary(k, pos, RET_DK, RET_THETA) * (RET_DK ** -0.5)
    c = RET_CHUNK if T % RET_CHUNK == 0 else T
    nc = T // c

    def chunks(a):
        return a.reshape(B, nc, c, *a.shape[2:]).swapaxes(0, 1)

    def step(s, xs):
        return retention_chunk(s, xs[0], xs[1], xs[2], log_gamma)

    state, o = lax.scan(step, state0, (chunks(q), chunks(k), chunks(v)))
    o = o.swapaxes(0, 1).reshape(B, T, RET_HEADS, RET_DV)
    o = rms_norm(o, gn).astype(gate.dtype).reshape(B, T, RET_V_W)
    return o * jax.nn.silu(gate), state

def compress(rows, pos_emb, w):
    B, L, G, dh = rows.shape
    nb = L // CMP_BLOCK
    blocks = rows[:, :nb * CMP_BLOCK].reshape(B, nb, CMP_BLOCK, G, dh) + pos_emb[None, None, :, None, :]
    return jnp.einsum('bnlgd,lde->bnge', blocks, w)

def gather_blocks(blocks, idx):
    bt = blocks.transpose(0, 3, 1, 2, 4)
    b = jnp.arange(idx.shape[0])[:, None, None, None]
    g = jnp.arange(idx.shape[2])[None, None, :, None]
    return bt[b, g, idx]

def sel_attend(q, q_pos, idx, ksb, vsb):
    B, Q, G, Hg, dh = q.shape
    kg = gather_blocks(ksb, idx)
    vg = gather_blocks(vsb, idx)
    kpos = idx[..., None] * SEL_BLOCK + jnp.arange(SEL_BLOCK)
    mask = (kpos <= q_pos[None, :, None, None, None]).reshape(B, Q, G, 1, -1)
    s = jnp.einsum('bqghd,bqgnld->bqghnl', q, kg) * (HEAD_DIM ** -0.5)
    pr = masked_softmax(s.reshape(B, Q, G, Hg, -1), mask)
    return jnp.einsum('bqghk,bqgkd->bqghd', pr.astype(vg.dtype), vg.reshape(B, Q, G, -1, dh))

def win_attend(q, q_pos, kw, vw, kw_pos):
    s = jnp.einsum('bqghd,bkgd->bqghk', q, kw) * (HEAD_DIM ** -0.5)
    dist = q_pos[:, None] - kw_pos[None, :]
    mask = (dist >= 0) & (dist <= WINDOW) & (kw_pos[None, :] >= 0)
    pr = masked_softmax(s, mask[None, :, None, None, :])
    return jnp.einsum('bqghk,bkgd->bqghd', pr.astype(vw.dtype), vw)

def nsa_branch(q, q_pos, kc, vc, ks, vs, kw, vw, kw_pos, gates, p):
    B, Tq = q.shape[:2]
    Lk = kc.shape[1]
    hg = NSA_HEADS // NSA_KV_HEADS
    qg = q.reshape(B, Tq, NSA_KV_HEADS, hg, HEAD_DIM)
    ck = compress(kc, p['cmp_pos_k'], p['cmp_w_k'])
    cv = compress(vc, p['cmp_pos_v'], p['cmp_w_v'])
    nbc = ck.shape[1]
    s_c = jnp.einsum('bqghd,bngd->bqghn', qg, ck) * (HEAD_DIM ** -0.5)
    vis = (jnp.arange(nbc) + 1) * CMP_BLOCK - 1 <= q_pos[:, None]
    p_c = masked_softmax(s_c, vis[None, :, None, None, :])
    o_cmp = jnp.einsum('bqghn,bngd->bqghd', p_c.astype(cv.dtype), cv)
    nbs = -(-Lk // SEL_BLOCK)
    r = SEL_BLOCK // CMP_BLOCK
    imp = jnp.pad(p_c.sum(axis=3), ((0, 0), (0, 0), (0, 0), (0, nbs * r - nbc)))
    imp = imp.reshape(B, Tq, NSA_KV_HEADS, nbs, r).sum(-1)
    blk_id = jnp.arange(nbs)[None, :]
    valid = (blk_id * SEL_BLOCK <= q_pos[:, None])[None, :, None, :]
    forced = ((blk_id == 0) | (blk_id == q_pos[:, None] // SEL_BLOCK))[None, :, None, :]
    score = jnp.where(forced, FORCE, jnp.where(valid, imp, -FORCE))
    _, idx = lax.top_k(score, min(SEL_TOPK, nbs))
    pad_s = ((0, 0), (0, nbs * SEL_BLOCK - Lk), (0, 0), (0, 0))
    ksb = jnp.pad(ks, pad_s).reshape(B, nbs, SEL_BLOCK, NSA_KV_HEADS, HEAD_DIM)
    vsb = jnp.pad(vs, pad_s).reshape(B, nbs, SEL_BLOCK, NSA_KV_HEADS, HEAD_DIM)
    qb = Q_BLOCK if Tq % Q_BLOCK == 0 else Tq
    nq = Tq // qb
    lw = kw.shape[1] - (nq - 1) * qb

    def chunks(a):
        return a.reshape(B, nq, qb, *a.shape[2:]).swapaxes(0, 1)

    def block(args):
        i, q_b, pos_b, idx_b = args
        o_sel = sel_attend(q_b, pos_b, idx_b, ksb, vsb)
        kw_b = lax.dynamic_slice_in_dim(kw, i * qb, lw, axis=1)
        vw_b = lax.dynamic_slice_in_dim(vw, i * qb, lw, axis=1)
        kp_b = lax.dynamic_slice_in_dim(kw_pos, i * qb, lw, axis=0)
        o_win = win_attend(q_b, pos_b, kw_b, vw_b, kp_b)
        return o_sel, o_win

    o_sel, o_win = lax.map(block, (jnp.arange(nq), chunks(qg), q_pos.reshape(nq, qb), chunks(idx)))

    def unchunk(a):
        return a.swapaxes(0, 1).reshape(B, Tq, NSA_KV_HEADS, hg, HEAD_DIM)

    g = gates.reshape(B, Tq, NSA_KV_HEADS, hg, 3)
    o = g[..., 0:1] * o_cmp + g[..., 1:2] * unchunk(o_sel) + g[..., 2:3] * unchunk(o_win)
    return o.reshape(B, Tq, NSA_Q_W).astype(q.dtype)

def memory_kv(mem, p):
    B, M, _ = mem.shape
    mk, mv = jnp.split(rms_norm(mem, p['norm_mem']) @ p['w_mem_kv'], 2, axis=-1)
    mk = rms_norm(mk.reshape(B, M, MEM_HEADS, MEM_HEAD_DIM), p['mem_k_norm'])
    return mk, mv.reshape(B, M, MEM_HEADS, MEM_HEAD_DIM)

def mem_attend(q, mk, mv):
    s = jnp.einsum('bthd,bmhd->bhtm', q, mk).astype(jnp.float32) * (MEM_HEAD_DIM ** -0.5)
    pr = jax.nn.softmax(s, axis=-1).astype(mv.dtype)
    return jnp.einsum('bhtm,bmhd->bthd', pr, mv)

def peer(h, p):
    n = h.shape[0]
    tb = TOK_BLOCK if n % TOK_BLOCK == 0 else n

    def block(hb):
        q = (hb @ p['peer_wq']).reshape(tb, PEER_HEADS, 2, PEER_DKEY // 2)
        s = jnp.einsum('nhpk,hpek->nhpe', q, p['peer_subkeys']).astype(jnp.float32)
        v, ix = lax.top_k(s, PEER_TOPK)
        cand = (v[:, :, 0, :, None] + v[:, :, 1, None, :]).reshape(tb, PEER_HEADS, -1)
        cid = (ix[:, :, 0, :, None] * PEER_KEYS + ix[:, :, 1, None, :]).reshape(tb, PEER_HEADS, -1)
        sc, sel = lax.top_k(cand, PEER_TOPK)
        eid = jnp.take_along_axis(cid, sel, axis=-1)
        g = jax.nn.softmax(sc, axis=-1)
        u = p['peer_u'][eid]
        act = jax.nn.gelu(jnp.einsum('nd,nhkd->nhk', hb, u), approximate=False)
        w = (g * act.astype(jnp.float32)).astype(hb.dtype)
        return jnp.einsum('nhk,nhkd->nd', w, p['peer_v'][eid])

    return lax.map(block, h.reshape(n // tb, tb, -1)).reshape(n, -1)

def layer(x, pos0, mem_k, mem_v, ret_state0, past, p):
    B, T, _ = x.shape
    pos = pos0 + jnp.arange(T)
    h = rms_norm(x, p['norm_attn'])
    (rq, rk, rv, rg, nq, kc, vc, ks, vs, kw, vw, ng, mq, mg) = split_in(h @ p['w_in'])
    o_ret, ret_state = retention_branch(
        rq.reshape(B, T, RET_HEADS, RET_DK), rk.reshape(B, T, RET_HEADS, RET_DK),
        rv.reshape(B, T, RET_HEADS, RET_DV), rg, pos, ret_state0, p['ret_gn'])
    def kvh(a):
        return a.reshape(B, T, NSA_KV_HEADS, HEAD_DIM)

    def prep_k(a, g):
        return rotary(rms_norm(kvh(a), g), pos, ROPE_DIMS, ROPE_THETA)

    qn = rotary(rms_norm(nq.reshape(B, T, NSA_HEADS, HEAD_DIM), p['nsa_q_norm']), pos, ROPE_DIMS, ROPE_THETA)
    kc = prep_k(kc, p['nsa_k_norm'][0])
    ks = prep_k(ks, p['nsa_k_norm'][1])
    kw = prep_k(kw, p['nsa_k_norm'][2])
    vc, vs, vw = kvh(vc), kvh(vs), kvh(vw)
    if past is None:
        full = (kc, vc, ks, vs)
        pad = ((0, 0), (WINDOW, 0), (0, 0), (0, 0))
        wk, wv = jnp.pad(kw, pad), jnp.pad(vw, pad)
        wpos = jnp.arange(WINDOW + T) - WINDOW
        nbuf = min(WINDOW, T)
    else:
        full = tuple(jnp.concatenate([a_past, a], axis=1) for a_past, a in zip(past[:4], (kc, vc, ks, vs)))
        nbuf = past[4].shape[1]
        wk = jnp.concatenate([past[4], kw], axis=1)
        wv = jnp.concatenate([past[5], vw], axis=1)
        wpos = pos0 - nbuf + jnp.arange(nbuf + T)
    win_k_new, win_v_new = wk[:, -nbuf:], wv[:, -nbuf:]
    gates = jax.nn.sigmoid(ng.reshape(B, T, NSA_HEADS, 3))
    o_nsa = nsa_branch(qn, pos, full[0], full[1], full[2], full[3], wk, wv, wpos, gates, p)
    qm = rms_norm(mq.reshape(B, T, MEM_HEADS, MEM_HEAD_DIM), p['mem_q_norm'])
    o_mem = mem_attend(qm, mem_k, mem_v).reshape(B, T, MEM_W)
    branches = jnp.stack([o_ret.astype(x.dtype), o_nsa, o_mem.astype(x.dtype)], axis=2)
    up = jnp.einsum('btcw,cwd->btcd', branches, p['w_branch'])
    gate = jax.nn.sigmoid(mg.reshape(B, T, N_BRANCH, D_MODEL))
    x = x + jnp.einsum('btcd,btcd->btd', gate, up) @ p['w_out']
    x = x + peer(rms_norm(x, p['norm_ffn']).reshape(B * T, D_MODEL), p).reshape(B, T, D_MODEL)
    return x, (kc, vc, ks, vs, win_k_new, win_v_new, ret_state.astype(x.dtype))

def gather_pages(pool, page_table):
    g = pool[page_table]
    return g.reshape(g.shape[0], -1, *g.shape[3:])

def setup_inputs(seed: int = 0) -> dict:
    key = jax.random.key(seed)
    keys = iter(jax.random.split(key, 40))

    def nrm(shape, scale):
        return jax.random.normal(next(keys), shape, jnp.float32) * scale

    def gain(shape):
        return 1.0 + nrm(shape, 0.02)

    n_pages = PAST_LEN // PAGE_SIZE
    n_used = DEC_BATCH * n_pages
    n_pool = n_used + max(1, n_used // 4)
    page_table = jax.random.permutation(next(keys), n_pool)[:n_used].reshape(DEC_BATCH, n_pages).astype(jnp.int32)
    nbuf = min(WINDOW, PAST_LEN)
    pool = (DEPTH, n_pool, PAGE_SIZE, NSA_KV_HEADS, HEAD_DIM)
    winb = (DEPTH, DEC_BATCH, nbuf, NSA_KV_HEADS, HEAD_DIM)
    memc = (DEPTH, DEC_BATCH, N_MEM, MEM_HEADS, MEM_HEAD_DIM)
    d = D_MODEL
    return {
        'x_prompt': nrm((BATCH, SEQ, d), 1.0),
        'x_sample': nrm((DEC_BATCH, DEC_SEQ, d), 1.0),
        'cache_cmp_k': nrm(pool, 1.0),
        'cache_cmp_v': nrm(pool, 1.0),
        'cache_sel_k': nrm(pool, 1.0),
        'cache_sel_v': nrm(pool, 1.0),
        'cache_win_k': nrm(winb, 1.0),
        'cache_win_v': nrm(winb, 1.0),
        'state_ret': nrm((DEPTH, DEC_BATCH, RET_HEADS, RET_DK, RET_DV), 0.5),
        'cache_mem_k': nrm(memc, 1.0),
        'cache_mem_v': nrm(memc, 1.0),
        'page_table': page_table,
        'mem_prompt': nrm((BATCH, N_MEM, d), 1.0),
        'norm_attn': gain((DEPTH, d)),
        'w_in': nrm((DEPTH, d, IN_WIDTH), d ** -0.5),
        'ret_gn': gain((DEPTH, RET_HEADS, RET_DV)),
        'nsa_q_norm': gain((DEPTH, HEAD_DIM)),
        'nsa_k_norm': gain((DEPTH, 3, HEAD_DIM)),
        'cmp_pos_k': nrm((DEPTH, CMP_BLOCK, HEAD_DIM), 0.02),
        'cmp_pos_v': nrm((DEPTH, CMP_BLOCK, HEAD_DIM), 0.02),
        'cmp_w_k': nrm((DEPTH, CMP_BLOCK, HEAD_DIM, HEAD_DIM), (CMP_BLOCK * HEAD_DIM) ** -0.5),
        'cmp_w_v': nrm((DEPTH, CMP_BLOCK, HEAD_DIM, HEAD_DIM), (CMP_BLOCK * HEAD_DIM) ** -0.5),
        'norm_mem': gain((DEPTH, d)),
        'w_mem_kv': nrm((DEPTH, d, 2 * MEM_W), d ** -0.5),
        'mem_q_norm': gain((DEPTH, MEM_HEAD_DIM)),
        'mem_k_norm': gain((DEPTH, MEM_HEAD_DIM)),
        'w_branch': nrm((DEPTH, N_BRANCH, BRANCH_W, d), BRANCH_W ** -0.5),
        'w_out': nrm((DEPTH, d, d), d ** -0.5),
        'norm_ffn': gain((DEPTH, d)),
        'peer_wq': nrm((DEPTH, d, PEER_HEADS * PEER_DKEY), d ** -0.5),
        'peer_subkeys': nrm((DEPTH, PEER_HEADS, 2, PEER_KEYS, PEER_DKEY // 2), (PEER_DKEY // 2) ** -0.5),
        'peer_u': nrm((DEPTH, PEER_N, d), d ** -0.5),
        'peer_v': nrm((DEPTH, PEER_N, d), PEER_HEADS ** -0.5),
    }

def reference(x_prompt, x_sample, cache_cmp_k, cache_cmp_v, cache_sel_k, cache_sel_v, cache_win_k, cache_win_v,
              state_ret, cache_mem_k, cache_mem_v, page_table, mem_prompt, norm_attn, w_in, ret_gn, nsa_q_norm,
              nsa_k_norm, cmp_pos_k, cmp_pos_v, cmp_w_k, cmp_w_v, norm_mem, w_mem_kv, mem_q_norm, mem_k_norm,
              w_branch, w_out, norm_ffn, peer_wq, peer_subkeys, peer_u, peer_v):
    past_len = page_table.shape[1] * cache_cmp_k.shape[2]
    xp, xs = x_prompt, x_sample
    st_p, st_s = [], []
    for l in range(DEPTH):
        p = {'norm_attn': norm_attn[l], 'w_in': w_in[l], 'ret_gn': ret_gn[l], 'nsa_q_norm': nsa_q_norm[l],
             'nsa_k_norm': nsa_k_norm[l], 'cmp_pos_k': cmp_pos_k[l], 'cmp_pos_v': cmp_pos_v[l],
             'cmp_w_k': cmp_w_k[l], 'cmp_w_v': cmp_w_v[l], 'norm_mem': norm_mem[l], 'w_mem_kv': w_mem_kv[l],
             'mem_q_norm': mem_q_norm[l], 'mem_k_norm': mem_k_norm[l], 'w_branch': w_branch[l],
             'w_out': w_out[l], 'norm_ffn': norm_ffn[l], 'peer_wq': peer_wq[l],
             'peer_subkeys': peer_subkeys[l], 'peer_u': peer_u[l], 'peer_v': peer_v[l]}
        mem_k, mem_v = memory_kv(mem_prompt, p)
        ret0 = jnp.zeros((xp.shape[0], RET_HEADS, RET_DK, RET_DV), jnp.float32)
        xp, new_p = layer(xp, 0, mem_k, mem_v, ret0, None, p)
        st_p.append(new_p + (mem_k, mem_v))
        past = (gather_pages(cache_cmp_k[l], page_table), gather_pages(cache_cmp_v[l], page_table),
                gather_pages(cache_sel_k[l], page_table), gather_pages(cache_sel_v[l], page_table),
                cache_win_k[l], cache_win_v[l])
        xs, new_s = layer(xs, past_len, cache_mem_k[l], cache_mem_v[l], state_ret[l].astype(jnp.float32), past, p)
        st_s.append(new_s)

    def stacked(states, i):
        return jnp.stack([s[i] for s in states])

    return (xp, xs,
            stacked(st_p, 0), stacked(st_p, 1), stacked(st_p, 2), stacked(st_p, 3), stacked(st_p, 4),
            stacked(st_p, 5), stacked(st_p, 6), stacked(st_p, 7), stacked(st_p, 8),
            stacked(st_s, 0), stacked(st_s, 1), stacked(st_s, 2), stacked(st_s, 3), stacked(st_s, 4),
            stacked(st_s, 5), stacked(st_s, 6))


_drawn_inputs = setup_inputs


def setup_inputs(seed=0):
    import zlib

    import numpy as np

    out = dict(_drawn_inputs(seed))
    spreads = {}
    factors = {'ret_gn': 9.915,
     'nsa_q_norm': 5.518,
     'nsa_k_norm': 8.371,
     'cmp_pos_k': 200.0,
     'cmp_pos_v': 10.283,
     'norm_mem': 2.815,
     'mem_q_norm': 8.0,
     'mem_k_norm': 3.039,
     'norm_ffn': 10.037}
    for name, (base, spread) in spreads.items():
        noise = np.random.default_rng([zlib.crc32(name.encode()), seed]).standard_normal(out[name].shape)
        drawn = base * np.exp(spread * noise) if base else spread * noise
        out[name] = jnp.asarray(drawn.astype(out[name].dtype))
    for name, factor in factors.items():
        out[name] = (out[name] * factor).astype(out[name].dtype)
    return out
```

```python
from contextlib import ExitStack, contextmanager

import numpy as np
import concourse.bass as bass
import concourse.mybir as mybir

F32 = mybir.dt.float32
I32 = mybir.dt.int32
U32 = mybir.dt.uint32
ACT = mybir.ActivationFunctionType
ALU = mybir.AluOpType
AX = mybir.AxisListType

P = 128
D = 2048
KD = D // P
SEQ, NS = 512, 8
T = SEQ + NS
HALF = T // 2
TILES = SEQ // P
RH, RDV = 4, 256
NH, NG, HG = 8, 2, 4
PAST, PAGES, N_POOL = 512, 4, 40
CMP, NCMP = 32, 16
WIN = 256
NM, MH, MD = 256, 4, 256
PH, PK, TOPK = 8, 128, 16
PICKS = PH * TOPK
EPS = 1e-6
NEG = -1e30
FORCE = 1e4
C_RQ, C_RK, C_RV, C_RG, C_NQ, C_KV, C_NG, C_MQ, C_MG = 0, 512, 1024, 2048, 3072, 4096, 5632, 5656, 6680
ROWS = NS * NH


def host_constants():
    f = np.float32
    c = {}
    ident = np.eye(P, dtype=f)
    c["base"] = np.concatenate([ident, np.ones((P, P), f)], 1)
    pos = np.concatenate([np.arange(SEQ), np.full(NS, PAST)]).astype(f)

    def rope(rot, theta):
        half = rot // 2
        inv = (f(theta) ** (-np.arange(half, dtype=f) * f(2.0) / f(rot))).astype(f)
        ang = (pos[None, :] * inv[:, None]).astype(f)
        cos, sin = np.ones((P, T), f), np.zeros((P, T), f)
        cos[:half] = cos[half:rot] = np.cos(ang)
        sin[:half] = sin[half:rot] = np.sin(ang)
        swap = np.zeros((P, P), f)
        for p in range(half):
            swap[p + half, p] = -1.0
            swap[p, p + half] = 1.0
        return np.concatenate([swap, cos, sin], 1)

    c["rope_ret"] = rope(128, 10000.0)
    c["rope_nsa"] = rope(32, 500000.0)
    gamma = 1.0 - 2.0 ** (-5.0 - np.arange(RH))
    i = np.arange(P)
    s = 128.0 ** -0.5
    rel = i[None, :] - i[:, None]
    dec = np.stack([np.where(rel >= 0, g ** np.maximum(rel, 0), 0.0) * s for g in gamma], 1)
    cross = np.broadcast_to(np.stack([g ** (i + 1.0) for g in gamma])[None], (P, RH, P))
    kdec = np.stack([g ** (P - 1.0 - i) * s for g in gamma], 1)
    gc = np.broadcast_to((gamma ** P)[None], (P, RH))
    c["ret"] = np.concatenate([dec.reshape(P, -1), cross.reshape(P, -1), kdec, gc], 1).astype(f)
    q = np.arange(P)[:, None]
    x = np.arange(896)[None]
    causal = np.where(x - 384 <= q, 0.0, NEG)
    x = np.arange(384)[None]
    dist = q - (x - 256)
    winb = np.where((dist >= 0) & (dist <= WIN), 0.0, NEG)
    qpos = (np.arange(TILES)[None, :] * P + np.arange(P)[:, None])[:, :, None]
    vis = (np.arange(NCMP) + 1) * CMP - 1 <= qpos
    blk = np.arange(8)
    forced = (blk == 0) | (blk == qpos // 64)
    valid = blk * 64 <= qpos
    vmask = (valid & ~forced) * 1.0
    vadd = np.where(forced, FORCE, np.where(valid, 0.0, -FORCE))
    c["nsa"] = np.concatenate([causal, winb, np.where(vis, 0.0, NEG).reshape(P, -1), (vis * 1.0).reshape(P, -1),
                               vmask.reshape(P, -1), vadd.reshape(P, -1),
                               np.broadcast_to(np.arange(9.0)[None], (P, 9))], 1).astype(f)
    row = np.arange(ROWS)
    unit = row // HG
    colu = np.arange(NS * NG * NCMP) // NCMP
    own = unit[:, None] == colu[None]
    same = unit[:, None] == unit[None]
    gb = np.arange(NG * NS)
    mine = (unit[:, None] // NG == gb[None] % NS) & (unit[:, None] % NG == gb[None] // NS)
    vm = np.ones((ROWS, 9)); vm[:, 0] = vm[:, 8] = 0
    va = np.zeros((ROWS, 9)); va[:, 0] = va[:, 8] = FORCE
    c["smp"] = np.concatenate([np.where(own, 0.0, NEG), same * 1.0, mine * 1.0, vm, va,
                               np.broadcast_to(np.arange(9.0)[None], (ROWS, 9))], 1).astype(f)
    c["peer"] = np.broadcast_to(np.arange(16.0, dtype=f)[None], (P, 16)).copy()
    onehot = np.zeros((NS, NS, P), f)
    for b in range(NS):
        onehot[b, b] = 1.0
    c["onehot"] = onehot.reshape(NS, NS * P)
    return c


def rows2(ap, g0):
    return ap[:, g0, :, 0:HALF]


def halves(ap):
    return ap.rearrange("p (a b) -> p a b", a=2)


def new_sem(nc, es, name):
    s = es.enter_context(nc.semaphore(name))
    nc._stage_sems.append(s)
    return s


@contextmanager
def stage_block(nc):
    sems, nc._stage_sems = nc._stage_sems, []
    with nc.Block() as block:
        yield block
    for s in sems:
        nc.gpsimd.sem_clear(s)
    nc.all_engine_barrier()


class Net:
    pass


def stage_load_consts(nc, n):
    with ExitStack() as es:
        n.s_base = new_sem(nc, es, "base_loaded")
        block = es.enter_context(stage_block(nc))

        @block.sync
        def _(sp):
            sp.dma_start(n.base[:, :], n.c["base"]).then_inc(n.s_base, 16)
            sp.dma_start(n.table[:, :], n.i["page_table"].rearrange("(o b) g -> o (b g)", o=1)).then_inc(n.s_base, 16)
            sp.wait_ge(n.s_base, 32)

        @block.gpsimd
        def _(pool):
            nc.gpsimd.memset(n_eps(nc)[:, :], EPS)


def stage_norm(nc, tag, tiles, gain, hT, ident, keep=None):
    with ExitStack() as es:
        xt = es.enter_context(nc.sbuf_tensor(tag + "_x", [P, 2, D], F32))
        sq = es.enter_context(nc.sbuf_tensor(tag + "_sq", [P, D], F32))
        gcol = es.enter_context(nc.sbuf_tensor(tag + "_g", [P, KD], F32))
        st = es.enter_context(nc.sbuf_tensor(tag + "_st", [P, 2, 3], F32))
        grow = es.enter_context(nc.sbuf_tensor(tag + "_gr", [P, D], F32)) if keep is not None else None
        ps = es.enter_context(nc.psum_tensor(tag + "_ps", [P, 2, 4, 512], F32))
        loaded = [new_sem(nc, es, f"{tag}_loaded{i}") for i in range(2)]
        g_loaded = new_sem(nc, es, tag + "_g_loaded")
        root_done = new_sem(nc, es, tag + "_root_done")
        scaled = new_sem(nc, es, tag + "_scaled")
        turned = new_sem(nc, es, tag + "_turned")
        saved = new_sem(nc, es, tag + "_saved")
        block = es.enter_context(stage_block(nc))

        @block.sync
        def _(sp):
            sp.dma_start(gcol[:, :], gain.rearrange("(k p) -> p k", p=P), allow_slow_non_contiguous=True).then_inc(g_loaded, 16)
            if keep is not None:
                sp.dma_start(grow[:, :], gain.rearrange("(o d) -> o d", o=1).to_broadcast([P, D])).then_inc(g_loaded, 16)
            for i, (src, rows, _c) in enumerate(tiles):
                if i >= 2:
                    sp.wait_ge(turned, i - 1)
                sp.dma_start(xt[0:rows, i % 2, :], src).then_inc(loaded[i % 2], 16)

        @block.scalar
        def _(act):
            for i, (_s, rows, _c) in enumerate(tiles):
                act.wait_ge(loaded[i % 2], 16 * (i // 2 + 1))
                nc.scalar.activation(sq[0:rows, :], xt[0:rows, i % 2, :], ACT.Square,
                                     accum_out=st[0:rows, i % 2, 0:1])
                act.drain()
                nc.scalar.activation(st[0:rows, i % 2, 1:2], st[0:rows, i % 2, 0:1], ACT.Sqrt,
                                     scale=1.0 / D, bias=n_eps(nc)[0:rows, :]).then_inc(root_done, 1)

        @block.vector
        def _(dve):
            dve.wait_ge(g_loaded, 16 if keep is None else 32)

            def scale(i):
                rows = tiles[i][1]
                dve.wait_ge(root_done, i + 1)
                nc.vector.reciprocal(st[0:rows, i % 2, 2:3], st[0:rows, i % 2, 1:2])
                dve.drain()
                if keep is not None:
                    nc.vector.scalar_tensor_tensor(keep[0:rows, i, :], xt[0:rows, i % 2, :], st[0:rows, i % 2, 2:3],
                                                   grow[0:rows, :], ALU.mult, ALU.mult)
                nc.vector.tensor_scalar(xt[0:rows, i % 2, :], xt[0:rows, i % 2, :], st[0:rows, i % 2, 2:3], None,
                                        ALU.mult).then_inc(scaled, 1)

            scale(0)
            for i, (_s, rows, col) in enumerate(tiles):
                if i + 1 < len(tiles):
                    scale(i + 1)
                dve.wait_ge(turned, i + 1)
                for b in range(4):
                    last = nc.vector.tensor_tensor(
                        hT[:, 4 * b:4 * b + 4, col:col + rows],
                        ps[:, i % 2, b, :].rearrange("p (k t) -> p k t", k=4)[:, :, 0:rows],
                        gcol[:, 4 * b:4 * b + 4].unsqueeze(2).to_broadcast([P, 4, rows]), ALU.mult)
                last.then_inc(saved, 1)

        @block.tensor
        def _(pe):
            for i, (_s, rows, _c) in enumerate(tiles):
                pe.wait_ge(scaled, i + 1)
                if i >= 2:
                    pe.wait_ge(saved, i - 1)
                for k in range(KD):
                    last = nc.tensor.transpose(ps[:, i % 2, k // 4, (k % 4) * P:(k % 4) * P + rows],
                                               xt[0:rows, i % 2, k * P:(k + 1) * P], ident[0:rows, 0:rows])
                last.then_inc(turned, 1)


def n_eps(nc):
    return nc._eps_tile


def stage_project(nc, tag, w, col0, nblk, src, dst, dst0, nk=KD, cols=T):
    parts = 2 if cols > 512 else 1
    half = cols // parts
    with ExitStack() as es:
        wt = es.enter_context(nc.sbuf_tensor(tag + "_w", [P, 2, nk, P], F32))
        ps = es.enter_context(nc.psum_tensor(tag + "_ps", [P, 2, parts, 512], F32))
        loaded = [new_sem(nc, es, f"{tag}_loaded{i}") for i in range(2)]
        ps_free = new_sem(nc, es, tag + "_ps_free")
        summed = new_sem(nc, es, tag + "_summed")
        block = es.enter_context(stage_block(nc))

        @block.sync
        def _(sp):
            def load(s, i):
                sp.dma_start(wt[:, s, :, :],
                             w[:, bass.ds(i * (2 * P) + (col0 + s * P), P)].rearrange("(k p) n -> p k n", p=P)
                             ).then_inc(loaded[s], 16)

            load(0, 0)
            load(1, 0)
            if nblk > 2:
                with sp.Fori(0, nblk // 2 - 1) as i:
                    for s in range(2):
                        sp.wait_ge(summed, i * 2 + (s + 1))
                        load(s, i + 1)

        @block.tensor
        def _(pe):
            with pe.Fori(0, nblk // 2) as i:
                for s in range(2):
                    pe.wait_ge(loaded[s], i * 16 + 16)
                    pe.wait_ge(ps_free, i * 2 + (s + 1))
                    for k in range(nk):
                        for h in range(parts):
                            last = nc.tensor.matmul(ps[:, s, h, 0:half], wt[:, s, k, :],
                                                    src[:, k, h * half:(h + 1) * half],
                                                    start=(k == 0), stop=(k == nk - 1))
                    last.then_inc(summed, 1)

        @block.scalar
        def _(act):
            act.sem_inc(ps_free, 2)
            with act.Fori(0, nblk // 2) as i:
                for s in range(2):
                    act.wait_ge(summed, i * 2 + (s + 1))
                    nc.scalar.copy(dst[:, bass.ds(i * 2 + (dst0 + s), 1), :].rearrange("p o (a b) -> p (o a) b", a=parts),
                                   ps[:, s, :, 0:half]).then_inc(ps_free, 1)


def stage_rope(nc, tag, Z, ranges, table, ones, norm_gain=None, gain_of=None):
    count = sum(b - a for a, b in ranges)
    with ExitStack() as es:
        tab = es.enter_context(nc.sbuf_tensor(tag + "_tab", [P, P + 2 * T], F32))
        sq = es.enter_context(nc.sbuf_tensor(tag + "_sq", [P, T], F32))
        ro = es.enter_context(nc.sbuf_tensor(tag + "_ro", [P, T], F32))
        ps = es.enter_context(nc.psum_tensor(tag + "_ps", [P, 2, 2, 512], F32))
        loaded = new_sem(nc, es, tag + "_loaded")
        squared = new_sem(nc, es, tag + "_squared")
        summed = new_sem(nc, es, tag + "_summed")
        rooted = new_sem(nc, es, tag + "_rooted")
        normed = new_sem(nc, es, tag + "_normed")
        swapped = new_sem(nc, es, tag + "_swapped")
        turned = new_sem(nc, es, tag + "_turned")
        if norm_gain is not None:
            gn = es.enter_context(nc.sbuf_tensor(tag + "_gn", [P, len(norm_gain)], F32))
        block = es.enter_context(stage_block(nc))
        loads = 1 + (len(norm_gain) if norm_gain is not None else 0)
        cos, sin = tab[:, P:P + T], tab[:, P + T:P + 2 * T]

        @block.sync
        def _(sp):
            sp.dma_start(tab[:, :], table).then_inc(loaded, 16)
            for g, gain in enumerate(norm_gain or ()):
                sp.dma_start(gn[:, g:g + 1], gain.rearrange("(p o) -> p o", o=1), allow_slow_non_contiguous=True).then_inc(loaded, 16)

        def blocks():
            base = 0
            for r, (a, b) in enumerate(ranges):
                yield a, b, base, (gain_of[r] if gain_of else 0)
                base += b - a

        @block.scalar
        def _(act):
            if norm_gain is None:
                return
            for a, b, base, _g in blocks():
                with act.Fori(0, b - a) as j:
                    nc.scalar.activation(sq[:, :], Z[:, bass.ds(j + a, 1), :].rearrange("p o t -> p (o t)"),
                                         ACT.Square).then_inc(squared, 1)
                    act.wait_ge(summed, j + (base + 1))
                    nc.scalar.activation(halves(sq[:, :]), rows2(ps, 0), ACT.Sqrt, scale=1.0 / P,
                                         bias=n_eps(nc)[:, :]).then_inc(rooted, 1)
                    act.wait_ge(normed, j + (base + 1))

        @block.tensor
        def _(pe):
            pe.wait_ge(loaded, 16 * loads)
            for a, b, base, _g in blocks():
                with pe.Fori(0, b - a) as j:
                    if norm_gain is not None:
                        pe.wait_ge(squared, j + (base + 1))
                        for h in range(2):
                            last = nc.tensor.matmul(ps[:, 0, h, 0:HALF], ones, sq[:, h * HALF:(h + 1) * HALF],
                                                    start=True, stop=True)
                        last.then_inc(summed, 1)
                    pe.wait_ge(normed, j + (base + 1))
                    for h in range(2):
                        last = nc.tensor.matmul(ps[:, 1, h, 0:HALF], tab[:, 0:P],
                                                Z[:, bass.ds(j + a, 1), h * HALF:(h + 1) * HALF].rearrange("p o t -> p (o t)"),
                                                start=True, stop=True)
                    last.then_inc(swapped, 1)

        @block.vector
        def _(dve):
            dve.wait_ge(loaded, 16 * loads)
            for a, b, base, g in blocks():
                with dve.Fori(0, b - a) as j:
                    z = Z[:, bass.ds(j + a, 1), :].rearrange("p o t -> p (o t)")
                    if norm_gain is not None:
                        dve.wait_ge(rooted, j + (base + 1))
                        nc.vector.reciprocal(ro[:, :], sq[:, :])
                        dve.drain()
                        nc.vector.scalar_tensor_tensor(z, z, gn[:, g:g + 1], ro[:, :], ALU.mult,
                                                       ALU.mult).then_inc(normed, 1)
                    else:
                        dve.sem_inc(normed, 1)
                    dve.wait_ge(swapped, j + (base + 1))
                    nc.vector.tensor_tensor(halves(ro[:, :]), rows2(ps, 1), halves(sin), ALU.mult)
                    nc.vector.tensor_tensor(z, z, cos, ALU.mult)
                    dve.drain()
                    nc.vector.tensor_tensor(z, z, ro[:, :], ALU.add).then_inc(turned, 1)
                    dve.drain()


def stage_rows(nc, tag, Z, b0, nblk, ident, rows, srows):
    with ExitStack() as es:
        zs = es.enter_context(nc.sbuf_tensor(tag + "_zs", [P, T], F32))
        ps = es.enter_context(nc.psum_tensor(tag + "_ps", [P, 2, 512], F32))
        staged = new_sem(nc, es, tag + "_staged")
        turned = new_sem(nc, es, tag + "_turned")
        saved = new_sem(nc, es, tag + "_saved")
        block = es.enter_context(stage_block(nc))

        @block.scalar
        def _(act):
            act.sem_inc(saved, 1)
            with act.Fori(0, nblk) as j:
                act.wait_ge(saved, j + 1)
                nc.scalar.copy(zs[:, :], Z[:, bass.ds(j + b0, 1), :].rearrange("p o t -> p (o t)")).then_inc(staged, 1)

        @block.tensor
        def _(pe):
            with pe.Fori(0, nblk) as j:
                pe.wait_ge(staged, j + 1)
                for t in range(TILES):
                    nc.tensor.transpose(ps[:, 0, t * P:(t + 1) * P], zs[:, t * P:(t + 1) * P], ident)
                nc.tensor.transpose(ps[0:NS, 1, 0:P], zs[:, SEQ:T], ident).then_inc(turned, 1)

        @block.vector
        def _(dve):
            with dve.Fori(0, nblk) as j:
                dve.wait_ge(turned, j + 1)
                nc.vector.tensor_copy(srows[:, bass.ds(j, 1), :].rearrange("p o t -> p (o t)"), ps[0:NS, 1, 0:P])
                nc.vector.tensor_copy(rows[:, bass.ds(j, 1), :, :].rearrange("p o t d -> p (o t) d"),
                                      ps[:, 0, :].rearrange("p (t d) -> p t d", d=P)).then_inc(saved, 1)


def stage_retention(nc, tag, n, Z, oT, p_ret):
    with ExitStack() as es:
        sb = lambda name, shape: es.enter_context(nc.sbuf_tensor(f"{tag}_{name}", shape, F32))
        sem = lambda name: new_sem(nc, es, f"{tag}_{name}")
        con = sb("con", [P, 1024 + 8])
        ks, vs, qd = sb("ks", [P, SEQ]), sb("vs", [P, 2, SEQ]), sb("qd", [P, SEQ])
        vt, kt, at = sb("vt", [P, RDV]), sb("kt", [P, P]), sb("at", [P, P])
        state = sb("state", [P, RDV])
        ps_v = es.enter_context(nc.psum_tensor(tag + "_psv", [P, 512], F32))
        ps_i = es.enter_context(nc.psum_tensor(tag + "_psi", [P, 512], F32))
        ps_o = es.enter_context(nc.psum_tensor(tag + "_pso", [P, 2, 512], F32))
        ps_s = es.enter_context(nc.psum_tensor(tag + "_pss", [P, 512], F32))
        loaded, staged, scored, rowed, summed, updated, head_done, stored = (
            sem("loaded"), sem("staged"), sem("scored"), sem("rowed"), sem("summed"), sem("updated"),
            sem("head_done"), sem("stored"))
        block = es.enter_context(stage_block(nc))
        dec, cross = con[:, 0:512], con[:, 512:1024]
        kdec, gc = con[:, 1024:1028], con[:, 1028:1032]

        @block.sync
        def _(sp):
            sp.dma_start(con[:, :], n.c["ret"]).then_inc(loaded, 16)
            with sp.Fori(0, RH) as h:
                sp.wait_ge(head_done, h + 1)
                sp.dma_start(p_ret[bass.ds(h, 1), :, :].rearrange("o d e -> d (o e)"), state[:, :]).then_inc(stored, 16)
            sp.wait_ge(stored, 16 * RH)

        @block.scalar
        def _(act):
            with act.Fori(0, RH) as h:
                nc.scalar.copy(ks[:, :], Z[:, bass.ds(h + 4, 1), 0:SEQ].rearrange("p o t -> p (o t)"))
                nc.scalar.copy(vs[:, :, :], Z[:, bass.ds(h * 2 + 8, 2), 0:SEQ]).then_inc(staged, 1)
                act.wait_ge(summed, h * TILES + TILES)

        @block.tensor
        def _(pe):
            with pe.Fori(0, RH) as h:
                pe.wait_ge(staged, h + 1)
                for c in range(TILES):
                    cc = slice(c * P, (c + 1) * P)
                    for e in range(2):
                        nc.tensor.transpose(ps_v[:, e * P:(e + 1) * P], vs[:, e, cc], n.ident)
                    nc.tensor.transpose(ps_v[:, 256:384], ks[:, cc], n.ident)
                    nc.tensor.matmul(ps_i[:, 0:P], ks[:, cc], Z[:, bass.ds(h, 1), cc].rearrange("p o t -> p (o t)"),
                                     start=True, stop=True).then_inc(scored, 1)
                    pe.wait_ge(rowed, h * TILES + (c + 1))
                    for e in range(2):
                        nc.tensor.matmul(ps_o[:, e, 0:P], vt[:, e * P:(e + 1) * P], at[:, :], start=True, stop=(c == 0))
                        if c:
                            nc.tensor.matmul(ps_o[:, e, 0:P], state[:, e * P:(e + 1) * P], qd[:, cc],
                                             start=False, stop=True)
                    nc.tensor.matmul(ps_s[:, 0:RDV], kt[:, :], vt[:, :], start=True, stop=True).then_inc(summed, 1)
                    pe.wait_ge(updated, h * TILES + (c + 1))

        @block.vector
        def _(dve):
            dve.wait_ge(loaded, 16)
            with dve.Fori(0, RH) as h:
                nc.vector.tensor_tensor(
                    qd[:, :].rearrange("p (c t) -> p c t", c=TILES),
                    Z[:, bass.ds(h, 1), 0:SEQ].rearrange("p o (c t) -> p (o c) t", c=TILES),
                    cross[:, bass.ds(h * P, P)].unsqueeze(1).to_broadcast([P, TILES, P]), ALU.mult)
                for c in range(TILES):
                    dve.wait_ge(scored, h * TILES + (c + 1))
                    nc.vector.tensor_copy(vt[:, :], ps_v[:, 0:256])
                    nc.vector.tensor_scalar(kt[:, :], ps_v[:, 256:384], kdec[:, bass.ds(h, 1)], None, ALU.mult)
                    nc.vector.tensor_tensor(at[:, :], ps_i[:, 0:P], dec[:, bass.ds(h * P, P)], ALU.mult).then_inc(rowed, 1)
                    dve.wait_ge(summed, h * TILES + (c + 1))
                    nc.vector.tensor_copy(oT[:, bass.ds(h * 2, 2), c * P:(c + 1) * P], ps_o[:, :, 0:P])
                    if c == 0:
                        last = nc.vector.tensor_copy(state[:, :], ps_s[:, 0:RDV])
                    else:
                        last = nc.vector.scalar_tensor_tensor(state[:, :], state[:, :], gc[:, bass.ds(h, 1)],
                                                              ps_s[:, 0:RDV], ALU.mult, ALU.add)
                    last.then_inc(updated, 1)
                    dve.drain()
                dve.sem_inc(head_done, 1)
                dve.wait_ge(stored, h * 16 + 16)


def stage_retention_sample(nc, tag, n, Z, oT, state_in, s_ret):
    gamma = [1.0 - 2.0 ** (-5.0 - h) for h in range(RH)]
    with ExitStack() as es:
        sb = lambda name, shape: es.enter_context(nc.sbuf_tensor(f"{tag}_{name}", shape, F32))
        sem = lambda name: new_sem(nc, es, f"{tag}_{name}")
        ktok, vtok, kone = sb("ktok", [NS, RH, P]), sb("vtok", [NS, RH, RDV]), sb("kone", [NS, RH, P])
        st = sb("st", [P, RH, RDV])
        new = sb("new", [P, RH, RDV])
        ps_t = es.enter_context(nc.psum_tensor(tag + "_pst", [P, 2, 512], F32))
        ps_k = es.enter_context(nc.psum_tensor(tag + "_psk", [P, RH * RDV], F32))
        ps_o = es.enter_context(nc.psum_tensor(tag + "_pso", [P, 512], F32))
        turned, rowed, masked, outer, updated, summed, saved, loaded, stored = (
            sem("turned"), sem("rowed"), sem("masked"), sem("outer"), sem("updated"), sem("summed"), sem("saved"),
            sem("loaded"), sem("stored"))
        block = es.enter_context(stage_block(nc))

        def moved(x, b):
            return x[bass.ds(b, 1), :, :, :].rearrange("o h d e -> d (o h) e")

        @block.sync
        def _(sp):
            sp.dma_start(st[:, :, :], state_in[0].rearrange("h d e -> d h e")).then_inc(loaded, 16)
            with sp.Fori(0, NS - 1) as b:
                sp.wait_ge(updated, b + 1)
                sp.dma_start(moved(s_ret, b), new[:, :, :]).then_inc(stored, 16)
                sp.dma_start(st[:, :, :], moved(state_in, b + 1)).then_inc(loaded, 16)
            sp.wait_ge(updated, NS)
            sp.dma_start(s_ret[NS - 1].rearrange("h d e -> d h e"), new[:, :, :]).then_inc(stored, 16)
            sp.wait_ge(stored, 16 * NS)

        @block.tensor
        def _(pe):
            for h in range(RH):
                nc.tensor.transpose(ps_t[0:NS, 0, h * P:(h + 1) * P], Z[:, 4 + h, SEQ:T], n.ident)
            for i in range(4):
                nc.tensor.transpose(ps_t[0:NS, 1, i * P:(i + 1) * P], Z[:, 8 + i, SEQ:T], n.ident)
            for i in range(4):
                last = nc.tensor.transpose(ps_o[0:NS, i * P:(i + 1) * P], Z[:, 12 + i, SEQ:T], n.ident)
            last.then_inc(turned, 1)
            pe.wait_ge(rowed, 1)
            with pe.Fori(0, NS) as b:
                pe.wait_ge(masked, b + 1)
                for h in range(RH):
                    last = nc.tensor.matmul(ps_k[:, h * RDV:(h + 1) * RDV], kone[:, h, :], vtok[:, h, :],
                                            start=True, stop=True)
                last.then_inc(outer, 1)
                pe.wait_ge(updated, b + 1)
                for h in range(RH):
                    for e in range(2):
                        last = nc.tensor.matmul(ps_o[:, 2 * h + e:2 * h + e + 1], new[:, h, e * P:(e + 1) * P],
                                                Z[:, h, bass.ds(b + SEQ, 1)], start=True, stop=True)
                last.then_inc(summed, 1)

        @block.scalar
        def _(act):
            with act.Fori(0, NS) as b:
                act.wait_ge(summed, b + 1)
                nc.scalar.copy(oT[:, 0:8, bass.ds(b + SEQ, 1)].rearrange("p k o -> p (k o)"), ps_o[:, 0:8]).then_inc(saved, 1)

        @block.vector
        def _(dve):
            dve.wait_ge(turned, 1)
            nc.vector.tensor_scalar(ktok[:, :, :], ps_t[0:NS, 0, :].rearrange("p (h d) -> p h d", h=RH), P ** -0.5, None, ALU.mult)
            nc.vector.tensor_copy(vtok[:, 0:2, :], ps_t[0:NS, 1, :].rearrange("p (h d) -> p h d", h=2))
            nc.vector.tensor_copy(vtok[:, 2:4, :], ps_o[0:NS, :].rearrange("p (h d) -> p h d", h=2)).then_inc(rowed, 1)
            dve.drain()

            def mask_key(b):
                nc.vector.tensor_scalar(kone[:, :, :], ktok[:, :, :], n.ident[0:NS, bass.ds(b, 1)], None,
                                        ALU.mult).then_inc(masked, 1)

            def update():
                for h in range(RH):
                    last = nc.vector.scalar_tensor_tensor(new[:, h, :], st[:, h, :], gamma[h],
                                                          ps_k[:, h * RDV:(h + 1) * RDV], ALU.mult, ALU.add)
                last.then_inc(updated, 1)

            mask_key(0)
            dve.wait_ge(outer, 1)
            dve.wait_ge(loaded, 16)
            update()
            with dve.Fori(1, NS) as b:
                mask_key(b)
                dve.wait_ge(outer, b + 1)
                dve.wait_ge(loaded, b * 16 + 16)
                dve.wait_ge(summed, b)
                dve.wait_ge(stored, b * 16)
                dve.wait_ge(saved, b)
                update()


def stage_retention_gate(nc, tag, n, Z, oT, gain):
    with ExitStack() as es:
        sb = lambda name, shape: es.enter_context(nc.sbuf_tensor(f"{tag}_{name}", shape, F32))
        sem = lambda name: new_sem(nc, es, f"{tag}_{name}")
        gn, sq, ro, sg = sb("gn", [P, 8]), sb("sq", [P, 2, T]), sb("ro", [P, T]), sb("sg", [P, 2, T])
        ps = es.enter_context(nc.psum_tensor(tag + "_ps", [P, 2, 512], F32))
        loaded, squared, summed, rooted, gated = sem("loaded"), sem("squared"), sem("summed"), sem("rooted"), sem("gated")
        block = es.enter_context(stage_block(nc))

        @block.sync
        def _(sp):
            sp.dma_start(gn[:, :], gain.rearrange("h (e p) -> p (h e)", p=P), allow_slow_non_contiguous=True).then_inc(loaded, 16)

        @block.scalar
        def _(act):
            act.sem_inc(gated, 1)
            with act.Fori(0, RH) as h:
                act.wait_ge(gated, h + 1)
                nc.scalar.activation(sq[:, :, :], oT[:, bass.ds(h * 2, 2), :], ACT.Square).then_inc(squared, 1)
                nc.scalar.activation(sg[:, :, :], Z[:, bass.ds(h * 2 + 16, 2), :], ACT.Sigmoid)
                act.wait_ge(summed, h + 1)
                nc.scalar.activation(halves(sq[:, 0, :]), ps[:, :, 0:HALF], ACT.Sqrt, scale=1.0 / RDV,
                                     bias=n_eps(nc)[:, :]).then_inc(rooted, 1)

        @block.tensor
        def _(pe):
            with pe.Fori(0, RH) as h:
                pe.wait_ge(squared, h + 1)
                for half in range(2):
                    for e in range(2):
                        last = nc.tensor.matmul(ps[:, half, 0:HALF], n.ones, sq[:, e, half * HALF:(half + 1) * HALF],
                                                start=(e == 0), stop=(e == 1))
                last.then_inc(summed, 1)

        @block.vector
        def _(dve):
            dve.wait_ge(loaded, 16)
            with dve.Fori(0, RH) as h:
                dve.wait_ge(rooted, h + 1)
                nc.vector.reciprocal(ro[:, :], sq[:, 0, :])
                nc.vector.tensor_tensor(sg[:, :, :], sg[:, :, :], Z[:, bass.ds(h * 2 + 16, 2), :], ALU.mult)
                dve.drain()
                for e in range(2):
                    o = oT[:, bass.ds(h * 2 + e, 1), :].rearrange("p o t -> p (o t)")
                    nc.vector.scalar_tensor_tensor(o, o, gn[:, bass.ds(h * 2 + e, 1)], ro[:, :], ALU.mult, ALU.mult)
                dve.drain()
                nc.vector.tensor_tensor(oT[:, bass.ds(h * 2, 2), :], oT[:, bass.ds(h * 2, 2), :], sg[:, :, :],
                                        ALU.mult).then_inc(gated, 1)



def stage_gates(nc, tag, n, hT, w, gt, gts, scratch, grow):
    C = 3 * NH
    with ExitStack() as es:
        sem = lambda name: new_sem(nc, es, f"{tag}_{name}")
        wt = es.enter_context(nc.sbuf_tensor(tag + "_w", [P, KD, C], F32))
        ps = es.enter_context(nc.psum_tensor(tag + "_ps", [P, TILES + 1, C], F32))
        loaded, summed, gated, bounced = sem("loaded"), sem("summed"), sem("gated"), sem("bounced")
        block = es.enter_context(stage_block(nc))

        @block.sync
        def _(sp):
            sp.dma_start(wt[:, :, :], w[:, C_NG:C_NG + C].rearrange("(k p) n -> p k n", p=P)).then_inc(loaded, 16)
            sp.wait_ge(gated, 1)
            sp.dma_start(scratch, gts[:, :]).then_inc(bounced, 16)
            sp.wait_ge(bounced, 16)
            sp.dma_start(grow[:, :], scratch.rearrange("b (h c) -> (b h) c", c=3)).then_inc(bounced, 16)
            sp.wait_ge(bounced, 32)

        @block.tensor
        def _(pe):
            pe.wait_ge(loaded, 16)
            for t in range(TILES + 1):
                rows = P if t < TILES else NS
                for k in range(KD):
                    last = nc.tensor.matmul(ps[0:rows, t, :], hT[:, k, t * P:t * P + rows], wt[:, k, :],
                                            start=(k == 0), stop=(k == KD - 1))
            last.then_inc(summed, 1)

        @block.scalar
        def _(act):
            act.wait_ge(summed, 1)
            nc.scalar.activation(gt[:, :, :], ps[:, 0:TILES, :], ACT.Sigmoid)
            nc.scalar.activation(gts[:, :], ps[0:NS, TILES, :], ACT.Sigmoid).then_inc(gated, 1)


def stage_store_rows(nc, tag, n, rows, srows):
    with ExitStack() as es:
        stored = new_sem(nc, es, tag + "_stored")
        block = es.enter_context(stage_block(nc))
        names = ["cmp_k", "cmp_v", "sel_k", "sel_v", "win_k", "win_v"]

        @block.sync
        def _(sp):
            for m, name in enumerate(names):
                for g in range(NG):
                    t0 = TILES - WIN // P if m >= 4 else 0
                    sp.dma_start(n.o["p_" + name][0, 0, :, g, :].rearrange("(t p) d -> p t d", p=P),
                                 rows[:, 2 * m + g, t0:TILES, :]).then_inc(stored, 16)
                dst = n.o["s_" + name][0, :, WIN - 1 if m >= 4 else 0, :, :]
                sp.dma_start(dst, srows[:, 2 * m:2 * m + 2, :]).then_inc(stored, 16)
            for name in names[4:]:
                sp.dma_start(n.o["s_" + name][0, :, 0:WIN - 1, :, :].rearrange("b t g d -> b (t g d)"),
                             n.i["cache_" + name][0, :, 1:WIN, :, :].rearrange("b t g d -> b (t g d)")).then_inc(stored, 16)
            sp.wait_ge(stored, 16 * (3 * 6 + 2))


def stage_compress(nc, tag, n, Z, b0, pool, pos, w, ck):
    COLS = NG * NCMP * (1 + NS)
    LC = 4
    with ExitStack() as es:
        sb = lambda name, shape, dt=F32: es.enter_context(nc.sbuf_tensor(f"{tag}_{name}", shape, dt))
        sem = lambda name: new_sem(nc, es, f"{tag}_{name}")
        kc = sb("kc", [P, (COLS + 1) * CMP])
        page = sb("page", [P, PAGES, NG * P])
        wt = sb("w", [P, 2, LC, P])
        posn = sb("pos", [CMP, P])
        bias = sb("bias", [P, 1])
        ps_t = es.enter_context(nc.psum_tensor(tag + "_pst", [P, 2, 512], F32))
        ps_p = es.enter_context(nc.psum_tensor(tag + "_psp", [P, 512], F32))
        ps = es.enter_context(nc.psum_tensor(tag + "_ps", [P, 512], F32))
        pos_loaded, turned, saved, w_used, summed = (sem("pos_loaded"), sem("turned"), sem("saved"), sem("w_used"), sem("summed"))
        gathered = sem("gathered")
        loaded = [sem(f"loaded{i}") for i in range(PAGES)]
        w_loaded = [sem(f"w_loaded{i}") for i in range(2)]
        block = es.enter_context(stage_block(nc))

        @block.sync
        def _(sp):
            sp.dma_start(posn[:, :], pos).then_inc(pos_loaded, 16)

            def load(slot, index):
                number = sp.value_load(n.table[0:1, bass.ds(index, 1)], min_val=0, max_val=N_POOL - 1)
                sp.dma_start(page[:, slot, :], pool[bass.ds(number, 1), :, :, :].rearrange("o t g d -> t (o g d)")
                             ).then_inc(loaded[slot], 16)

            for pg in range(PAGES):
                load(pg, pg)
            with sp.Fori(0, NS - 1) as b:
                for pg in range(PAGES):
                    sp.wait_ge(turned, b * PAGES + (pg + 1))
                    load(pg, b * PAGES + (pg + PAGES))

        def load_weights(act):
            wv = w.rearrange("l d e -> d l e")
            for i in range(CMP // LC):
                if i >= 2:
                    act.wait_ge(w_used, i - 1)
                act.dma_start(wt[:, i % 2, :, :], wv[:, i * LC:(i + 1) * LC, :]).then_inc(w_loaded[i % 2], 16)

        @block.tensor
        def _(pe):
            pe.wait_ge(pos_loaded, 16)
            nc.tensor.transpose(ps_p[:, 0:CMP], posn[:, :], n.ident[0:CMP, 0:CMP])
            with pe.Fori(0, NS) as b:
                for pg in range(PAGES):
                    s = pg % 2
                    pe.wait_ge(loaded[pg], b * 16 + 16)
                    pe.wait_ge(saved, b * PAGES + (pg + 1))
                    for g in range(NG):
                        last = nc.tensor.transpose(ps_t[:, s, g * P:(g + 1) * P], page[:, pg, g * P:(g + 1) * P], n.ident)
                    last.then_inc(turned, 1)
            pe.wait_ge(gathered, 2)
            kv = kc[:, :].rearrange("p (c l) -> p c l", l=CMP)
            for l in range(CMP):
                i = l // LC
                if l % LC == 0:
                    pe.wait_ge(w_loaded[i % 2], 16 * (i // 2 + 1))
                last = nc.tensor.matmul(ps[:, 0:COLS + 1], wt[:, i % 2, l % LC, :], kv[:, :, l], start=(l == 0), stop=(l == CMP - 1))
                if l % LC == LC - 1:
                    last.then_inc(w_used, 1)

        @block.scalar
        def _(act):
            nc.scalar.copy(kc[:, 0:NG * SEQ].rearrange("p (g t) -> p g t", g=NG), Z[:, b0:b0 + 2, 0:SEQ]).then_inc(gathered, 1)
            load_weights(act)

        @block.vector
        def _(dve):
            dve.sem_inc(saved, 2)
            with dve.Fori(0, NS) as b:
                for pg in range(PAGES):
                    dve.wait_ge(turned, b * PAGES + (pg + 1))
                    nc.vector.tensor_copy(
                        kc[:, bass.ds(b * (NG * PAST) + NG * SEQ, NG * PAST)].rearrange("p (g t) -> p g t", g=NG)[:, :, pg * P:(pg + 1) * P],
                        ps_t[:, pg % 2, 0:NG * P].rearrange("p (g t) -> p g t", g=NG)).then_inc(saved, 1)
            nc.vector.tensor_copy(kc[:, COLS * CMP:(COLS + 1) * CMP], ps_p[:, 0:CMP]).then_inc(gathered, 1)
            dve.wait_ge(w_used, CMP // LC)
            nc.vector.tensor_copy(bias[:, :], ps[:, COLS:COLS + 1])
            dve.drain()
            nc.vector.tensor_scalar(ck[:, :], ps[:, 0:COLS], bias[:, :], None, ALU.add)


def stage_cv_rows(nc, tag, n, cv, cvp, cvs):
    with ExitStack() as es:
        ps = es.enter_context(nc.psum_tensor(tag + "_ps", [P, 512], F32))
        turned = new_sem(nc, es, tag + "_turned")
        block = es.enter_context(stage_block(nc))

        @block.tensor
        def _(pe):
            for g in range(NG):
                nc.tensor.transpose(ps[0:NCMP, g * P:(g + 1) * P], cv[:, g * NCMP:(g + 1) * NCMP], n.ident)
            for a in range(2):
                last = nc.tensor.transpose(ps[:, (2 + a) * P:(3 + a) * P], cv[:, 32 + a * P:32 + (a + 1) * P], n.ident)
            last.then_inc(turned, 1)

        @block.vector
        def _(dve):
            dve.wait_ge(turned, 1)
            nc.vector.tensor_copy(cvp[:, :, :], ps[0:NCMP, 0:256].rearrange("p (g d) -> p g d", g=2))
            nc.vector.tensor_copy(cvs[:, :, :], ps[:, 256:512].rearrange("p (g d) -> p g d", g=2))


def pick_blocks(nc, dve, score, v8, i8, if4, hit, sel, iota, nblk):
    nc.vector.max(v8, score)
    dve.drain()
    nc.vector.max_index(i8, v8, score)
    dve.drain()
    nc.vector.tensor_copy(if4, i8[:, 0:4])
    dve.drain()
    rows = score.shape[0]
    nc.vector.tensor_tensor(hit, iota.unsqueeze(2).to_broadcast([rows, nblk, 4]),
                            if4.unsqueeze(1).to_broadcast([rows, nblk, 4]), ALU.is_equal)
    dve.drain()
    nc.vector.tensor_reduce(sel, hit, AX.X, ALU.add)
    dve.drain()


def stage_nsa_group(nc, tag, n, g, Z, rows, ck, cvp, gt, oT):
    B_KS, B_KW, R_VS, R_VW = 12 + g, 16 + g, 6 + g, 10 + g
    with ExitStack() as es:
        sb = lambda name, shape, dt=F32: es.enter_context(nc.sbuf_tensor(f"{tag}_{name}", shape, dt))
        pb = lambda name, shape: es.enter_context(nc.psum_tensor(f"{tag}_{name}", shape, F32))
        sem = lambda name: new_sem(nc, es, f"{tag}_{name}")
        con = sb("con", [P, 896 + 384 + 64 + 64 + 32 + 32 + 9])
        qs = sb("qs", [P, SEQ])
        pc = sb("pc", [P, HG, TILES, NCMP])
        half = sb("half", [P, TILES, NCMP // 2])
        cm, cr = sb("cm", [P, TILES]), sb("cr", [P, TILES])
        imp, pcs = sb("imp", [P, TILES, 8]), sb("pcs", [P, TILES * NCMP])
        v8, i8, if4, hit, sel = sb("v8", [P, 8]), sb("i8", [P, 8], U32), sb("if4", [P, 4]), sb("hit", [P, 8, 4]), sb("sel", [P, 8])
        bias = sb("bias", [P, TILES, 512])
        sc = sb("sc", [P, 2, 896])
        mx, rs = sb("mx", [P, 2, 2]), sb("rs", [P, 2, 3])
        pcg = sb("pcg", [P, 2, NCMP])
        pt = sb("pt", [P, 8, P])
        ps_s, ps_w = pb("pss", [P, 2, 512]), pb("psw", [P, 2, 512])
        ps_t, ps_o = pb("pst", [P, 2, 512]), pb("pso", [P, 2, 512])
        loaded, q_staged, c_scored, c_biased, c_exped, c_done, mask_done = (
            sem("loaded"), sem("q_staged"), sem("c_scored"), sem("c_biased"), sem("c_exped"), sem("c_done"), sem("mask_done"))
        scored, biased, exped, weighted, turned, pt_saved, summed, o_saved, q_used = (
            sem("scored"), sem("biased"), sem("exped"), sem("weighted"), sem("turned"), sem("pt_saved"), sem("summed"),
            sem("o_saved"), sem("q_used"))
        block = es.enter_context(stage_block(nc))
        o = 0
        parts = {}
        for name, width in (("causal", 896), ("win", 384), ("cbias", 64), ("cmask", 64), ("vmask", 32), ("vadd", 32), ("iota", 9)):
            parts[name] = con[:, o:o + width]
            o += width

        def nsel(t):
            return (t + 1) * P

        def wtiles(t):
            return range(max(0, t - 2), t + 1)

        @block.sync
        def _(sp):
            sp.dma_start(con[:, :], n.c["nsa"]).then_inc(loaded, 16)

        def stage_q(act, h):
            nc.scalar.activation(qs[:, :], Z[:, bass.ds(h + g * HG, 1), 0:SEQ].rearrange("p o t -> p (o t)"), ACT.Copy,
                                 scale=P ** -0.5).then_inc(q_staged, 1)

        @block.scalar
        def _(act):
            with act.Fori(0, HG) as h:
                stage_q(act, h)
                act.wait_ge(c_biased, h + 1)
                p = pc[:, bass.ds(h, 1), :, :].rearrange("p o t c -> p (o t c)")
                nc.scalar.activation(p, p, ACT.Exp).then_inc(c_exped, 1)
                act.wait_ge(c_done, h + 1)
            with act.Fori(0, HG) as h:
                stage_q(act, h)

                def softmax(t):
                    s = t % 2
                    act.wait_ge(biased, h * TILES + (t + 1))
                    nc.scalar.activation(sc[:, s, 0:nsel(t)], sc[:, s, 0:nsel(t)], ACT.Exp, bias=mx[:, s, 0:1],
                                         accum_out=rs[:, s, 0:1])
                    w = len(wtiles(t)) * P
                    nc.scalar.activation(sc[:, s, 512:512 + w], sc[:, s, 512:512 + w], ACT.Exp, bias=mx[:, s, 1:2],
                                         accum_out=rs[:, s, 1:2]).then_inc(exped, 1)

                def save_pt(t):
                    act.wait_ge(turned, h * TILES + (t + 1))
                    nc.scalar.copy(pt[:, 0:t + 1, :], ps_t[:, 0, 0:nsel(t)].rearrange("p (k q) -> p k q", q=P))
                    w = len(wtiles(t))
                    nc.scalar.copy(pt[:, 4:4 + w, :], ps_t[:, 1, 0:w * P].rearrange("p (k q) -> p k q", q=P))
                    nc.scalar.copy(pt[0:NCMP, 7, :], ps_t[0:NCMP, 1, 384:512]).then_inc(pt_saved, 1)

                softmax(0)
                for t in range(TILES):
                    if t + 1 < TILES:
                        softmax(t + 1)
                    save_pt(t)

        @block.tensor
        def _(pe):
            with pe.Fori(0, HG) as h:
                pe.wait_ge(q_staged, h + 1)
                for t in range(TILES):
                    last = nc.tensor.matmul(ps_o[:, 0, t * NCMP:(t + 1) * NCMP], qs[:, t * P:(t + 1) * P],
                                            ck[:, g * NCMP:(g + 1) * NCMP], start=True, stop=True)
                last.then_inc(c_scored, 1)
            pe.wait_ge(mask_done, 1)
            with pe.Fori(0, HG) as h:
                pe.wait_ge(q_staged, h + (HG + 1))

                def scores(t):
                    qt = qs[:, t * P:(t + 1) * P]
                    nc.tensor.matmul(ps_s[:, t % 2, 0:nsel(t)], qt, Z[:, B_KS, 0:nsel(t)], start=True, stop=True)
                    w0, w1 = wtiles(t)[0] * P, nsel(t)
                    nc.tensor.matmul(ps_w[:, t % 2, 0:w1 - w0], qt, Z[:, B_KW, w0:w1], start=True, stop=True).then_inc(scored, 1)

                scores(0)
                for t in range(TILES):
                    if t + 1 < TILES:
                        scores(t + 1)
                    pe.wait_ge(weighted, h * TILES + (t + 1))
                    s = t % 2
                    for k in range(t + 1):
                        nc.tensor.transpose(ps_t[:, 0, k * P:(k + 1) * P], sc[:, s, k * P:(k + 1) * P], n.ident)
                    for k in range(len(wtiles(t))):
                        nc.tensor.transpose(ps_t[:, 1, k * P:(k + 1) * P], sc[:, s, 512 + k * P:512 + (k + 1) * P], n.ident)
                    nc.tensor.transpose(ps_t[0:NCMP, 1, 384:512], pcg[:, s, :], n.ident).then_inc(turned, 1)
                    pe.wait_ge(pt_saved, h * TILES + (t + 1))
                    po = ps_o[:, s, 0:P]
                    nc.tensor.matmul(po, cvp[:, g, :], pt[0:NCMP, 7, :], start=True, stop=False)
                    for k in range(t + 1):
                        nc.tensor.matmul(po, rows[:, R_VS, k, :], pt[:, k, :], start=False, stop=False)
                    for j, k in enumerate(wtiles(t)):
                        last = nc.tensor.matmul(po, rows[:, R_VW, k, :], pt[:, 4 + j, :], start=False, stop=(k == t))
                    last.then_inc(summed, 1)

        @block.vector
        def _(dve):
            dve.wait_ge(loaded, 16)
            with dve.Fori(0, HG) as h:
                p = pc[:, bass.ds(h, 1), :, :].rearrange("p o t c -> p (o t) c")
                spread = lambda x: x.unsqueeze(2).to_broadcast([P, TILES, NCMP])
                table = lambda name: parts[name].rearrange("p (t c) -> p t c", c=NCMP)
                dve.wait_ge(c_scored, h + 1)
                nc.vector.tensor_tensor(p, ps_o[:, 0, 0:64].rearrange("p (t c) -> p t c", c=NCMP), table("cbias"), ALU.add)
                dve.drain()
                nc.vector.tensor_reduce(cm[:, :], p, AX.X, ALU.max)
                dve.drain()
                nc.vector.tensor_tensor(p, p, spread(cm[:, :]), ALU.subtract).then_inc(c_biased, 1)
                dve.wait_ge(c_exped, h + 1)
                nc.vector.tensor_tensor(half[:, :, 0:8], p[:, :, 0:8], p[:, :, 8:16], ALU.add)
                dve.drain()
                for w in (4, 2, 1):
                    nc.vector.tensor_tensor(half[:, :, 0:w], half[:, :, 0:w], half[:, :, w:2 * w], ALU.add)
                    dve.drain()
                nc.vector.reciprocal(cr[:, :], half[:, :, 0])
                dve.drain()
                nc.vector.tensor_tensor(p, p, spread(cr[:, :]), ALU.mult)
                dve.drain()
                nc.vector.tensor_tensor(p, p, table("cmask"), ALU.mult).then_inc(c_done, 1)
                dve.drain()
            nc.vector.tensor_reduce(pcs[:, :], pc[:, :, :, :].rearrange("p h t c -> p (t c) h"), AX.X, ALU.add)
            dve.drain()
            nc.vector.tensor_reduce(imp[:, :, :].rearrange("p t b -> p (t b)"),
                                    pcs[:, :].rearrange("p (b r) -> p b r", r=2), AX.X, ALU.add)
            dve.drain()
            nc.vector.tensor_tensor(imp[:, :, :].rearrange("p t b -> p (t b)"), imp[:, :, :].rearrange("p t b -> p (t b)"),
                                    parts["vmask"], ALU.mult)
            dve.drain()
            nc.vector.tensor_tensor(imp[:, :, :].rearrange("p t b -> p (t b)"), imp[:, :, :].rearrange("p t b -> p (t b)"),
                                    parts["vadd"], ALU.add)
            dve.drain()
            for t in range(TILES):
                pick_blocks(nc, dve, imp[:, t, :], v8[:, :], i8[:, :], if4[:, :], hit[:, :, :], sel[:, :], parts["iota"][:, 0:8], 8)
                nc.vector.tensor_scalar(sel[:, :], sel[:, :], -NEG, NEG, ALU.mult, ALU.add)
                dve.drain()
                nc.vector.tensor_tensor(bias[:, t, :].rearrange("p (b k) -> p b k", k=64),
                                        sel[:, :].unsqueeze(2).to_broadcast([P, 8, 64]),
                                        parts["causal"][:, 384 - t * P:896 - t * P].rearrange("p (b k) -> p b k", k=64), ALU.add)
                dve.drain()
            dve.sem_inc(mask_done, 1)
            with dve.Fori(0, HG) as h:
                def bias_scores(t):
                    s = t % 2
                    dve.wait_ge(scored, h * TILES + (t + 1))
                    w = len(wtiles(t)) * P
                    nc.vector.tensor_tensor(sc[:, s, 0:nsel(t)], ps_s[:, s, 0:nsel(t)], bias[:, t, 0:nsel(t)], ALU.add)
                    nc.vector.tensor_tensor(sc[:, s, 512:512 + w], ps_w[:, s, 0:w], parts["win"][:, 384 - w:384], ALU.add)
                    dve.drain()
                    nc.vector.tensor_reduce(mx[:, s, 0:1], sc[:, s, 0:nsel(t)], AX.X, ALU.max, negate=True)
                    nc.vector.tensor_reduce(mx[:, s, 1:2], sc[:, s, 512:512 + w], AX.X, ALU.max, negate=True).then_inc(biased, 1)

                def weigh(t):
                    s = t % 2
                    w = len(wtiles(t)) * P
                    gate = lambda br: gt[:, t, bass.ds(h * 3 + (3 * HG * g + br), 1)]
                    nc.vector.tensor_scalar(pcg[:, s, :], pc[:, bass.ds(h, 1), t, :].rearrange("p o c -> p (o c)"), gate(0), None, ALU.mult)
                    dve.wait_ge(exped, h * TILES + (t + 1))
                    nc.vector.reciprocal(rs[:, s, 0:2], rs[:, s, 0:2])
                    dve.drain()
                    nc.vector.tensor_tensor(rs[:, s, 0:2], rs[:, s, 0:2], gt[:, t, bass.ds(h * 3 + (3 * HG * g + 1), 2)], ALU.mult)
                    dve.drain()
                    nc.vector.tensor_scalar(sc[:, s, 0:nsel(t)], sc[:, s, 0:nsel(t)], rs[:, s, 0:1], None, ALU.mult)
                    nc.vector.tensor_scalar(sc[:, s, 512:512 + w], sc[:, s, 512:512 + w], rs[:, s, 1:2], None, ALU.mult).then_inc(weighted, 1)

                bias_scores(0)
                for t in range(TILES):
                    if t + 1 < TILES:
                        bias_scores(t + 1)
                    weigh(t)
                    dve.wait_ge(summed, h * TILES + (t + 1))
                    nc.vector.tensor_copy(oT[:, bass.ds(h + (8 + g * HG), 1), t * P:(t + 1) * P].rearrange("p o t -> p (o t)"),
                                          ps_o[:, t % 2, 0:P])
                dve.drain()



def stage_cached_scores(nc, tag, n, q, units, dblocks, npg, loads, load, st):
    rows = q.shape[2]
    per = rows // NS // units
    nt = units * dblocks
    SLOTS = 4
    with ExitStack() as es:
        sb = lambda name, shape: es.enter_context(nc.sbuf_tensor(f"{tag}_{name}", shape, F32))
        sem = lambda name: new_sem(nc, es, f"{tag}_{name}")
        keys = sb("keys", [P, SLOTS, npg, nt * P])
        kt = sb("kt", [P, nt, npg * P])
        ps_t = es.enter_context(nc.psum_tensor(tag + "_pst", [P, nt, npg * P], F32))
        ps_s = es.enter_context(nc.psum_tensor(tag + "_pss", [P, npg, rows], F32))
        turned, copied, scored = sem("turned"), sem("copied"), sem("scored")
        loaded = [sem(f"loaded{i}") for i in range(SLOTS)]
        block = es.enter_context(stage_block(nc))

        @block.sync
        def _(sp):
            for s in range(SLOTS):
                load(sp, keys[:, s, :, :], s, loaded[s])
            with sp.Fori(0, NS // SLOTS - 1) as i:
                for s in range(SLOTS):
                    sp.wait_ge(turned, i * SLOTS + (s + 1))
                    load(sp, keys[:, s, :, :], i * SLOTS + (s + SLOTS), loaded[s])

        @block.tensor
        def _(pe):
            with pe.Fori(0, NS // SLOTS) as i:
                for s in range(SLOTS):
                    pe.wait_ge(loaded[s], i * (16 * loads) + 16 * loads)
                    for u in range(nt):
                        for pg in range(npg):
                            last = nc.tensor.transpose(ps_t[:, u, pg * P:(pg + 1) * P], keys[:, s, pg, u * P:(u + 1) * P], n.ident)
                    last.then_inc(turned, 1)
                    pe.wait_ge(copied, i * SLOTS + (s + 1))
                    for u in range(units):
                        col = i * (SLOTS * units * per) + (s * units + u) * per
                        for pg in range(npg):
                            for d in range(dblocks):
                                last = nc.tensor.matmul(ps_s[:, pg, bass.ds(col, per)],
                                                        kt[:, u * dblocks + d, pg * P:(pg + 1) * P],
                                                        q[:, d, bass.ds(col, per)], start=(d == 0), stop=(d == dblocks - 1))
                    last.then_inc(scored, 1)

        @block.scalar
        def _(act):
            with act.Fori(0, NS) as b:
                act.wait_ge(turned, b + 1)
                nc.scalar.copy(kt[:, :, :], ps_t[:, :, :]).then_inc(copied, 1)

        @block.vector
        def _(dve):
            dve.wait_ge(scored, NS)
            nc.vector.tensor_copy(st[:, :, :], ps_s[:, :, :])


def stage_row_softmax(nc, tag, n, rows, st, npg, pt, direct=None, bias=None, block_bias=None, new_score=None,
                      gate=None, keep=None, new_weight=None):
    keys = npg * P
    total = keys + (1 if new_score is not None else 0)
    with ExitStack() as es:
        sb = lambda name, shape: es.enter_context(nc.sbuf_tensor(f"{tag}_{name}", shape, F32))
        sem = lambda name: new_sem(nc, es, f"{tag}_{name}")
        s_ = sb("s", [rows, total])
        sm = sb("sm", [rows, 3])
        ps = es.enter_context(nc.psum_tensor(tag + "_ps", [P, 512], F32))
        ps_t = es.enter_context(nc.psum_tensor(tag + "_pst", [P, npg, rows], F32))
        scored, biased, exped, weighted, turned = sem("scored"), sem("biased"), sem("exped"), sem("weighted"), sem("turned")
        block = es.enter_context(stage_block(nc))

        @block.tensor
        def _(pe):
            if direct is not None:
                last = nc.tensor.matmul(ps[0:rows, 0:keys], direct[0], direct[1], start=True, stop=True)
            else:
                for pg in range(npg):
                    last = nc.tensor.transpose(ps[0:rows, pg * P:(pg + 1) * P], st[:, pg, :], n.ident)
            last.then_inc(scored, 1)
            pe.wait_ge(weighted, 1)
            for pg in range(npg):
                last = nc.tensor.transpose(ps_t[:, pg, :], s_[:, pg * P:(pg + 1) * P], n.ident[0:rows, 0:rows])
            last.then_inc(turned, 1)

        @block.scalar
        def _(act):
            act.wait_ge(biased, 1)
            nc.scalar.activation(s_[:, :], s_[:, :], ACT.Exp, bias=sm[:, 0:1], accum_out=sm[:, 1:2]).then_inc(exped, 1)
            act.wait_ge(turned, 1)
            nc.scalar.copy(pt[:, :, :], ps_t[:, :, :])

        @block.vector
        def _(dve):
            dve.wait_ge(scored, 1)
            if bias is not None:
                nc.vector.tensor_tensor(s_[:, 0:keys], ps[0:rows, 0:keys], bias, ALU.add)
            elif block_bias is not None:
                nb = keys // 64
                nc.vector.tensor_tensor(s_[:, 0:keys].rearrange("p (b k) -> p b k", k=64),
                                        ps[0:rows, 0:keys].rearrange("p (b k) -> p b k", k=64),
                                        block_bias[:, 0:nb].unsqueeze(2).to_broadcast([rows, nb, 64]), ALU.add)
            else:
                nc.vector.tensor_copy(s_[:, 0:keys], ps[0:rows, 0:keys])
            if new_score is not None:
                if block_bias is not None:
                    nc.vector.tensor_tensor(s_[:, keys:total], new_score, block_bias[:, keys // 64:keys // 64 + 1], ALU.add)
                else:
                    nc.vector.tensor_copy(s_[:, keys:total], new_score)
            dve.drain()
            nc.vector.tensor_reduce(sm[:, 0:1], s_[:, :], AX.X, ALU.max, negate=True).then_inc(biased, 1)
            dve.wait_ge(exped, 1)
            nc.vector.reciprocal(sm[:, 2:3], sm[:, 1:2])
            dve.drain()
            if keep is not None:
                nc.vector.tensor_scalar(keep, s_[:, 0:keys], sm[:, 2:3], None, ALU.mult)
            if gate is not None:
                nc.vector.tensor_scalar(s_[:, :], s_[:, :], sm[:, 2:3], gate, ALU.mult, ALU.mult).then_inc(weighted, 1)
            else:
                nc.vector.tensor_scalar(s_[:, :], s_[:, :], sm[:, 2:3], None, ALU.mult).then_inc(weighted, 1)
            if new_weight is not None:
                dve.drain()
                nc.vector.tensor_copy(new_weight, s_[:, keys:total])


def stage_cached_values(nc, tag, n, pt, units, dblocks, npg, loads, load, acc, add):
    rows = pt.shape[2]
    per = rows // NS // units
    nt = units * dblocks
    SLOTS = 4
    with ExitStack() as es:
        sem = lambda name: new_sem(nc, es, f"{tag}_{name}")
        vals = es.enter_context(nc.sbuf_tensor(tag + "_vals", [P, SLOTS, npg, nt * P], F32))
        ps = es.enter_context(nc.psum_tensor(tag + "_ps", [P, dblocks, rows], F32))
        summed = sem("summed")
        loaded = [sem(f"loaded{i}") for i in range(SLOTS)]
        block = es.enter_context(stage_block(nc))

        @block.sync
        def _(sp):
            for s in range(SLOTS):
                load(sp, vals[:, s, :, :], s, loaded[s])
            with sp.Fori(0, NS // SLOTS - 1) as i:
                for s in range(SLOTS):
                    sp.wait_ge(summed, i * SLOTS + (s + 1))
                    load(sp, vals[:, s, :, :], i * SLOTS + (s + SLOTS), loaded[s])

        @block.tensor
        def _(pe):
            with pe.Fori(0, NS // SLOTS) as i:
                for s in range(SLOTS):
                    pe.wait_ge(loaded[s], i * (16 * loads) + 16 * loads)
                    for u in range(units):
                        col = i * (SLOTS * units * per) + (s * units + u) * per
                        for d in range(dblocks):
                            c = (u * dblocks + d) * P
                            for pg in range(npg):
                                last = nc.tensor.matmul(ps[:, d, bass.ds(col, per)], vals[:, s, pg, c:c + P],
                                                        pt[:, pg, bass.ds(col, per)], start=(pg == 0), stop=(pg == npg - 1))
                    last.then_inc(summed, 1)

        @block.vector
        def _(dve):
            dve.wait_ge(summed, NS)
            if add:
                nc.vector.tensor_tensor(acc, acc, ps[:, :, :], ALU.add)
            else:
                nc.vector.tensor_copy(acc, ps[:, :, :])


def stage_new_scores(nc, tag, n, q, Z, con_mine, out):
    with ExitStack() as es:
        sem = lambda name: new_sem(nc, es, f"{tag}_{name}")
        nk = es.enter_context(nc.sbuf_tensor(tag + "_nk", [P, 2, NG, NS], F32))
        tmp = es.enter_context(nc.sbuf_tensor(tag + "_tmp", [ROWS, 2, NG * NS], F32))
        ps = es.enter_context(nc.psum_tensor(tag + "_ps", [P, 2, NG * NS], F32))
        copied, scored = sem("copied"), sem("scored")
        block = es.enter_context(stage_block(nc))

        @block.scalar
        def _(act):
            nc.scalar.copy(nk[:, 0, :, :], Z[:, 12:14, SEQ:T])
            nc.scalar.copy(nk[:, 1, :, :], Z[:, 16:18, SEQ:T]).then_inc(copied, 1)

        @block.tensor
        def _(pe):
            pe.wait_ge(copied, 1)
            for j in range(2):
                last = nc.tensor.matmul(ps[0:ROWS, j, :], q[:, 0, :], nk[:, j, :, :].rearrange("p g b -> p (g b)"),
                                        start=True, stop=True)
            last.then_inc(scored, 1)

        @block.vector
        def _(dve):
            dve.wait_ge(scored, 1)
            nc.vector.tensor_tensor(tmp[:, :, :], ps[0:ROWS, :, :], con_mine.unsqueeze(1).to_broadcast([ROWS, 2, NG * NS]), ALU.mult)
            dve.drain()
            nc.vector.tensor_reduce(out, tmp[:, :, :], AX.X, ALU.add)


def stage_pick_sample(nc, tag, n, pk, con, bsel):
    same, vm, va, iota = con[:, 256:320], con[:, 336:345], con[:, 345:354], con[:, 354:363]
    with ExitStack() as es:
        sb = lambda name, shape, dt=F32: es.enter_context(nc.sbuf_tensor(f"{tag}_{name}", shape, dt))
        sem = lambda name: new_sem(nc, es, f"{tag}_{name}")
        own, pb_, score = sb("own", [ROWS, NCMP]), sb("pb", [ROWS, 8]), sb("score", [ROWS, 9])
        v8, i8, if4, hit = sb("v8", [ROWS, 8]), sb("i8", [ROWS, 8], U32), sb("if4", [ROWS, 4]), sb("hit", [ROWS, 9, 4])
        ps = es.enter_context(nc.psum_tensor(tag + "_ps", [P, NCMP], F32))
        reduced, summed = sem("reduced"), sem("summed")
        block = es.enter_context(stage_block(nc))

        @block.tensor
        def _(pe):
            pe.wait_ge(reduced, 1)
            nc.tensor.matmul(ps[0:ROWS, :], same, own[:, :], start=True, stop=True).then_inc(summed, 1)

        @block.vector
        def _(dve):
            nc.vector.tensor_reduce(own[:, :], pk.rearrange("p (u c) -> p c u", c=NCMP), AX.X, ALU.add).then_inc(reduced, 1)
            dve.wait_ge(summed, 1)
            nc.vector.tensor_reduce(pb_[:, :], ps[0:ROWS, :].rearrange("p (b r) -> p b r", r=2), AX.X, ALU.add)
            dve.drain()
            nc.vector.tensor_tensor(score[:, 0:8], pb_[:, :], vm[:, 0:8], ALU.mult)
            nc.vector.tensor_copy(score[:, 8:9], va[:, 8:9])
            dve.drain()
            nc.vector.tensor_tensor(score[:, 0:8], score[:, 0:8], va[:, 0:8], ALU.add)
            dve.drain()
            pick_blocks(nc, dve, score[:, :], v8[:, :], i8[:, :], if4[:, :], hit[:, :, :], bsel, iota, 9)
            nc.vector.tensor_scalar(bsel, bsel, -NEG, NEG, ALU.mult, ALU.add)


def stage_sample_sum(nc, tag, n, ptc, cvs, srows, mine, new_w, acc, oT):
    with ExitStack() as es:
        sem = lambda name: new_sem(nc, es, f"{tag}_{name}")
        m = es.enter_context(nc.sbuf_tensor(tag + "_m", [ROWS, 2, NG * NS], F32))
        mt = es.enter_context(nc.sbuf_tensor(tag + "_mt", [NS, 2 * NG, ROWS], F32))
        ps_t = es.enter_context(nc.psum_tensor(tag + "_pst", [P, 2 * NG, ROWS], F32))
        ps = es.enter_context(nc.psum_tensor(tag + "_ps", [P, ROWS], F32))
        spread, turned, copied, summed = sem("spread"), sem("turned"), sem("copied"), sem("summed")
        block = es.enter_context(stage_block(nc))

        @block.vector
        def _(dve):
            for j in range(2):
                last = nc.vector.tensor_scalar(m[:, j, :], mine, new_w[:, j:j + 1], None, ALU.mult)
            last.then_inc(spread, 1)
            dve.wait_ge(turned, 1)
            nc.vector.tensor_copy(mt[:, :, :], ps_t[0:NS, :, :]).then_inc(copied, 1)
            dve.wait_ge(summed, 1)
            nc.vector.tensor_tensor(acc, acc, ps[:, :].unsqueeze(1), ALU.add)
            dve.drain()
            nc.vector.tensor_copy(oT[:, 8:16, SEQ:T].rearrange("p h b -> p b h"),
                                  acc.rearrange("p o (b h) -> p (o b) h", h=NH))

        @block.tensor
        def _(pe):
            pe.wait_ge(spread, 1)
            for j in range(2):
                for g in range(NG):
                    last = nc.tensor.transpose(ps_t[0:NS, 2 * j + g, :], m[:, j, g * NS:(g + 1) * NS], n.ident[0:ROWS, 0:ROWS])
            last.then_inc(turned, 1)
            pe.wait_ge(copied, 1)
            for a in range(2):
                nc.tensor.matmul(ps[:, :], cvs[:, a, :], ptc[:, a, :], start=(a == 0), stop=False)
            for j in range(2):
                for g in range(NG):
                    last = nc.tensor.matmul(ps[:, :], srows[:, (6 if j == 0 else 10) + g, :], mt[:, 2 * j + g, :],
                                            start=False, stop=(j == 1 and g == 1))
            last.then_inc(summed, 1)


def stage_sample_queries(nc, tag, n, Z, q, heads, dblocks, scale, con=None):
    with ExitStack() as es:
        loaded = new_sem(nc, es, tag + "_loaded")
        block = es.enter_context(stage_block(nc))

        @block.sync
        def _(sp):
            if con is not None:
                sp.dma_start(con[:, :], n.c["smp"]).then_inc(loaded, 16)
                sp.wait_ge(loaded, 16)

        @block.vector
        def _(dve):
            for d in range(dblocks):
                nc.vector.tensor_scalar(q[:, d, :].rearrange("p (b h) -> p h b", h=heads),
                                        Z[:, d:heads * dblocks:dblocks, SEQ:T], scale, None, ALU.mult)


def sample_nsa(nc, n, Z, ck, cvs, srows, grow, oT):

    def paged(pool):
        def load(sp, dst, b, done):
            for pg in range(PAGES):
                at = b * PAGES + pg
                number = sp.value_load(n.table[0:1, bass.ds(at, 1)], min_val=0, max_val=N_POOL - 1)
                sp.dma_start(dst[:, pg, :], pool[bass.ds(number, 1), :, :, :].rearrange("o t g d -> t (o g d)")).then_inc(done, 16)
        return load

    def window(cache):
        def load(sp, dst, b, done):
            sp.dma_start(dst, cache[bass.ds(b, 1), :, :, :].rearrange("o (t p) g d -> p (o t) (g d)", p=P)).then_inc(done, 16)
        return load

    with ExitStack() as es:
        sb = lambda name, shape: es.enter_context(nc.sbuf_tensor("sn_" + name, shape, F32))
        q = sb("q", [P, 1, ROWS])
        con = sb("con", [ROWS, 363])
        acc = sb("acc", [P, 1, ROWS])
        new_s, new_w, bsel = sb("new_s", [ROWS, 2]), sb("new_w", [ROWS, 2]), sb("bsel", [ROWS, 9])
        ptc, pk = sb("ptc", [P, 2, ROWS]), sb("pk", [ROWS, 256])
        st, pt = sb("st", [P, PAGES, ROWS]), sb("pt", [P, PAGES, ROWS])
        mine = con[:, 320:336]
        stage_sample_queries(nc, "sq", n, Z, q, NH, 1, P ** -0.5, con)
        stage_new_scores(nc, "sn", n, q, Z, mine, new_s[:, :])
        stage_row_softmax(nc, "sc", n, ROWS, None, 2, ptc, direct=(q[:, 0, :], ck[:, 32:288]), bias=con[:, 0:256],
                          gate=grow[:, 0:1], keep=pk[:, :])
        stage_pick_sample(nc, "sk", n, pk[:, :], con, bsel[:, :])
        stage_cached_scores(nc, "ss", n, q, NG, 1, PAGES, PAGES, paged(n.i["cache_sel_k"][0]), st)
        stage_row_softmax(nc, "sf", n, ROWS, st, PAGES, pt, block_bias=bsel, new_score=new_s[:, 0:1],
                          gate=grow[:, 1:2], new_weight=new_w[:, 0:1])
        stage_cached_values(nc, "sv", n, pt, NG, 1, PAGES, PAGES, paged(n.i["cache_sel_v"][0]), acc[:, :, :], False)
        stage_cached_scores(nc, "ws", n, q, NG, 1, 2, 1, window(n.i["cache_win_k"][0]), st[:, 0:2, :])
        stage_row_softmax(nc, "wf", n, ROWS, st, 2, pt[:, 0:2, :], new_score=new_s[:, 1:2], gate=grow[:, 2:3],
                          new_weight=new_w[:, 1:2])
        stage_cached_values(nc, "wv", n, pt[:, 0:2, :], NG, 1, 2, 1, window(n.i["cache_win_v"][0]), acc[:, :, :], True)
        stage_sample_sum(nc, "sx", n, ptc, cvs, srows, mine, new_w, acc[:, :, :], oT)


def stage_head_norm(nc, tag, n, Z, heads, gain, cols):
    parts = 2 if cols > 512 else 1
    half = cols // parts
    with ExitStack() as es:
        sb = lambda name, shape: es.enter_context(nc.sbuf_tensor(f"{tag}_{name}", shape, F32))
        sem = lambda name: new_sem(nc, es, f"{tag}_{name}")
        gn, sq, ro = sb("gn", [P, 2]), sb("sq", [P, 2, cols]), sb("ro", [P, cols])
        ps = es.enter_context(nc.psum_tensor(tag + "_ps", [P, parts, 512], F32))
        loaded, squared, summed, rooted, normed = sem("loaded"), sem("squared"), sem("summed"), sem("rooted"), sem("normed")
        block = es.enter_context(stage_block(nc))

        @block.sync
        def _(sp):
            sp.dma_start(gn[:, :], gain.rearrange("(e p) -> p e", p=P), allow_slow_non_contiguous=True).then_inc(loaded, 16)

        @block.scalar
        def _(act):
            act.sem_inc(normed, 1)
            with act.Fori(0, heads) as h:
                act.wait_ge(normed, h + 1)
                nc.scalar.activation(sq[:, :, :], Z[:, bass.ds(h * 2, 2), :], ACT.Square).then_inc(squared, 1)
                act.wait_ge(summed, h + 1)
                nc.scalar.activation(sq[:, 0, :].rearrange("p (a b) -> p a b", a=parts), ps[:, :, 0:half], ACT.Sqrt,
                                     scale=1.0 / MD, bias=n_eps(nc)[:, :]).then_inc(rooted, 1)

        @block.tensor
        def _(pe):
            with pe.Fori(0, heads) as h:
                pe.wait_ge(squared, h + 1)
                for a in range(parts):
                    for e in range(2):
                        last = nc.tensor.matmul(ps[:, a, 0:half], n.ones, sq[:, e, a * half:(a + 1) * half],
                                                start=(e == 0), stop=(e == 1))
                last.then_inc(summed, 1)

        @block.vector
        def _(dve):
            dve.wait_ge(loaded, 16)
            with dve.Fori(0, heads) as h:
                dve.wait_ge(rooted, h + 1)
                nc.vector.reciprocal(ro[:, :], sq[:, 0, :])
                dve.drain()
                for e in range(2):
                    z = Z[:, bass.ds(h * 2 + e, 1), :].rearrange("p o t -> p (o t)")
                    last = nc.vector.scalar_tensor_tensor(z, z, gn[:, e:e + 1], ro[:, :], ALU.mult, ALU.mult)
                last.then_inc(normed, 1)


def stage_memory_rows(nc, tag, n, M, b0, rows, out):
    with ExitStack() as es:
        sem = lambda name: new_sem(nc, es, f"{tag}_{name}")
        ps = es.enter_context(nc.psum_tensor(tag + "_ps", [P, 2, MH * MD], F32))
        turned, copied, stored = sem("turned"), sem("copied"), sem("stored")
        block = es.enter_context(stage_block(nc))

        @block.tensor
        def _(pe):
            for t in range(2):
                for k in range(8):
                    last = nc.tensor.transpose(ps[:, t, k * P:(k + 1) * P], M[:, b0 + k, t * P:(t + 1) * P], n.ident)
            last.then_inc(turned, 1)

        @block.vector
        def _(dve):
            dve.wait_ge(turned, 1)
            nc.vector.tensor_copy(rows[:, :, :], ps[:, :, :]).then_inc(copied, 1)

        @block.sync
        def _(sp):
            sp.wait_ge(copied, 1)
            sp.dma_start(out.rearrange("(t p) h d -> p t (h d)", p=P), rows[:, :, :]).then_inc(stored, 16)
            sp.wait_ge(stored, 16)


def stage_memory_attend(nc, tag, n, Z, M, vrows, oT):
    with ExitStack() as es:
        sb = lambda name, shape: es.enter_context(nc.sbuf_tensor(f"{tag}_{name}", shape, F32))
        pb = lambda name, shape: es.enter_context(nc.psum_tensor(f"{tag}_{name}", shape, F32))
        sem = lambda name: new_sem(nc, es, f"{tag}_{name}")
        qs = sb("qs", [P, 2, SEQ])
        pr = sb("pr", [P, 2, NM])
        sm = sb("sm", [P, 2, 3])
        pt = sb("pt", [P, 2, P])
        vh = sb("vh", [P, 2, MD])
        ps_s, ps_t, ps_o = pb("pss", [P, 2, 512]), pb("pst", [P, 512]), pb("pso", [P, 2, 512])
        staged, scored, maxed, exped, weighted, turned, pt_saved, summed = (
            sem("staged"), sem("scored"), sem("maxed"), sem("exped"), sem("weighted"), sem("turned"), sem("pt_saved"), sem("summed"))
        block = es.enter_context(stage_block(nc))

        @block.scalar
        def _(act):
            with act.Fori(0, MH) as h:
                nc.scalar.copy(vh[:, :, :], vrows[:, :, bass.ds(h * MD, MD)])
                nc.scalar.activation(qs[:, :, :], Z[:, bass.ds(h * 2, 2), 0:SEQ], ACT.Copy, scale=MD ** -0.5).then_inc(staged, 1)

                def softmax(t):
                    act.wait_ge(maxed, h * TILES + (t + 1))
                    nc.scalar.activation(pr[:, t % 2, :], ps_s[:, t % 2, 0:NM], ACT.Exp, bias=sm[:, t % 2, 0:1],
                                         accum_out=sm[:, t % 2, 1:2]).then_inc(exped, 1)

                softmax(0)
                for t in range(TILES):
                    if t + 1 < TILES:
                        softmax(t + 1)
                    act.wait_ge(turned, h * TILES + (t + 1))
                    nc.scalar.copy(pt[:, :, :], ps_t[:, 0:NM].rearrange("p (k q) -> p k q", q=P)).then_inc(pt_saved, 1)
                act.wait_ge(summed, h * TILES + TILES)

        @block.tensor
        def _(pe):
            with pe.Fori(0, MH) as h:
                pe.wait_ge(staged, h + 1)

                def scores(t):
                    for d in range(2):
                        last = nc.tensor.matmul(ps_s[:, t % 2, 0:NM], qs[:, d, t * P:(t + 1) * P],
                                                M[:, bass.ds(h * 2 + d, 1), :].rearrange("p o m -> p (o m)"),
                                                start=(d == 0), stop=(d == 1))
                    last.then_inc(scored, 1)

                scores(0)
                for t in range(TILES):
                    if t + 1 < TILES:
                        scores(t + 1)
                    pe.wait_ge(weighted, h * TILES + (t + 1))
                    for k in range(2):
                        last = nc.tensor.transpose(ps_t[:, k * P:(k + 1) * P], pr[:, t % 2, k * P:(k + 1) * P], n.ident)
                    last.then_inc(turned, 1)
                    pe.wait_ge(pt_saved, h * TILES + (t + 1))
                    for e in range(2):
                        for k in range(2):
                            last = nc.tensor.matmul(ps_o[:, t % 2, e * P:(e + 1) * P], vh[:, k, e * P:(e + 1) * P],
                                                    pt[:, k, :], start=(k == 0), stop=(k == 1))
                    last.then_inc(summed, 1)

        @block.vector
        def _(dve):
            with dve.Fori(0, MH) as h:
                def top(t):
                    dve.wait_ge(scored, h * TILES + (t + 1))
                    nc.vector.tensor_reduce(sm[:, t % 2, 0:1], ps_s[:, t % 2, 0:NM], AX.X, ALU.max, negate=True).then_inc(maxed, 1)

                top(0)
                for t in range(TILES):
                    if t + 1 < TILES:
                        top(t + 1)
                    dve.wait_ge(exped, h * TILES + (t + 1))
                    nc.vector.reciprocal(sm[:, t % 2, 2:3], sm[:, t % 2, 1:2])
                    dve.drain()
                    nc.vector.tensor_scalar(pr[:, t % 2, :], pr[:, t % 2, :], sm[:, t % 2, 2:3], None, ALU.mult).then_inc(weighted, 1)
                    dve.wait_ge(summed, h * TILES + (t + 1))
                    nc.vector.tensor_copy(oT[:, bass.ds(h * 2 + 16, 2), t * P:(t + 1) * P],
                                          ps_o[:, t % 2, 0:2 * P].rearrange("p (e q) -> p e q", e=2))
                dve.drain()


def stage_copy_rows(nc, tag, dst, src):
    with nc.Block() as block:
        @block.vector
        def _(dve):
            nc.vector.tensor_copy(dst, src)


def sample_memory(nc, n, Z, oT):
    rows = NS * MH

    def cached(cache):
        def load(sp, dst, b, done):
            sp.dma_start(dst, cache[bass.ds(b, 1), :, :, :].rearrange("o (t p) h d -> p (o t) (h d)", p=P)).then_inc(done, 16)
        return load

    with ExitStack() as es:
        sb = lambda name, shape: es.enter_context(nc.sbuf_tensor("sm_" + name, shape, F32))
        q, st, pt, acc = sb("q", [P, 2, rows]), sb("st", [P, 2, rows]), sb("pt", [P, 2, rows]), sb("acc", [P, 2, rows])
        stage_sample_queries(nc, "mq", n, Z, q, MH, 2, MD ** -0.5)
        stage_cached_scores(nc, "ms", n, q, MH, 2, 2, 1, cached(n.i["cache_mem_k"][0]), st)
        stage_row_softmax(nc, "mf", n, rows, st, 2, pt)
        stage_cached_values(nc, "mv", n, pt, MH, 2, 2, 1, cached(n.i["cache_mem_v"][0]), acc[:, :, :], False)
        for d in range(2):
            stage_copy_rows(nc, f"mc{d}", oT[:, 16 + d:24:2, SEQ:T].rearrange("p h b -> p b h"),
                            acc[:, d, :].rearrange("p (b h) -> p b h", h=MH))



def stage_merge(nc, tag, n, hT, oT, w_in, w_branch, mT):
    U = 6
    with ExitStack() as es:
        sb = lambda name, shape: es.enter_context(nc.sbuf_tensor(f"{tag}_{name}", shape, F32))
        sem = lambda name: new_sem(nc, es, f"{tag}_{name}")
        wt = sb("w", [P, 2, 24, P])
        sg, up = sb("sg", [P, 2, T]), sb("up", [P, T])
        ps_g = es.enter_context(nc.psum_tensor(tag + "_psg", [P, 2, 2, 512], F32))
        ps_u = es.enter_context(nc.psum_tensor(tag + "_psu", [P, 2, 2, 512], F32))
        loaded = [sem(f"loaded{i}") for i in range(2)]
        summed, gated, merged = sem("summed"), sem("gated"), sem("merged")
        block = es.enter_context(stage_block(nc))

        @block.sync
        def _(sp):
            def load(slot, j, c):
                col = j * P
                sp.dma_start(wt[:, slot, 0:16, :], w_in[:, bass.ds(col + (C_MG + c * D), P)].rearrange("(k p) n -> p k n", p=P)
                             ).then_inc(loaded[slot], 16)
                sp.dma_start(wt[:, slot, 16:24, :], w_branch[c][:, bass.ds(col, P)].rearrange("(k p) n -> p k n", p=P)
                             ).then_inc(loaded[slot], 16)

            load(0, 0, 0)
            load(1, 0, 1)
            with sp.Fori(0, KD // 2 - 1) as i:
                for u in range(U):
                    sp.wait_ge(summed, i * U + (u + 1))
                    load(u % 2, i * 2 + (u + 2) // 3, (u + 2) % 3)
            for u in range(U - 2):
                sp.wait_ge(summed, (KD // 2 - 1) * U + u + 1)
                load(u % 2, KD - 2 + (u + 2) // 3, (u + 2) % 3)

        @block.tensor
        def _(pe):
            with pe.Fori(0, KD // 2) as i:
                for u in range(U):
                    s, c = u % 2, u % 3
                    pe.wait_ge(loaded[s], i * 96 + (u // 2 + 1) * 32)
                    pe.wait_ge(merged, i * U + (u + 1))
                    for k in range(16):
                        for h in range(2):
                            nc.tensor.matmul(ps_g[:, s, h, 0:HALF], wt[:, s, k, :], hT[:, k, h * HALF:(h + 1) * HALF],
                                             start=(k == 0), stop=(k == 15))
                    for k in range(8):
                        for h in range(2):
                            last = nc.tensor.matmul(ps_u[:, s, h, 0:HALF], wt[:, s, 16 + k, :],
                                                    oT[:, c * 8 + k, h * HALF:(h + 1) * HALF],
                                                    start=(k == 0), stop=(k == 7))
                    last.then_inc(summed, 1)

        @block.scalar
        def _(act):
            with act.Fori(0, KD // 2) as i:
                for u in range(U):
                    act.wait_ge(summed, i * U + (u + 1))
                    act.wait_ge(merged, i * U + (u + 1))
                    nc.scalar.activation(halves(sg[:, u % 2, :]), ps_g[:, u % 2, :, 0:HALF], ACT.Sigmoid).then_inc(gated, 1)

        @block.vector
        def _(dve):
            dve.sem_inc(merged, 2)
            with dve.Fori(0, KD // 2) as i:
                for u in range(U):
                    m = mT[:, bass.ds(i * 2 + u // 3, 1), :].rearrange("p o t -> p (o t)")
                    dve.wait_ge(gated, i * U + (u + 1))
                    dst = m if u % 3 == 0 else up[:, :]
                    last = nc.vector.tensor_tensor(halves(dst), halves(sg[:, u % 2, :]), ps_u[:, u % 2, :, 0:HALF], ALU.mult)
                    if u % 3:
                        dve.drain()
                        last = nc.vector.tensor_tensor(m, m, up[:, :], ALU.add)
                    last.then_inc(merged, 1)
                    dve.drain()


def stage_residual(nc, tag, n, aT, tiles, x1):
    with ExitStack() as es:
        sem = lambda name: new_sem(nc, es, f"{tag}_{name}")
        ps = es.enter_context(nc.psum_tensor(tag + "_ps", [P, 2, D], F32))
        loaded, turned, added = sem("loaded"), sem("turned"), sem("added")
        block = es.enter_context(stage_block(nc))

        @block.sync
        def _(sp):
            for t, (src, rows, _c) in enumerate(tiles):
                sp.dma_start(x1[0:rows, t, :], src).then_inc(loaded, 16)

        @block.tensor
        def _(pe):
            for t, (_s, rows, col) in enumerate(tiles):
                if t >= 2:
                    pe.wait_ge(added, t - 1)
                for k in range(KD):
                    last = nc.tensor.transpose(ps[0:rows, t % 2, k * P:(k + 1) * P], aT[:, k, col:col + rows], n.ident)
                last.then_inc(turned, 1)

        @block.vector
        def _(dve):
            dve.wait_ge(loaded, 16 * len(tiles))
            for t, (_s, rows, _c) in enumerate(tiles):
                dve.wait_ge(turned, t + 1)
                nc.vector.tensor_tensor(x1[0:rows, t, :], x1[0:rows, t, :], ps[0:rows, t % 2, :], ALU.add).then_inc(added, 1)


def stage_subkeys(nc, tag, n, subkeys, sk):
    with ExitStack() as es:
        sem = lambda name: new_sem(nc, es, f"{tag}_{name}")
        nat = es.enter_context(nc.sbuf_tensor(tag + "_nat", [PK, PH, 2, 64], F32))
        ps = es.enter_context(nc.psum_tensor(tag + "_ps", [P, PH, PK], F32))
        loaded, turned = sem("loaded"), sem("turned")
        block = es.enter_context(stage_block(nc))

        @block.sync
        def _(sp):
            for h in range(PH):
                sp.dma_start(nat[:, h, :, :], subkeys[h].rearrange("a e k -> e a k")).then_inc(loaded, 16)

        @block.tensor
        def _(pe):
            pe.wait_ge(loaded, 16 * PH)
            for h in range(PH):
                last = nc.tensor.transpose(ps[:, h, :], nat[:, h, :, :].rearrange("e a k -> e (a k)"), n.ident)
            last.then_inc(turned, 1)

        @block.vector
        def _(dve):
            dve.wait_ge(turned, 1)
            nc.vector.tensor_copy(sk[:, :, :], ps[:, :, :])


def stage_experts(nc, tag, n, u, v, qT, sk, h2, x1, x1_dram, y_prompt, y_sample):
    R = 8
    RUNS = PICKS // R
    PARTS = 4
    G = 2 * PH
    LOW = -3e38
    with ExitStack() as es:
        sb = lambda name, shape, dt=F32: es.enter_context(nc.sbuf_tensor(f"{tag}_{name}", shape, dt))
        sem = lambda name: new_sem(nc, es, f"{tag}_{name}")
        eid, gate = sb("eid", [P, TILES + 1, PICKS], I32), sb("gate", [P, TILES + 1, PICKS])
        eids, gates = sb("eids", [P, NS], I32), sb("gates", [P, NS])
        iota = sb("iota", [P, TOPK])
        qs = sb("qs", [P, PH, P])
        s0 = x1[:, TILES, :].rearrange("p (g k) -> p g k", k=PK)
        s1 = sb("s1", [P, G, PK])
        val, idx, idf = sb("val", [P, PH, 2, TOPK]), sb("idx", [P, PH, 2, TOPK], U32), sb("idf", [P, PH, 2, TOPK])
        top, pos = sb("top", [P, PH, TOPK]), sb("pos", [P, PH, TOPK], U32)
        part, parf = sb("part", [P, 2, PICKS], U32), sb("parf", [P, 2, PICKS])
        e01, ef = sb("e01", [P, 2, PICKS]), sb("ef", [P, PICKS])
        sm = sb("sm", [P, PH])
        ring = sb("ring", [P, R, D])
        slot_ids = sb("slot_ids", [P, R], I32)
        onehot = sb("onehot", [NS, NS * P])
        dot8 = sb("dot8", [P, R])
        dots, dotb = sb("dots", [P, TILES, PICKS]), sb("dotb", [P, NS])
        diag = sb("diag", [P, NS * NS])
        ps = es.enter_context(nc.psum_tensor(tag + "_ps", [P, 2, D], F32))
        ps_s = ps[:, 0, :].rearrange("p (g k) -> p g k", k=PK)
        ps_t = ps[:, 1, 0:2 * NS].rearrange("p (a b) -> p a b", b=NS)
        iota_loaded, staged, scored, shifted, exped, routed, turned, sample_routed = (
            sem("iota_loaded"), sem("staged"), sem("scored"), sem("shifted"), sem("exped"), sem("routed"), sem("turned"),
            sem("sample_routed"))
        landed = [sem(f"landed{i}") for i in range(R)]
        onehot_loaded, x1_loaded, idx_ready, started, used, spread, dotted, gelued, weighted, summed, added, stored = (
            sem("onehot_loaded"), sem("x1_loaded"), sem("idx_ready"), sem("started"), sem("used"), sem("spread"),
            sem("dotted"), sem("gelued"), sem("weighted"), sem("summed"), sem("added"), sem("stored"))
        block = es.enter_context(stage_block(nc))
        HALF_USES = TILES * RUNS + 1

        @block.gpsimd
        def _(pool):
            def gather(table, ids, s, number):
                pool.wait_ge(used, number + 1)
                nc.gpsimd.tensor_copy(slot_ids[:, s:s + 1], ids).then_inc(idx_ready, 1)
                pool.wait_ge(idx_ready, number + 1)
                pool.sem_inc(started, 1)
                nc.gpsimd.indirect_dma_start(ring[:, s, :], None, table, bass.IndirectOffsetOnAxis(slot_ids[:, s:s + 1], 0)
                                             ).then_inc(landed[s], 16)

            for a, table in enumerate((u, v)):
                first = a * HALF_USES * R
                with pool.Fori(0, TILES) as t:
                    if a == 0:
                        pool.wait_ge(routed, t + 1)
                        pool.sem_inc(started, 1)
                    with pool.Fori(0, RUNS) as i:
                        for s in range(R):
                            gather(table, eid[:, bass.ds(t, 1), bass.ds(i * R + s, 1)].rearrange("p o k -> p (o k)"), s,
                                   t * (RUNS * R) + i * R + (first + s))
                if a == 0:
                    pool.wait_ge(sample_routed, 1)
                for s in range(R):
                    gather(table, eids[:, s:s + 1], s, first + TILES * RUNS * R + s)

        @block.tensor
        def _(pe):
            def score(t, rows):
                pe.wait_ge(staged, t + 1)
                for h in range(PH):
                    for a in range(2):
                        last = nc.tensor.matmul(ps_s[0:rows, a * PH + h, :], qs[64 * a:64 * a + 64, h, 0:rows],
                                                sk[64 * a:64 * a + 64, h, :], start=True, stop=True)
                last.then_inc(scored, 1)

            with pe.Fori(0, TILES) as t:
                score(t, P)
            score(TILES, NS)
            pe.wait_ge(routed, TILES + 1)
            nc.tensor.transpose(ps_t[:, 0, :], ef[0:NS, :], n.ident[0:NS, 0:NS])
            nc.tensor.transpose(ps_t[:, 1, :], gate[0:NS, TILES, :], n.ident[0:NS, 0:NS]).then_inc(turned, 1)
            pe.wait_ge(onehot_loaded, 16)
            pe.wait_ge(sample_routed, 1)
            for b in range(NS):
                if b >= 2:
                    pe.wait_ge(dotted, b - 1)
                for c in range(4):
                    last = nc.tensor.matmul(ps[:, b % 2, c * 512:(c + 1) * 512], onehot[:, b * P:(b + 1) * P],
                                            h2[0:NS, TILES, c * 512:(c + 1) * 512], start=True, stop=True)
                last.then_inc(spread, 1)
            pe.wait_ge(weighted, 1)
            for b in range(NS):
                pe.wait_ge(landed[b], 2 * HALF_USES * 16)
                for c in range(4):
                    last = nc.tensor.matmul(ps[0:NS, 0, c * 512:(c + 1) * 512], diag[:, b * NS:(b + 1) * NS],
                                            ring[:, b, c * 512:(c + 1) * 512], start=(b == 0), stop=(b == NS - 1))
            last.then_inc(summed, 1)

        @block.scalar
        def _(act):
            nc.scalar.copy(qs[:, :, :], qT[:, :, 0:P]).then_inc(staged, 1)
            with act.Fori(0, TILES - 1) as t:
                act.wait_ge(shifted, t + 1)
                g = gate[:, bass.ds(t, 1), :].rearrange("p o k -> p (o k)")
                nc.scalar.activation(g, g, ACT.Exp).then_inc(exped, 1)
                nc.scalar.copy(qs[:, :, :], qT[:, :, bass.ds(t * P + P, P)]).then_inc(staged, 1)
            act.wait_ge(shifted, TILES)
            nc.scalar.activation(gate[:, TILES - 1, :], gate[:, TILES - 1, :], ACT.Exp).then_inc(exped, 1)
            nc.scalar.copy(qs[:, :, 0:NS], qT[:, :, SEQ:T]).then_inc(staged, 1)
            act.wait_ge(shifted, TILES + 1)
            nc.scalar.activation(gate[0:NS, TILES, :], gate[0:NS, TILES, :], ACT.Exp).then_inc(exped, 1)
            act.wait_ge(dotted, NS)
            nc.scalar.activation(dots[:, :, :], dots[:, :, :], ACT.Gelu)
            nc.scalar.activation(dotb[:, :], dotb[:, :], ACT.Gelu).then_inc(gelued, 1)

        @block.vector
        def _(dve):
            def top16(scores, spare, v, i):
                for src, lo in ((scores, 0), (spare, 8)):
                    for j in range(len(v)):
                        nc.vector.max(v[j][:, lo:lo + 8], src[j])
                    dve.drain()
                    for j in range(len(v)):
                        nc.vector.max_index(i[j][:, lo:lo + 8], v[j][:, lo:lo + 8], src[j])
                        if lo == 0:
                            nc.vector.match_replace(spare[j], v[j][:, 0:8], src[j], LOW)
                    dve.drain()

            def route(p, t, rows, g, out):
                r = slice(0, rows)
                cand = s0[r].rearrange("p g k -> p (g k)").rearrange("p (h a b) -> p h a b", h=PH, a=TOPK)
                gh = g.rearrange("p (h k) -> p h k", h=PH)
                if p < 2:
                    if p == 0:
                        dve.wait_ge(scored, t + 1)
                        nc.vector.tensor_copy(s0[r], ps_s[r])
                        dve.drain()
                    js = range(p * PH, (p + 1) * PH)
                    top16([s0[r, j % 2 * PH + j // 2, :] for j in js], [s1[r, j, :] for j in js],
                          [val[r, j // 2, j % 2, :] for j in js], [idx[r, j // 2, j % 2, :] for j in js])
                elif p == 2:
                    nc.vector.tensor_copy(idf[r], idx[r])
                    nc.vector.tensor_tensor(cand, val[r, :, 0, :].unsqueeze(3).to_broadcast([rows, PH, TOPK, TOPK]),
                                            val[r, :, 1, :].unsqueeze(2).to_broadcast([rows, PH, TOPK, TOPK]), ALU.add)
                    dve.drain()
                    c1 = s0[r].rearrange("p g k -> p (g k)").rearrange("p (h c) -> p h c", h=PH)
                    c2 = s1[r].rearrange("p g k -> p (g k)").rearrange("p (h c) -> p h c", h=PH)
                    top16([c1[:, h, :] for h in range(PH)], [c2[:, h, :] for h in range(PH)],
                          [top[r, h, :] for h in range(PH)], [pos[r, h, :] for h in range(PH)])
                    nc.vector.tensor_tensor(gh, top[r], top[r, :, 0:1].to_broadcast([rows, PH, TOPK]),
                                            ALU.subtract).then_inc(shifted, 1)
                else:
                    flat = pos[r].rearrange("p h k -> p (h k)")
                    nc.vector.tensor_scalar(part[r, 0, :], flat, 4, None, ALU.logical_shift_right)
                    nc.vector.tensor_scalar(part[r, 1, :], flat, 15, None, ALU.bitwise_and)
                    dve.drain()
                    nc.vector.tensor_copy(parf[r], part[r])
                    dve.drain()
                    for a in range(2):
                        hot = s0[r].rearrange("p g k -> p (g k)").rearrange("p (h k c) -> p h k c", h=PH, k=TOPK)
                        hot3 = s0[r].rearrange("p g k -> p (g k)").rearrange("p (k c) -> p k c", c=TOPK)
                        nc.vector.tensor_tensor(hot3, parf[r, a, :].unsqueeze(2).to_broadcast([rows, PICKS, TOPK]),
                                                iota[r].unsqueeze(1).to_broadcast([rows, PICKS, TOPK]), ALU.is_equal)
                        dve.drain()
                        nc.vector.tensor_tensor(hot, hot, idf[r, :, a, :].unsqueeze(2).to_broadcast([rows, PH, TOPK, TOPK]),
                                                ALU.mult)
                        dve.drain()
                        nc.vector.tensor_reduce(e01[r, a, :], hot3, AX.X, ALU.add)
                        dve.drain()
                    nc.vector.scalar_tensor_tensor(ef[r], e01[r, 0, :], float(PK), e01[r, 1, :], ALU.mult, ALU.add)
                    dve.drain()
                    dve.wait_ge(exped, t + 1)
                    nc.vector.tensor_scalar(out, ef[r], 0.0, None, ALU.add)
                    dve.drain()
                    nc.vector.tensor_reduce(sm[r], gh, AX.X, ALU.add)
                    dve.drain()
                    nc.vector.reciprocal(sm[r], sm[r])
                    dve.drain()
                    nc.vector.tensor_tensor(gh, gh, sm[r].unsqueeze(2).to_broadcast([rows, PH, TOPK]), ALU.mult
                                            ).then_inc(routed, 1)
                    dve.drain()

            def dot(p, t):
                with dve.Fori(0, RUNS // PARTS) as i:
                    run0 = p * (RUNS // PARTS)
                    for s in range(R):
                        dve.wait_ge(landed[s], t * (RUNS * 16) + i * 16 + (run0 + 1) * 16)
                        nc.vector.scalar_tensor_tensor(ring[:, s, :], ring[:, s, :], 1.0, h2[:, bass.ds(t, 1), :].rearrange("p o d -> p (o d)"),
                                                       ALU.mult, ALU.mult, accum_out=dot8[:, s:s + 1]).then_inc(used, 1)
                    dve.drain()
                    d8 = dots[:, bass.ds(t, 1), bass.ds(i * R + run0 * R, R)].rearrange("p o k -> p (o k)")
                    nc.vector.tensor_copy(d8, dot8[:, :])
                    dve.drain()

            last_tile = TILES - 1
            dve.wait_ge(iota_loaded, 16)
            for p in range(PARTS):
                route(p, 0, P, gate[:, 0, :], eid[:, 0, :])
            dve.sem_inc(used, R)
            with dve.Fori(0, TILES - 1) as t:
                for p in range(PARTS):
                    route(p, t + 1, P, gate[:, bass.ds(t + 1, 1), :].rearrange("p o k -> p (o k)"),
                          eid[:, bass.ds(t + 1, 1), :].rearrange("p o k -> p (o k)"))
                    dot(p, t)
            for p in range(PARTS):
                route(p, TILES, NS, gate[0:NS, TILES, :], eid[0:NS, TILES, :])
                if p == PARTS - 1:
                    dve.wait_ge(turned, 1)
                    nc.vector.tensor_copy(eids[:, :], ps_t[:, 0, :])
                    nc.vector.tensor_copy(gates[:, :], ps_t[:, 1, :])
                    dve.drain()
                    dve.sem_inc(sample_routed, 1)
                dot(p, last_tile)
            for b in range(NS):
                dve.wait_ge(landed[b], HALF_USES * 16)
                dve.wait_ge(spread, b + 1)
                nc.vector.scalar_tensor_tensor(ring[:, b, :], ring[:, b, :], 1.0, ps[:, b % 2, :], ALU.mult, ALU.mult,
                                               accum_out=dotb[:, b:b + 1]).then_inc(dotted, 1)
                dve.drain()
                dve.sem_inc(used, 1)
            nc.vector.memset(diag[:, :], 0.0)
            dve.drain()
            dve.wait_ge(gelued, 1)
            nc.vector.tensor_tensor(dots[:, :, :], dots[:, :, :], gate[:, 0:TILES, :], ALU.mult)
            nc.vector.tensor_tensor(diag[:, 0:NS * NS:NS + 1], dotb[:, :], gates[:, :], ALU.mult).then_inc(weighted, 1)
            dve.drain()
            dve.wait_ge(x1_loaded, 16 * (TILES + 1))
            with dve.Fori(0, TILES) as t:
                x = x1[:, bass.ds(t, 1), :].rearrange("p o d -> p (o d)")
                with dve.Fori(0, RUNS) as i:
                    for s in range(R):
                        dve.wait_ge(landed[s], t * (RUNS * 16) + i * 16 + (HALF_USES + 1) * 16)
                        nc.vector.scalar_tensor_tensor(
                            x, ring[:, s, :], dots[:, bass.ds(t, 1), bass.ds(i * R + s, 1)].rearrange("p o k -> p (o k)"),
                            x, ALU.mult, ALU.add).then_inc(used, 1)
                        dve.drain()
                dve.sem_inc(added, 1)
            dve.wait_ge(summed, 1)
            nc.vector.tensor_tensor(x1[0:NS, TILES, :], x1[0:NS, TILES, :], ps[0:NS, 0, :], ALU.add).then_inc(added, 1)

        @block.sync
        def _(sp):
            sp.dma_start(iota[:, :], n.c["peer"]).then_inc(iota_loaded, 16)
            sp.dma_start(onehot[:, :], n.c["onehot"]).then_inc(onehot_loaded, 16)
            for t in range(TILES):
                sp.dma_start(x1[:, t, :], x1_dram[t * P:(t + 1) * P, :]).then_inc(x1_loaded, 16)
            sp.wait_ge(routed, TILES + 1)
            sp.dma_start(x1[0:NS, TILES, :], x1_dram[SEQ:T, :]).then_inc(x1_loaded, 16)
            for t in range(TILES):
                sp.wait_ge(added, t + 1)
                sp.dma_start(y_prompt[t * P:(t + 1) * P, :], x1[:, t, :]).then_inc(stored, 16)
            sp.wait_ge(added, TILES + 1)
            sp.dma_start(y_sample, x1[0:NS, TILES, :]).then_inc(stored, 16)
            sp.wait_ge(stored, 16 * (TILES + 1))


def stage_spill(nc, tag, x, dram):
    with ExitStack() as es:
        stored = new_sem(nc, es, tag + "_stored")
        block = es.enter_context(stage_block(nc))

        @block.sync
        def _(sp):
            sp.dma_start(dram[0:SEQ, :].rearrange("(t p) d -> p t d", p=P), x[:, 0:TILES, :]).then_inc(stored, 16)
            sp.dma_start(dram[SEQ:T, :], x[0:NS, TILES, :]).then_inc(stored, 16)
            sp.wait_ge(stored, 32)


OUTPUTS = [("y_prompt", (1, SEQ, D)), ("y_sample", (NS, 1, D)),
           ("p_cmp_k", (1, 1, SEQ, NG, P)), ("p_cmp_v", (1, 1, SEQ, NG, P)), ("p_sel_k", (1, 1, SEQ, NG, P)),
           ("p_sel_v", (1, 1, SEQ, NG, P)), ("p_win_k", (1, 1, WIN, NG, P)), ("p_win_v", (1, 1, WIN, NG, P)),
           ("p_ret", (1, 1, RH, P, RDV)), ("p_mem_k", (1, 1, NM, MH, MD)), ("p_mem_v", (1, 1, NM, MH, MD)),
           ("s_cmp_k", (1, NS, 1, NG, P)), ("s_cmp_v", (1, NS, 1, NG, P)), ("s_sel_k", (1, NS, 1, NG, P)),
           ("s_sel_v", (1, NS, 1, NG, P)), ("s_win_k", (1, NS, WIN, NG, P)), ("s_win_v", (1, NS, WIN, NG, P)),
           ("s_ret", (1, NS, RH, P, RDV))]


def trunk(nc, i, c, o, debug=None, upto=99):
    n = Net()
    nc._stage_sems = []
    n.c, n.i, n.o = c, i, o
    with ExitStack() as es:
        n.base = es.enter_context(nc.sbuf_tensor("base", [P, 2 * P], F32))
        n.ident, n.ones = n.base[:, 0:P], n.base[:, P:2 * P]
        nc._eps_tile = es.enter_context(nc.sbuf_tensor("eps", [P, 1], F32))
        n.table = es.enter_context(nc.sbuf_tensor("table", [1, NS * PAGES], I32))
        scratch = nc.dram_tensor("gate_rows", (NS, 3 * NH), F32, kind="Internal").ap()
        x1d = nc.dram_tensor("x_after_attention", (T, D), F32, kind="Internal").ap()
        stage_load_consts(nc, n)
        front = es.enter_context(ExitStack())
        hT = front.enter_context(nc.sbuf_tensor("hT", [P, KD, T], F32))
        oT = front.enter_context(nc.sbuf_tensor("oT", [P, 24, T], F32))
        w_in = i["w_in"][0]
        xp = i["x_prompt"][0]
        xs = i["x_sample"].rearrange("b o d -> (b o) d")
        tiles = [(xp[t * P:(t + 1) * P, :], P, t * P) for t in range(TILES)] + [(xs, NS, SEQ)]
        stage_norm(nc, "na", tiles, i["norm_attn"][0], hT, n.ident)
        with nc.sbuf_tensor("Zr", [P, 24, T], F32) as Z:
            stage_project(nc, "pr", w_in, C_RQ, 24, hT, Z, 0)
            stage_rope(nc, "rr", Z, [(0, 8)], c["rope_ret"], n.ones)
            stage_retention(nc, "rt", n, Z, oT, o["p_ret"][0, 0])
            stage_retention_sample(nc, "rs", n, Z, oT, i["state_ret"][0], o["s_ret"][0])
            stage_retention_gate(nc, "rg", n, Z, oT, i["ret_gn"][0])
            if debug == "ret": return dump(nc, n, oT[:, 0:8, :])
        with ExitStack() as nsa:
            sb = lambda name, shape, dt=F32: nsa.enter_context(nc.sbuf_tensor(name, shape, dt))
            rows, srows = sb("rows", [P, 12, TILES, P]), sb("srows", [NS, 12, P])
            gt, gts, grow = sb("gt", [P, TILES, 3 * NH]), sb("gts", [NS, 3 * NH]), sb("grow", [ROWS, 3])
            ck, cv = sb("ck", [P, 288]), sb("cv", [P, 288])
            cvp, cvs = sb("cvp", [NCMP, NG, P]), sb("cvs", [P, 2, P])
            Z = sb("Zn", [P, 20, T])
            stage_gates(nc, "ga", n, hT, w_in, gt, gts, scratch, grow)
            stage_project(nc, "pn", w_in, C_NQ, 20, hT, Z, 0)
            kn = i["nsa_k_norm"][0]
            stage_rope(nc, "rn", Z, [(0, 8), (8, 10), (12, 14), (16, 18)], c["rope_nsa"], n.ones,
                       norm_gain=[i["nsa_q_norm"][0], kn[0], kn[1], kn[2]], gain_of=[0, 1, 2, 3])
            stage_rows(nc, "ro", Z, 8, 12, n.ident, rows, srows)
            stage_store_rows(nc, "sr", n, rows, srows)
            stage_compress(nc, "ck", n, Z, 8, i["cache_cmp_k"][0], i["cmp_pos_k"][0], i["cmp_w_k"][0], ck)
            stage_compress(nc, "cv", n, Z, 10, i["cache_cmp_v"][0], i["cmp_pos_v"][0], i["cmp_w_v"][0], cv)
            stage_cv_rows(nc, "cr", n, cv, cvp, cvs)
            for g in range(NG):
                stage_nsa_group(nc, f"ng{g}", n, g, Z, rows, ck, cvp, gt, oT)
            sample_nsa(nc, n, Z, ck, cvs, srows, grow, oT)
            if debug == "nsa": return dump(nc, n, oT[:, 8:16, :])
        with ExitStack() as mem:
            sb = lambda name, shape, dt=F32: mem.enter_context(nc.sbuf_tensor(name, shape, dt))
            mp = i["mem_prompt"][0]
            Z = sb("Zm", [P, 8, T])
            stage_project(nc, "pm", w_in, C_MQ, 8, hT, Z, 0)
            stage_head_norm(nc, "mn", n, Z, MH, i["mem_q_norm"][0], T)
            M = sb("M", [P, 16, NM])
            with nc.sbuf_tensor("hm", [P, KD, NM], F32) as hm:
                stage_norm(nc, "nm", [(mp[t * P:(t + 1) * P, :], P, t * P) for t in range(2)], i["norm_mem"][0], hm, n.ident)
                stage_project(nc, "pk", i["w_mem_kv"][0], 0, 16, hm, M, 0, cols=NM)
            stage_head_norm(nc, "mk", n, M, MH, i["mem_k_norm"][0], NM)
            krows, vrows = sb("krows", [P, 2, MH * MD]), sb("vrows", [P, 2, MH * MD])
            stage_memory_rows(nc, "m1", n, M, 0, krows, o["p_mem_k"][0, 0])
            stage_memory_rows(nc, "m2", n, M, 8, vrows, o["p_mem_v"][0, 0])
            stage_memory_attend(nc, "ma", n, Z, M, vrows, oT)
            sample_memory(nc, n, Z, oT)
            if debug == "mem": return dump(nc, n, oT[:, 16:24, :])

        mT = front.enter_context(nc.sbuf_tensor("mT", [P, KD, T], F32))
        stage_merge(nc, "mg", n, hT, oT, w_in, i["w_branch"][0], mT)
        stage_project(nc, "po", i["w_out"][0], 0, KD, mT, hT, 0)
        with nc.sbuf_tensor("xa", [P, TILES + 1, D], F32) as xa:
            stage_residual(nc, "re", n, hT, tiles, xa)
            stage_spill(nc, "sp", xa, x1d)
        front.close()
        x1, h2 = [es.enter_context(nc.sbuf_tensor(name, [P, TILES + 1, D], F32)) for name in ("x1", "h2")]
        qT = es.enter_context(nc.sbuf_tensor("qT", [P, PH, T], F32))
        sk = es.enter_context(nc.sbuf_tensor("sk", [P, PH, PK], F32))
        with nc.sbuf_tensor("h2T", [P, KD, T], F32) as h2T:
            x1tiles = [(x1d[t * P:t * P + rows, :], rows, t * P) for t, (_s, rows, _c) in enumerate(tiles)]
            stage_norm(nc, "nf", x1tiles, i["norm_ffn"][0], h2T, n.ident, keep=h2)
            stage_project(nc, "pq", i["peer_wq"][0], 0, PH, h2T, qT, 0)
        if debug == "q": return dump(nc, n, qT[:, :, :])
        stage_subkeys(nc, "su", n, i["peer_subkeys"][0], sk)
        stage_experts(nc, "ex", n, i["peer_u"][0], i["peer_v"][0], qT, sk, h2, x1, x1d, o["y_prompt"][0],
                      o["y_sample"].rearrange("b o d -> (b o) d"))


def dump(nc, n, ap):
    with nc.semaphore("dump") as s, nc.Block() as block:
        @block.sync
        def _(sp):
            sp.dma_start(n.o["dbg"], ap).then_inc(s, 16)
            sp.wait_ge(s, 16)


def kernel(**inputs):
    import concourse.bacc as bacc
    from concourse.bass_utils import run_bass_kernel_spmd

    nc = bacc.Bacc("TRN2", target_bir_lowering=False, num_devices=1)
    arrays, ins, consts, outs = {}, {}, {}, {}
    for name, a in inputs.items():
        a = np.ascontiguousarray(a)
        arrays["in_" + name] = a
        ins[name] = nc.dram_tensor("in_" + name, a.shape, mybir.dt.from_np(a.dtype), kind="ExternalInput").ap()
    for name, a in host_constants().items():
        arrays["const_" + name] = a
        consts[name] = nc.dram_tensor("const_" + name, a.shape, F32, kind="ExternalInput").ap()
    for name, shape in OUTPUTS:
        outs[name] = nc.dram_tensor("out_" + name, shape, F32, kind="ExternalOutput").ap()
    trunk(nc, ins, consts, outs)
    r = run_bass_kernel_spmd(nc, [arrays], core_ids=[0])
    return tuple(r.results[0]["out_" + name] for name, _ in OUTPUTS)
```

```python
from contextlib import ExitStack, contextmanager

import numpy as np
import concourse.bass as bass
import concourse.mybir as mybir

F32 = mybir.dt.float32
I32 = mybir.dt.int32
U32 = mybir.dt.uint32
ACT = mybir.ActivationFunctionType
ALU = mybir.AluOpType
AX = mybir.AxisListType

P = 128
D = 2048
KD = D // P
SEQ, NS = 512, 8
T = SEQ + NS
HALF = T // 2
TILES = SEQ // P
RH, RDV = 4, 256
NH, NG, HG = 8, 2, 4
PAST, PAGES, N_POOL = 512, 4, 40
CMP, NCMP = 32, 16
WIN = 256
NM, MH, MD = 256, 4, 256
PH, PK, TOPK = 8, 128, 16
PICKS = PH * TOPK
EPS = 1e-6
NEG = -1e30
FORCE = 1e4
C_RQ, C_RK, C_RV, C_RG, C_NQ, C_KV, C_NG, C_MQ, C_MG = 0, 512, 1024, 2048, 3072, 4096, 5632, 5656, 6680
ROWS = NS * NH


def host_constants():
    f = np.float32
    c = {}
    ident = np.eye(P, dtype=f)
    c["base"] = np.concatenate([ident, np.ones((P, P), f)], 1)
    pos = np.concatenate([np.arange(SEQ), np.full(NS, PAST)]).astype(f)

    def rope(rot, theta):
        half = rot // 2
        inv = (f(theta) ** (-np.arange(half, dtype=f) * f(2.0) / f(rot))).astype(f)
        ang = (pos[None, :] * inv[:, None]).astype(f)
        cos, sin = np.ones((P, T), f), np.zeros((P, T), f)
        cos[:half] = cos[half:rot] = np.cos(ang)
        sin[:half] = sin[half:rot] = np.sin(ang)
        swap = np.zeros((P, P), f)
        for p in range(half):
            swap[p + half, p] = -1.0
            swap[p, p + half] = 1.0
        return np.concatenate([swap, cos, sin], 1)

    c["rope_ret"] = rope(128, 10000.0)
    c["rope_nsa"] = rope(32, 500000.0)
    gamma = 1.0 - 2.0 ** (-5.0 - np.arange(RH))
    i = np.arange(P)
    s = 128.0 ** -0.5
    rel = i[None, :] - i[:, None]
    dec = np.stack([np.where(rel >= 0, g ** np.maximum(rel, 0), 0.0) * s for g in gamma], 1)
    cross = np.broadcast_to(np.stack([g ** (i + 1.0) for g in gamma])[None], (P, RH, P))
    kdec = np.stack([g ** (P - 1.0 - i) * s for g in gamma], 1)
    gc = np.broadcast_to((gamma ** P)[None], (P, RH))
    c["ret"] = np.concatenate([dec.reshape(P, -1), cross.reshape(P, -1), kdec, gc], 1).astype(f)
    q = np.arange(P)[:, None]
    x = np.arange(896)[None]
    causal = np.where(x - 384 <= q, 0.0, NEG)
    x = np.arange(384)[None]
    dist = q - (x - 256)
    winb = np.where((dist >= 0) & (dist <= WIN), 0.0, NEG)
    qpos = (np.arange(TILES)[None, :] * P + np.arange(P)[:, None])[:, :, None]
    vis = (np.arange(NCMP) + 1) * CMP - 1 <= qpos
    blk = np.arange(8)
    forced = (blk == 0) | (blk == qpos // 64)
    valid = blk * 64 <= qpos
    vmask = (valid & ~forced) * 1.0
    vadd = np.where(forced, FORCE, np.where(valid, 0.0, -FORCE))
    c["nsa"] = np.concatenate([causal, winb, np.where(vis, 0.0, NEG).reshape(P, -1), (vis * 1.0).reshape(P, -1),
                               vmask.reshape(P, -1), vadd.reshape(P, -1),
                               np.broadcast_to(np.arange(9.0)[None], (P, 9))], 1).astype(f)
    row = np.arange(ROWS)
    unit = row // HG
    colu = np.arange(NS * NG * NCMP) // NCMP
    own = unit[:, None] == colu[None]
    same = unit[:, None] == unit[None]
    gb = np.arange(NG * NS)
    mine = (unit[:, None] // NG == gb[None] % NS) & (unit[:, None] % NG == gb[None] // NS)
    vm = np.ones((ROWS, 9)); vm[:, 0] = vm[:, 8] = 0
    va = np.zeros((ROWS, 9)); va[:, 0] = va[:, 8] = FORCE
    c["smp"] = np.concatenate([np.where(own, 0.0, NEG), same * 1.0, mine * 1.0, vm, va,
                               np.broadcast_to(np.arange(9.0)[None], (ROWS, 9))], 1).astype(f)
    c["peer"] = np.broadcast_to(np.arange(16.0, dtype=f)[None], (P, 16)).copy()
    onehot = np.zeros((NS, NS, P), f)
    for b in range(NS):
        onehot[b, b] = 1.0
    c["onehot"] = onehot.reshape(NS, NS * P)
    return c


def rows2(ap, g0):
    return ap[:, g0, :, 0:HALF]


def halves(ap):
    return ap.rearrange("p (a b) -> p a b", a=2)


def new_sem(nc, es, name):
    s = es.enter_context(nc.semaphore(name))
    nc._stage_sems.append(s)
    return s


@contextmanager
def stage_block(nc):
    sems, nc._stage_sems = nc._stage_sems, []
    with nc.Block() as block:
        yield block
    for s in sems:
        nc.gpsimd.sem_clear(s)
    nc.all_engine_barrier()


class Net:
    pass


def stage_load_consts(nc, n):
    with ExitStack() as es:
        n.s_base = new_sem(nc, es, "base_loaded")
        block = es.enter_context(stage_block(nc))

        @block.sync
        def _(sp):
            sp.dma_start(n.base[:, :], n.c["base"]).then_inc(n.s_base, 16)
            sp.dma_start(n.table[:, :], n.i["page_table"].rearrange("(o b) g -> o (b g)", o=1)).then_inc(n.s_base, 16)
            sp.wait_ge(n.s_base, 32)

        @block.gpsimd
        def _(pool):
            nc.gpsimd.memset(n_eps(nc)[:, :], EPS)


def stage_norm(nc, tag, tiles, gain, hT, ident, keep=None):
    with ExitStack() as es:
        xt = es.enter_context(nc.sbuf_tensor(tag + "_x", [P, 2, D], F32))
        sq = es.enter_context(nc.sbuf_tensor(tag + "_sq", [P, D], F32))
        gcol = es.enter_context(nc.sbuf_tensor(tag + "_g", [P, KD], F32))
        st = es.enter_context(nc.sbuf_tensor(tag + "_st", [P, 2, 3], F32))
        grow = es.enter_context(nc.sbuf_tensor(tag + "_gr", [P, D], F32)) if keep is not None else None
        ps = es.enter_context(nc.psum_tensor(tag + "_ps", [P, 2, 4, 512], F32))
        loaded = [new_sem(nc, es, f"{tag}_loaded{i}") for i in range(2)]
        g_loaded = new_sem(nc, es, tag + "_g_loaded")
        root_done = new_sem(nc, es, tag + "_root_done")
        scaled = new_sem(nc, es, tag + "_scaled")
        turned = new_sem(nc, es, tag + "_turned")
        saved = new_sem(nc, es, tag + "_saved")
        block = es.enter_context(stage_block(nc))

        @block.sync
        def _(sp):
            sp.dma_start(gcol[:, :], gain.rearrange("(k p) -> p k", p=P), allow_slow_non_contiguous=True).then_inc(g_loaded, 16)
            if keep is not None:
                sp.dma_start(grow[:, :], gain.rearrange("(o d) -> o d", o=1).to_broadcast([P, D])).then_inc(g_loaded, 16)
            for i, (src, rows, _c) in enumerate(tiles):
                if i >= 2:
                    sp.wait_ge(turned, i - 1)
                sp.dma_start(xt[0:rows, i % 2, :], src).then_inc(loaded[i % 2], 16)

        @block.scalar
        def _(act):
            for i, (_s, rows, _c) in enumerate(tiles):
                act.wait_ge(loaded[i % 2], 16 * (i // 2 + 1))
                nc.scalar.activation(sq[0:rows, :], xt[0:rows, i % 2, :], ACT.Square,
                                     accum_out=st[0:rows, i % 2, 0:1])
                act.drain()
                nc.scalar.activation(st[0:rows, i % 2, 1:2], st[0:rows, i % 2, 0:1], ACT.Sqrt,
                                     scale=1.0 / D, bias=n_eps(nc)[0:rows, :]).then_inc(root_done, 1)

        @block.vector
        def _(dve):
            dve.wait_ge(g_loaded, 16 if keep is None else 32)

            def scale(i):
                rows = tiles[i][1]
                dve.wait_ge(root_done, i + 1)
                nc.vector.reciprocal(st[0:rows, i % 2, 2:3], st[0:rows, i % 2, 1:2])
                dve.drain()
                if keep is not None:
                    nc.vector.scalar_tensor_tensor(keep[0:rows, i, :], xt[0:rows, i % 2, :], st[0:rows, i % 2, 2:3],
                                                   grow[0:rows, :], ALU.mult, ALU.mult)
                nc.vector.tensor_scalar(xt[0:rows, i % 2, :], xt[0:rows, i % 2, :], st[0:rows, i % 2, 2:3], None,
                                        ALU.mult).then_inc(scaled, 1)

            scale(0)
            for i, (_s, rows, col) in enumerate(tiles):
                if i + 1 < len(tiles):
                    scale(i + 1)
                dve.wait_ge(turned, i + 1)
                for b in range(4):
                    last = nc.vector.tensor_tensor(
                        hT[:, 4 * b:4 * b + 4, col:col + rows],
                        ps[:, i % 2, b, :].rearrange("p (k t) -> p k t", k=4)[:, :, 0:rows],
                        gcol[:, 4 * b:4 * b + 4].unsqueeze(2).to_broadcast([P, 4, rows]), ALU.mult)
                last.then_inc(saved, 1)

        @block.tensor
        def _(pe):
            for i, (_s, rows, _c) in enumerate(tiles):
                pe.wait_ge(scaled, i + 1)
                if i >= 2:
                    pe.wait_ge(saved, i - 1)
                for k in range(KD):
                    last = nc.tensor.transpose(ps[:, i % 2, k // 4, (k % 4) * P:(k % 4) * P + rows],
                                               xt[0:rows, i % 2, k * P:(k + 1) * P], ident[0:rows, 0:rows])
                last.then_inc(turned, 1)


def n_eps(nc):
    return nc._eps_tile


class Finish:

    def __init__(self, kind, steps, ones, gains=(), table=None, tail=False):
        self.kind, self.steps, self.ones, self.gains, self.table, self.tail = kind, steps, ones, gains, table, tail


def stage_project(nc, tag, w, col0, nblk, src, dst, dst0, nk=KD, cols=T, finish=None):
    parts = 2 if cols > 512 else 1
    half = cols // parts
    kind = finish.kind if finish else None
    norm, rope = kind in ("norm", "norm_rope"), kind in ("rope", "norm_rope")
    width = MD if kind == "norm" else P
    steps = finish.steps if finish else [(nblk // 2, [(0, 1, False, (0, 0))])]
    with ExitStack() as es:
        sb = lambda name, shape: es.enter_context(nc.sbuf_tensor(f"{tag}_{name}", shape, F32))
        sem = lambda name: new_sem(nc, es, f"{tag}_{name}")
        wt = sb("w", [P, 2, nk, P])
        ps = es.enter_context(nc.psum_tensor(tag + "_ps", [P, 2, parts, 512], F32))
        loaded = [sem(f"loaded{i}") for i in range(2)]
        ps_free, summed = sem("ps_free"), sem("summed")
        if finish:
            ro = sb("ro", [P, 2, cols])
            psf = es.enter_context(nc.psum_tensor(tag + "_psf", [P, 2, parts, 512], F32))
            const_loaded, normed, turned, rooted, swapped, squared, totalled = (
                sem("const_loaded"), sem("normed"), sem("turned"), sem("rooted"), sem("swapped"), sem("squared"),
                sem("totalled"))
            sq = sb("sq", [P, 2, cols]) if norm else None
            gn = sb("gn", [P, len(finish.gains)]) if norm else None
            tab = sb("tab", [P, P + 2 * T]) if rope else None
            consts = 16 * ((1 if rope else 0) + len(finish.gains))
        block = es.enter_context(stage_block(nc))
        parted = lambda x: x.rearrange("p (a b) -> p a b", a=parts)

        @block.sync
        def _(sp):
            def load(s, i):
                sp.dma_start(wt[:, s, :, :],
                             w[:, bass.ds(i * (2 * P) + (col0 + s * P), P)].rearrange("(k p) n -> p k n", p=P)
                             ).then_inc(loaded[s], 16)

            load(0, 0)
            load(1, 0)
            if finish and rope:
                sp.dma_start(tab[:, :], finish.table).then_inc(const_loaded, 16)
            for g, gain in enumerate(finish.gains if finish else ()):
                sp.dma_start(gn[:, g:g + 1], gain.rearrange("(p o) -> p o", o=1), allow_slow_non_contiguous=True
                             ).then_inc(const_loaded, 16)
            with sp.Fori(0, nblk // 2 - 1) as i:
                for s in range(2):
                    sp.wait_ge(summed, i * 2 + (s + 1))
                    load(s, i + 1)

        def loops(engine, body, tail):
            done = 0
            for passes, steps_ in steps:
                finishes = sum(1 for st in steps_ if st[2])
                if passes == 1:
                    for first, _stride, fin, (g0, _dg) in steps_:
                        body(first, done if fin else None, g0)
                else:
                    with engine.Fori(0, passes) as r:
                        for first, stride, fin, (g0, dg) in steps_:
                            body(r * stride + first, (r + done) if fin else None, r * dg + g0 if dg else g0)
                done += finishes * passes
            if finish and finish.tail:
                tail(nblk // 2, done)

        def head(pair, e):
            return dst[:, bass.ds(pair * 2 + (dst0 - 2 + e), 1), :].rearrange("p o t -> p (o t)")

        @block.tensor
        def _(pe):
            def product(p, s):
                pe.wait_ge(loaded[s], p * 16 + 16)
                pe.wait_ge(ps_free, p * 2 + (s + 1))
                for k in range(nk):
                    for h in range(parts):
                        last = nc.tensor.matmul(ps[:, s, h, 0:half], wt[:, s, k, :],
                                                src[:, k, h * half:(h + 1) * half],
                                                start=(k == 0), stop=(k == nk - 1))
                last.then_inc(summed, 1)

            def total(f):
                pe.wait_ge(turned, f + 1)
                pe.wait_ge(squared, f + 1)
                for e in range(2):
                    for h in range(parts):
                        if kind == "norm":
                            last = nc.tensor.matmul(psf[:, 0, h, 0:half], finish.ones, sq[:, e, h * half:(h + 1) * half],
                                                    start=(e == 0), stop=(e == 1))
                        else:
                            last = nc.tensor.matmul(psf[:, e, h, 0:half], finish.ones, sq[:, e, h * half:(h + 1) * half],
                                                    start=True, stop=True)
                last.then_inc(totalled, 1)

            def swap(p, f):
                if norm:
                    pe.wait_ge(normed, f + 2)
                else:
                    pe.wait_ge(turned, f + 1)
                for e in range(2):
                    for h in range(parts):
                        last = nc.tensor.matmul(psf[:, e, h, 0:half], tab[:, 0:P], head(p, e)[:, h * half:(h + 1) * half],
                                                start=True, stop=True)
                last.then_inc(swapped, 1)

            def body(p, f, _g):
                product(p, 0)
                if f is not None and norm:
                    total(f)
                product(p, 1)
                if f is not None and rope:
                    swap(p, f)

            def tail(p, f):
                if norm:
                    total(f)
                if rope:
                    swap(p, f)

            if finish:
                pe.wait_ge(const_loaded, consts)
            loops(pe, body, tail)

        @block.scalar
        def _(act):
            def copy(p, s):
                act.wait_ge(summed, p * 2 + (s + 1))
                nc.scalar.copy(dst[:, bass.ds(p * 2 + (dst0 + s), 1), :].rearrange("p o (a b) -> p (o a) b", a=parts),
                               ps[:, s, :, 0:half]).then_inc(ps_free, 1)

            def square(p, f):
                act.wait_ge(ps_free, p * 2 + 2)
                act.wait_ge(normed, f + 1)
                for e in range(2):
                    last = nc.scalar.activation(sq[:, e, :], head(p, e), ACT.Square)
                last.then_inc(squared, 1)

            def root(f):
                act.wait_ge(totalled, f + 1)
                for e in range(1 if kind == "norm" else 2):
                    last = nc.scalar.activation(parted(sq[:, e, :]), psf[:, e, :, 0:half], ACT.Sqrt,
                                                scale=1.0 / width, bias=n_eps(nc)[:, :])
                last.then_inc(rooted, 1)

            def body(p, f, _g):
                if f is not None and norm:
                    square(p, f)
                copy(p, 0)
                if f is not None and norm:
                    root(f)
                copy(p, 1)

            def tail(p, f):
                if norm:
                    square(p, f)
                    root(f)

            act.sem_inc(ps_free, 2)
            loops(act, body, tail)

        @block.vector
        def _(dve):
            def body(p, f, g):
                if f is None:
                    return
                if norm:
                    dve.wait_ge(rooted, f + 1)
                    used = 1 if kind == "norm" else 2
                    nc.vector.reciprocal(ro[:, 0:used, :], sq[:, 0:used, :])
                    dve.drain()
                    for e in range(2):
                        gain = gn[:, e:e + 1] if kind == "norm" else gn[:, g:g + 1] if isinstance(g, int) else gn[:, bass.ds(g, 1)]
                        last = nc.vector.scalar_tensor_tensor(head(p, e), head(p, e), gain, ro[:, e % used, :],
                                                              ALU.mult, ALU.mult)
                    last.then_inc(normed, 1)
                if rope:
                    dve.wait_ge(swapped, f + 1)
                    for e in range(2):
                        nc.vector.tensor_tensor(parted(ro[:, e, :]), psf[:, e, :, 0:half], parted(tab[:, P + T:P + 2 * T]), ALU.mult)
                        nc.vector.tensor_tensor(head(p, e), head(p, e), tab[:, P:P + T], ALU.mult)
                    dve.drain()
                    for e in range(2):
                        last = nc.vector.tensor_tensor(head(p, e), head(p, e), ro[:, e, :], ALU.add)
                    last.then_inc(turned, 1)
                else:
                    dve.sem_inc(turned, 1)
                dve.drain()

            if finish:
                dve.sem_inc(normed, 1)
                dve.sem_inc(turned, 1)
                dve.wait_ge(const_loaded, consts)
                loops(dve, body, lambda p, f: body(p, f, 0))


def stage_rows(nc, tag, Z, b0, nblk, ident, rows, srows):
    with ExitStack() as es:
        zs = es.enter_context(nc.sbuf_tensor(tag + "_zs", [P, 2, T], F32))
        ps = es.enter_context(nc.psum_tensor(tag + "_ps", [P, 2, 2, 512], F32))
        staged = new_sem(nc, es, tag + "_staged")
        turned = new_sem(nc, es, tag + "_turned")
        saved = new_sem(nc, es, tag + "_saved")
        block = es.enter_context(stage_block(nc))

        @block.scalar
        def _(act):
            act.sem_inc(saved, 2)
            with act.Fori(0, nblk // 2) as i:
                for s in range(2):
                    act.wait_ge(saved, i * 2 + (s + 1))
                    nc.scalar.copy(zs[:, s, :], Z[:, bass.ds(i * 2 + (b0 + s), 1), :].rearrange("p o t -> p (o t)")
                                   ).then_inc(staged, 1)

        @block.tensor
        def _(pe):
            with pe.Fori(0, nblk // 2) as i:
                for s in range(2):
                    pe.wait_ge(staged, i * 2 + (s + 1))
                    for t in range(TILES):
                        nc.tensor.transpose(ps[:, s, 0, t * P:(t + 1) * P], zs[:, s, t * P:(t + 1) * P], ident)
                    nc.tensor.transpose(ps[0:NS, s, 1, 0:P], zs[:, s, SEQ:T], ident).then_inc(turned, 1)

        @block.vector
        def _(dve):
            with dve.Fori(0, nblk // 2) as i:
                for s in range(2):
                    dve.wait_ge(turned, i * 2 + (s + 1))
                    nc.vector.tensor_copy(srows[:, bass.ds(i * 2 + s, 1), :].rearrange("p o t -> p (o t)"), ps[0:NS, s, 1, 0:P])
                    nc.vector.tensor_copy(rows[:, bass.ds(i * 2 + s, 1), :, :].rearrange("p o t d -> p (o t) d"),
                                          ps[:, s, 0, :].rearrange("p (t d) -> p t d", d=P)).then_inc(saved, 1)


def stage_retention(nc, tag, n, Z, oT, p_ret):
    with ExitStack() as es:
        sb = lambda name, shape: es.enter_context(nc.sbuf_tensor(f"{tag}_{name}", shape, F32))
        sem = lambda name: new_sem(nc, es, f"{tag}_{name}")
        con = sb("con", [P, 1024 + 8])
        ks, vs, qd = sb("ks", [P, SEQ]), sb("vs", [P, 2, SEQ]), sb("qd", [P, SEQ])
        vt, kt, at = sb("vt", [P, RDV]), sb("kt", [P, P]), sb("at", [P, P])
        state = sb("state", [P, RDV])
        ps_v = es.enter_context(nc.psum_tensor(tag + "_psv", [P, 512], F32))
        ps_i = es.enter_context(nc.psum_tensor(tag + "_psi", [P, 512], F32))
        ps_o = es.enter_context(nc.psum_tensor(tag + "_pso", [P, 2, 512], F32))
        ps_s = es.enter_context(nc.psum_tensor(tag + "_pss", [P, 512], F32))
        loaded, staged, scored, rowed, summed, head_done, stored = (
            sem("loaded"), sem("staged"), sem("scored"), sem("rowed"), sem("summed"), sem("head_done"), sem("stored"))
        block = es.enter_context(stage_block(nc))
        dec, cross = con[:, 0:512], con[:, 512:1024]
        kdec, gc = con[:, 1024:1028], con[:, 1028:1032]

        @block.sync
        def _(sp):
            sp.dma_start(con[:, :], n.c["ret"]).then_inc(loaded, 16)
            with sp.Fori(0, RH) as h:
                sp.wait_ge(head_done, h + 1)
                sp.dma_start(p_ret[bass.ds(h, 1), :, :].rearrange("o d e -> d (o e)"), state[:, :]).then_inc(stored, 16)
            sp.wait_ge(stored, 16 * RH + 16)

        @block.scalar
        def _(act):
            with act.Fori(0, RH) as h:
                nc.scalar.copy(ks[:, :], Z[:, bass.ds(h + 4, 1), 0:SEQ].rearrange("p o t -> p (o t)"))
                nc.scalar.copy(vs[:, :, :], Z[:, bass.ds(h * 2 + 8, 2), 0:SEQ]).then_inc(staged, 1)
                act.wait_ge(summed, h * TILES + TILES)

        @block.tensor
        def _(pe):
            with pe.Fori(0, RH) as h:
                pe.wait_ge(staged, h + 1)
                for c in range(TILES):
                    cc = slice(c * P, (c + 1) * P)
                    for e in range(2):
                        nc.tensor.transpose(ps_v[:, e * P:(e + 1) * P], vs[:, e, cc], n.ident)
                    nc.tensor.transpose(ps_v[:, 256:384], ks[:, cc], n.ident)
                    nc.tensor.matmul(ps_i[:, 0:P], ks[:, cc], Z[:, bass.ds(h, 1), cc].rearrange("p o t -> p (o t)"),
                                     start=True, stop=True).then_inc(scored, 1)
                    pe.wait_ge(rowed, h * TILES + (c + 1))
                    for e in range(2):
                        nc.tensor.matmul(ps_o[:, e, 0:P], vt[:, e * P:(e + 1) * P], at[:, :], start=True, stop=(c == 0))
                        if c:
                            nc.tensor.matmul(ps_o[:, e, 0:P], state[:, e * P:(e + 1) * P], qd[:, cc],
                                             start=False, stop=True)
                    nc.tensor.matmul(ps_s[:, 0:RDV], kt[:, :], vt[:, :], start=True, stop=True).then_inc(summed, 1)

        @block.vector
        def _(dve):
            dve.wait_ge(loaded, 16)
            dve.sem_inc(stored, 16)
            with dve.Fori(0, RH) as h:
                nc.vector.tensor_tensor(
                    qd[:, :].rearrange("p (c t) -> p c t", c=TILES),
                    Z[:, bass.ds(h, 1), 0:SEQ].rearrange("p o (c t) -> p (o c) t", c=TILES),
                    cross[:, bass.ds(h * P, P)].unsqueeze(1).to_broadcast([P, TILES, P]), ALU.mult)
                for c in range(TILES):
                    dve.wait_ge(scored, h * TILES + (c + 1))
                    nc.vector.tensor_copy(vt[:, :], ps_v[:, 0:256])
                    nc.vector.tensor_scalar(kt[:, :], ps_v[:, 256:384], kdec[:, bass.ds(h, 1)], None, ALU.mult)
                    nc.vector.tensor_tensor(at[:, :], ps_i[:, 0:P], dec[:, bass.ds(h * P, P)], ALU.mult).then_inc(rowed, 1)
                    dve.wait_ge(summed, h * TILES + (c + 1))
                    nc.vector.tensor_copy(oT[:, bass.ds(h * 2, 2), c * P:(c + 1) * P], ps_o[:, :, 0:P])
                    if c == 0:
                        dve.wait_ge(stored, h * 16 + 16)
                        nc.vector.tensor_copy(state[:, :], ps_s[:, 0:RDV])
                    else:
                        nc.vector.scalar_tensor_tensor(state[:, :], state[:, :], gc[:, bass.ds(h, 1)],
                                                       ps_s[:, 0:RDV], ALU.mult, ALU.add)
                    dve.drain()
                dve.sem_inc(head_done, 1)


def stage_retention_sample(nc, tag, n, Z, oT, state_in, s_ret):
    gamma = [1.0 - 2.0 ** (-5.0 - h) for h in range(RH)]
    with ExitStack() as es:
        sb = lambda name, shape: es.enter_context(nc.sbuf_tensor(f"{tag}_{name}", shape, F32))
        sem = lambda name: new_sem(nc, es, f"{tag}_{name}")
        ktok, vtok, kone = sb("ktok", [NS, RH, P]), sb("vtok", [NS, RH, RDV]), sb("kone", [NS, 2, RH, P])
        st = sb("st", [P, 2, RH, RDV])
        new = sb("new", [P, 2, RH, RDV])
        ps_t = es.enter_context(nc.psum_tensor(tag + "_pst", [P, 2, 512], F32))
        ps_k = es.enter_context(nc.psum_tensor(tag + "_psk", [P, 2, RH * RDV], F32))
        ps_o = es.enter_context(nc.psum_tensor(tag + "_pso", [P, 2, 512], F32))
        turned, rowed, masked, outer, updated, summed, saved = (
            sem("turned"), sem("rowed"), sem("masked"), sem("outer"), sem("updated"), sem("summed"), sem("saved"))
        loaded, stored = [sem(f"loaded{i}") for i in range(2)], [sem(f"stored{i}") for i in range(2)]
        block = es.enter_context(stage_block(nc))

        def moved(x, b):
            return x[bass.ds(b, 1), :, :, :].rearrange("o h d e -> d (o h) e")

        @block.sync
        def _(sp):
            def load(b, s):
                sp.dma_start(st[:, s, :, :], moved(state_in, b)).then_inc(loaded[s], 16)

            load(0, 0)
            load(1, 1)
            with sp.Fori(0, NS // 2 - 1) as i:
                for s in range(2):
                    sp.wait_ge(updated, i * 2 + (s + 1))
                    sp.dma_start(moved(s_ret, i * 2 + s), new[:, s, :, :]).then_inc(stored[s], 16)
                    load(i * 2 + (s + 2), s)
            for s in range(2):
                sp.wait_ge(updated, NS - 1 + s)
                sp.dma_start(moved(s_ret, NS - 2 + s), new[:, s, :, :]).then_inc(stored[s], 16)
            for s in range(2):
                sp.wait_ge(stored[s], 16 * (NS // 2) + 16)

        @block.tensor
        def _(pe):
            for h in range(RH):
                nc.tensor.transpose(ps_t[0:NS, 0, h * P:(h + 1) * P], Z[:, 4 + h, SEQ:T], n.ident)
            for i in range(4):
                nc.tensor.transpose(ps_t[0:NS, 1, i * P:(i + 1) * P], Z[:, 8 + i, SEQ:T], n.ident)
            for i in range(4):
                last = nc.tensor.transpose(ps_o[0:NS, 0, i * P:(i + 1) * P], Z[:, 12 + i, SEQ:T], n.ident)
            last.then_inc(turned, 1)
            pe.wait_ge(rowed, 1)
            def outer_products(s):
                for h in range(RH):
                    last = nc.tensor.matmul(ps_k[:, s, h * RDV:(h + 1) * RDV], kone[:, s, h, :], vtok[:, h, :],
                                            start=True, stop=True)
                last.then_inc(outer, 1)

            def outputs(b, s):
                for h in range(RH):
                    for e in range(2):
                        last = nc.tensor.matmul(ps_o[:, s, 2 * h + e:2 * h + e + 1], new[:, s, h, e * P:(e + 1) * P],
                                                Z[:, h, bass.ds(b + SEQ, 1)], start=True, stop=True)
                last.then_inc(summed, 1)

            pe.wait_ge(masked, 1)
            outer_products(0)
            with pe.Fori(0, NS // 2 - 1) as i:
                for s in range(2):
                    pe.wait_ge(masked, i * 2 + (s + 2))
                    outer_products(1 - s)
                    pe.wait_ge(updated, i * 2 + (s + 1))
                    pe.wait_ge(saved, i * 2 + (s + 1))
                    outputs(i * 2 + s, s)
            pe.wait_ge(masked, NS)
            outer_products(1)
            for s in range(2):
                pe.wait_ge(updated, NS - 1 + s)
                pe.wait_ge(saved, NS - 1 + s)
                outputs(NS - 2 + s, s)

        @block.scalar
        def _(act):
            act.sem_inc(saved, 2)
            with act.Fori(0, NS // 2) as i:
                for s in range(2):
                    act.wait_ge(summed, i * 2 + (s + 1))
                    nc.scalar.copy(oT[:, 0:8, bass.ds(i * 2 + (SEQ + s), 1)].rearrange("p k o -> p (k o)"),
                                   ps_o[:, s, 0:8]).then_inc(saved, 1)

        @block.vector
        def _(dve):
            dve.wait_ge(turned, 1)
            nc.vector.tensor_scalar(ktok[:, :, :], ps_t[0:NS, 0, :].rearrange("p (h d) -> p h d", h=RH), P ** -0.5, None, ALU.mult)
            nc.vector.tensor_copy(vtok[:, 0:2, :], ps_t[0:NS, 1, :].rearrange("p (h d) -> p h d", h=2))
            nc.vector.tensor_copy(vtok[:, 2:4, :], ps_o[0:NS, 0, :].rearrange("p (h d) -> p h d", h=2)).then_inc(rowed, 1)
            dve.drain()

            def mask_key(b, s):
                nc.vector.tensor_scalar(kone[:, s, :, :], ktok[:, :, :], n.ident[0:NS, bass.ds(b, 1)], None,
                                        ALU.mult).then_inc(masked, 1)

            def update(i, s):
                dve.wait_ge(outer, i * 2 + (s + 1))
                dve.wait_ge(loaded[s], i * 16 + 16)
                dve.wait_ge(stored[s], i * 16 + 16)
                dve.wait_ge(saved, i * 2 + (s + 1))
                for h in range(RH):
                    last = nc.vector.scalar_tensor_tensor(new[:, s, h, :], st[:, s, h, :], gamma[h],
                                                          ps_k[:, s, h * RDV:(h + 1) * RDV], ALU.mult, ALU.add)
                last.then_inc(updated, 1)

            for s in range(2):
                dve.sem_inc(stored[s], 16)
            mask_key(0, 0)
            with dve.Fori(0, NS // 2 - 1) as i:
                for s in range(2):
                    mask_key(i * 2 + (s + 1), 1 - s)
                    update(i, s)
            mask_key(NS - 1, 1)
            update(NS // 2 - 1, 0)
            update(NS // 2 - 1, 1)


def stage_retention_gate(nc, tag, n, Z, oT, gain):
    with ExitStack() as es:
        sb = lambda name, shape: es.enter_context(nc.sbuf_tensor(f"{tag}_{name}", shape, F32))
        sem = lambda name: new_sem(nc, es, f"{tag}_{name}")
        gn, sq, ro, sg = sb("gn", [P, 8]), sb("sq", [P, 2, 2, T]), sb("ro", [P, T]), sb("sg", [P, 2, 2, T])
        ps = es.enter_context(nc.psum_tensor(tag + "_ps", [P, 2, 2, 512], F32))
        loaded, squared, summed, rooted, gated = sem("loaded"), sem("squared"), sem("summed"), sem("rooted"), sem("gated")
        block = es.enter_context(stage_block(nc))

        @block.sync
        def _(sp):
            sp.dma_start(gn[:, :], gain.rearrange("h (e p) -> p (h e)", p=P), allow_slow_non_contiguous=True).then_inc(loaded, 16)

        @block.scalar
        def _(act):
            act.sem_inc(gated, 2)
            with act.Fori(0, RH // 2) as i:
                for s in range(2):
                    act.wait_ge(gated, i * 2 + (s + 1))
                    nc.scalar.activation(sq[:, s, :, :], oT[:, bass.ds(i * 4 + 2 * s, 2), :], ACT.Square).then_inc(squared, 1)
                for s in range(2):
                    nc.scalar.activation(sg[:, s, :, :], Z[:, bass.ds(i * 4 + (16 + 2 * s), 2), :], ACT.Sigmoid)
                for s in range(2):
                    act.wait_ge(summed, i * 2 + (s + 1))
                    nc.scalar.activation(halves(sq[:, s, 0, :]), ps[:, s, :, 0:HALF], ACT.Sqrt, scale=1.0 / RDV,
                                         bias=n_eps(nc)[:, :]).then_inc(rooted, 1)

        @block.tensor
        def _(pe):
            with pe.Fori(0, RH // 2) as i:
                for s in range(2):
                    pe.wait_ge(squared, i * 2 + (s + 1))
                    for half in range(2):
                        for e in range(2):
                            last = nc.tensor.matmul(ps[:, s, half, 0:HALF], n.ones, sq[:, s, e, half * HALF:(half + 1) * HALF],
                                                    start=(e == 0), stop=(e == 1))
                    last.then_inc(summed, 1)

        @block.vector
        def _(dve):
            dve.wait_ge(loaded, 16)
            with dve.Fori(0, RH // 2) as i:
                for s in range(2):
                    dve.wait_ge(rooted, i * 2 + (s + 1))
                    nc.vector.reciprocal(ro[:, :], sq[:, s, 0, :])
                    nc.vector.tensor_tensor(sg[:, s, :, :], sg[:, s, :, :], Z[:, bass.ds(i * 4 + (16 + 2 * s), 2), :], ALU.mult)
                    dve.drain()
                    for e in range(2):
                        o = oT[:, bass.ds(i * 4 + (2 * s + e), 1), :].rearrange("p o t -> p (o t)")
                        nc.vector.scalar_tensor_tensor(o, o, gn[:, bass.ds(i * 4 + (2 * s + e), 1)], ro[:, :], ALU.mult, ALU.mult)
                    dve.drain()
                    o = oT[:, bass.ds(i * 4 + 2 * s, 2), :]
                    nc.vector.tensor_tensor(o, o, sg[:, s, :, :], ALU.mult).then_inc(gated, 1)


def stage_gates(nc, tag, n, hT, w, gt, gts, scratch, grow):
    C = 3 * NH
    with ExitStack() as es:
        sem = lambda name: new_sem(nc, es, f"{tag}_{name}")
        wt = es.enter_context(nc.sbuf_tensor(tag + "_w", [P, KD, C], F32))
        ps = es.enter_context(nc.psum_tensor(tag + "_ps", [P, TILES + 1, C], F32))
        loaded, summed, gated, bounced = sem("loaded"), sem("summed"), sem("gated"), sem("bounced")
        block = es.enter_context(stage_block(nc))

        @block.sync
        def _(sp):
            sp.dma_start(wt[:, :, :], w[:, C_NG:C_NG + C].rearrange("(k p) n -> p k n", p=P)).then_inc(loaded, 16)
            sp.wait_ge(gated, 1)
            sp.dma_start(scratch, gts[:, :]).then_inc(bounced, 16)
            sp.wait_ge(bounced, 16)
            sp.dma_start(grow[:, :], scratch.rearrange("b (h c) -> (b h) c", c=3)).then_inc(bounced, 16)
            sp.wait_ge(bounced, 32)

        @block.tensor
        def _(pe):
            pe.wait_ge(loaded, 16)
            for t in range(TILES + 1):
                rows = P if t < TILES else NS
                for k in range(KD):
                    last = nc.tensor.matmul(ps[0:rows, t, :], hT[:, k, t * P:t * P + rows], wt[:, k, :],
                                            start=(k == 0), stop=(k == KD - 1))
            last.then_inc(summed, 1)

        @block.scalar
        def _(act):
            act.wait_ge(summed, 1)
            nc.scalar.activation(gt[:, :, :], ps[:, 0:TILES, :], ACT.Sigmoid)
            nc.scalar.activation(gts[:, :], ps[0:NS, TILES, :], ACT.Sigmoid).then_inc(gated, 1)


def store_rows(sp, n, rows, srows, stored):
    names = ["cmp_k", "cmp_v", "sel_k", "sel_v", "win_k", "win_v"]
    for m, name in enumerate(names):
        for g in range(NG):
            t0 = TILES - WIN // P if m >= 4 else 0
            sp.dma_start(n.o["p_" + name][0, 0, :, g, :].rearrange("(t p) d -> p t d", p=P),
                         rows[:, 2 * m + g, t0:TILES, :]).then_inc(stored, 16)
        dst = n.o["s_" + name][0, :, WIN - 1 if m >= 4 else 0, :, :]
        sp.dma_start(dst, srows[:, 2 * m:2 * m + 2, :]).then_inc(stored, 16)
    for name in names[4:]:
        sp.dma_start(n.o["s_" + name][0, :, 0:WIN - 1, :, :].rearrange("b t g d -> b (t g d)"),
                     n.i["cache_" + name][0, :, 1:WIN, :, :].rearrange("b t g d -> b (t g d)")).then_inc(stored, 16)
    sp.wait_ge(stored, 16 * (3 * 6 + 2))


def stage_compress(nc, tag, n, Z, b0, pool, pos, w, ck):
    COLS = NG * NCMP * (1 + NS)
    LC = 4
    with ExitStack() as es:
        sb = lambda name, shape, dt=F32: es.enter_context(nc.sbuf_tensor(f"{tag}_{name}", shape, dt))
        sem = lambda name: new_sem(nc, es, f"{tag}_{name}")
        kc = sb("kc", [P, (COLS + 1) * CMP])
        page = sb("page", [P, PAGES, NG * P])
        wt = sb("w", [P, 2, LC, P])
        posn = sb("pos", [CMP, P])
        bias = sb("bias", [P, 1])
        ps_t = es.enter_context(nc.psum_tensor(tag + "_pst", [P, 2, 512], F32))
        ps_p = es.enter_context(nc.psum_tensor(tag + "_psp", [P, 512], F32))
        ps = es.enter_context(nc.psum_tensor(tag + "_ps", [P, 512], F32))
        pos_loaded, turned, saved, w_used, summed = (sem("pos_loaded"), sem("turned"), sem("saved"), sem("w_used"), sem("summed"))
        gathered = sem("gathered")
        loaded = [sem(f"loaded{i}") for i in range(PAGES)]
        w_loaded = [sem(f"w_loaded{i}") for i in range(2)]
        block = es.enter_context(stage_block(nc))

        def load_pages(queue, mine):
            def load(pg, b):
                number = queue.value_load(n.table[0:1, bass.ds(b * PAGES + pg, 1)], min_val=0, max_val=N_POOL - 1)
                queue.dma_start(page[:, pg, :], pool[bass.ds(number, 1), :, :, :].rearrange("o t g d -> t (o g d)")
                                ).then_inc(loaded[pg], 16)

            for pg in mine:
                load(pg, 0)
            with queue.Fori(0, NS - 1) as b:
                for pg in mine:
                    queue.wait_ge(turned, b * PAGES + (pg + 1))
                    load(pg, b + 1)

        @block.sync
        def _(sp):
            sp.dma_start(posn[:, :], pos).then_inc(pos_loaded, 16)
            load_pages(sp, range(0, PAGES, 2))

        @block.tensor
        def _(pe):
            pe.wait_ge(pos_loaded, 16)
            nc.tensor.transpose(ps_p[:, 0:CMP], posn[:, :], n.ident[0:CMP, 0:CMP])
            with pe.Fori(0, NS) as b:
                for pg in range(PAGES):
                    s = pg % 2
                    pe.wait_ge(loaded[pg], b * 16 + 16)
                    pe.wait_ge(saved, b * PAGES + (pg + 1))
                    for g in range(NG):
                        last = nc.tensor.transpose(ps_t[:, s, g * P:(g + 1) * P], page[:, pg, g * P:(g + 1) * P], n.ident)
                    last.then_inc(turned, 1)
            pe.wait_ge(gathered, 2)
            kv = kc[:, :].rearrange("p (c l) -> p c l", l=CMP)
            for l in range(CMP):
                i = l // LC
                if l % LC == 0:
                    pe.wait_ge(w_loaded[i % 2], 16 * (i // 2 + 1))
                last = nc.tensor.matmul(ps[:, 0:COLS + 1], wt[:, i % 2, l % LC, :], kv[:, :, l], start=(l == 0), stop=(l == CMP - 1))
                if l % LC == LC - 1:
                    last.then_inc(w_used, 1)

        @block.scalar
        def _(act):
            wv = w.rearrange("l d e -> d l e")

            def load_weights(i):
                act.dma_start(wt[:, i % 2, :, :], wv[:, i * LC:(i + 1) * LC, :]).then_inc(w_loaded[i % 2], 16)

            load_weights(0)
            load_weights(1)
            load_pages(act, range(1, PAGES, 2))
            nc.scalar.copy(kc[:, 0:NG * SEQ].rearrange("p (g t) -> p g t", g=NG), Z[:, b0:b0 + 2, 0:SEQ]).then_inc(gathered, 1)
            for i in range(2, CMP // LC):
                act.wait_ge(w_used, i - 1)
                load_weights(i)

        @block.vector
        def _(dve):
            dve.sem_inc(saved, 2)
            with dve.Fori(0, NS) as b:
                for pg in range(PAGES):
                    dve.wait_ge(turned, b * PAGES + (pg + 1))
                    nc.vector.tensor_copy(
                        kc[:, bass.ds(b * (NG * PAST) + NG * SEQ, NG * PAST)].rearrange("p (g t) -> p g t", g=NG)[:, :, pg * P:(pg + 1) * P],
                        ps_t[:, pg % 2, 0:NG * P].rearrange("p (g t) -> p g t", g=NG)).then_inc(saved, 1)
            nc.vector.tensor_copy(kc[:, COLS * CMP:(COLS + 1) * CMP], ps_p[:, 0:CMP]).then_inc(gathered, 1)
            dve.wait_ge(w_used, CMP // LC)
            nc.vector.tensor_copy(bias[:, :], ps[:, COLS:COLS + 1])
            dve.drain()
            nc.vector.tensor_scalar(ck[:, :], ps[:, 0:COLS], bias[:, :], None, ALU.add)


def stage_cv_rows(nc, tag, n, cv, cvp, cvs):
    with ExitStack() as es:
        ps = es.enter_context(nc.psum_tensor(tag + "_ps", [P, 512], F32))
        turned = new_sem(nc, es, tag + "_turned")
        block = es.enter_context(stage_block(nc))

        @block.tensor
        def _(pe):
            for g in range(NG):
                nc.tensor.transpose(ps[0:NCMP, g * P:(g + 1) * P], cv[:, g * NCMP:(g + 1) * NCMP], n.ident)
            for a in range(2):
                last = nc.tensor.transpose(ps[:, (2 + a) * P:(3 + a) * P], cv[:, 32 + a * P:32 + (a + 1) * P], n.ident)
            last.then_inc(turned, 1)

        @block.vector
        def _(dve):
            dve.wait_ge(turned, 1)
            nc.vector.tensor_copy(cvp[:, :, :], ps[0:NCMP, 0:256].rearrange("p (g d) -> p g d", g=2))
            nc.vector.tensor_copy(cvs[:, :, :], ps[:, 256:512].rearrange("p (g d) -> p g d", g=2))


def pick_blocks(nc, dve, score, v8, i8, if4, hit, sel, iota, nblk):
    nc.vector.max(v8, score)
    dve.drain()
    nc.vector.max_index(i8, v8, score)
    dve.drain()
    nc.vector.tensor_copy(if4, i8[:, 0:4])
    dve.drain()
    rows = score.shape[0]
    nc.vector.tensor_tensor(hit, iota.unsqueeze(2).to_broadcast([rows, nblk, 4]),
                            if4.unsqueeze(1).to_broadcast([rows, nblk, 4]), ALU.is_equal)
    dve.drain()
    nc.vector.tensor_reduce(sel, hit, AX.X, ALU.add)
    dve.drain()


def stage_nsa_group(nc, tag, n, g, Z, rows, srows, ck, cvp, gt, oT):
    B_KS, B_KW, R_VS, R_VW = 12 + g, 16 + g, 6 + g, 10 + g
    with ExitStack() as es:
        sb = lambda name, shape, dt=F32: es.enter_context(nc.sbuf_tensor(f"{tag}_{name}", shape, dt))
        pb = lambda name, shape: es.enter_context(nc.psum_tensor(f"{tag}_{name}", shape, F32))
        sem = lambda name: new_sem(nc, es, f"{tag}_{name}")
        con = sb("con", [P, 896 + 384 + 64 + 64 + 32 + 32 + 9])
        qs = sb("qs", [P, SEQ])
        pc = sb("pc", [P, HG, TILES, NCMP])
        half = sb("half", [P, TILES, NCMP // 2])
        cm, cr = sb("cm", [P, TILES]), sb("cr", [P, TILES])
        imp, pcs = sb("imp", [P, TILES, 8]), sb("pcs", [P, TILES * NCMP])
        v8, i8, if4, hit, sel = sb("v8", [P, 8]), sb("i8", [P, 8], U32), sb("if4", [P, 4]), sb("hit", [P, 8, 4]), sb("sel", [P, 8])
        bias = sb("bias", [P, TILES, 512])
        sc = sb("sc", [P, 2, 896])
        mx, rs = sb("mx", [P, 2, 2]), sb("rs", [P, 2, 3])
        pcg = sb("pcg", [P, 2, NCMP])
        pt = sb("pt", [P, 8, P])
        ps_s, ps_w = pb("pss", [P, 2, 512]), pb("psw", [P, 2, 512])
        ps_t, ps_o = pb("pst", [P, 2, 512]), pb("pso", [P, 2, 512])
        loaded, q_staged, c_scored, c_biased, c_exped, c_done, mask_done = (
            sem("loaded"), sem("q_staged"), sem("c_scored"), sem("c_biased"), sem("c_exped"), sem("c_done"), sem("mask_done"))
        scored, biased, exped, weighted, turned, pt_saved, summed = (
            sem("scored"), sem("biased"), sem("exped"), sem("weighted"), sem("turned"), sem("pt_saved"), sem("summed"))
        stored = sem("stored")
        block = es.enter_context(stage_block(nc))
        o = 0
        parts = {}
        for name, width in (("causal", 896), ("win", 384), ("cbias", 64), ("cmask", 64), ("vmask", 32), ("vadd", 32), ("iota", 9)):
            parts[name] = con[:, o:o + width]
            o += width

        def nsel(t):
            return (t + 1) * P

        def wtiles(t):
            return range(max(0, t - 2), t + 1)

        @block.sync
        def _(sp):
            sp.dma_start(con[:, :], n.c["nsa"]).then_inc(loaded, 16)
            if g == 0:
                store_rows(sp, n, rows, srows, stored)

        def stage_q(act, h):
            nc.scalar.activation(qs[:, :], Z[:, bass.ds(h + g * HG, 1), 0:SEQ].rearrange("p o t -> p (o t)"), ACT.Copy,
                                 scale=P ** -0.5).then_inc(q_staged, 1)

        @block.scalar
        def _(act):
            with act.Fori(0, HG) as h:
                stage_q(act, h)
                act.wait_ge(c_biased, h + 1)
                p = pc[:, bass.ds(h, 1), :, :].rearrange("p o t c -> p (o t c)")
                nc.scalar.activation(p, p, ACT.Exp).then_inc(c_exped, 1)
                act.wait_ge(c_done, h + 1)
            with act.Fori(0, HG) as h:
                stage_q(act, h)

                def softmax(t):
                    s = t % 2
                    act.wait_ge(biased, h * TILES + (t + 1))
                    nc.scalar.activation(sc[:, s, 0:nsel(t)], sc[:, s, 0:nsel(t)], ACT.Exp, bias=mx[:, s, 0:1],
                                         accum_out=rs[:, s, 0:1])
                    w = len(wtiles(t)) * P
                    nc.scalar.activation(sc[:, s, 512:512 + w], sc[:, s, 512:512 + w], ACT.Exp, bias=mx[:, s, 1:2],
                                         accum_out=rs[:, s, 1:2]).then_inc(exped, 1)

                def save_pt(t):
                    act.wait_ge(turned, h * TILES + (t + 1))
                    nc.scalar.copy(pt[:, 0:t + 1, :], ps_t[:, 0, 0:nsel(t)].rearrange("p (k q) -> p k q", q=P))
                    w = len(wtiles(t))
                    nc.scalar.copy(pt[:, 4:4 + w, :], ps_t[:, 1, 0:w * P].rearrange("p (k q) -> p k q", q=P))
                    nc.scalar.copy(pt[0:NCMP, 7, :], ps_t[0:NCMP, 1, 384:512]).then_inc(pt_saved, 1)

                softmax(0)
                for t in range(TILES):
                    save_pt(t)
                    if t + 1 < TILES:
                        softmax(t + 1)

        @block.tensor
        def _(pe):
            with pe.Fori(0, HG) as h:
                pe.wait_ge(q_staged, h + 1)
                for t in range(TILES):
                    last = nc.tensor.matmul(ps_o[:, 0, t * NCMP:(t + 1) * NCMP], qs[:, t * P:(t + 1) * P],
                                            ck[:, g * NCMP:(g + 1) * NCMP], start=True, stop=True)
                last.then_inc(c_scored, 1)
            pe.wait_ge(mask_done, 1)
            with pe.Fori(0, HG) as h:
                pe.wait_ge(q_staged, h + (HG + 1))

                def scores(t):
                    qt = qs[:, t * P:(t + 1) * P]
                    nc.tensor.matmul(ps_s[:, t % 2, 0:nsel(t)], qt, Z[:, B_KS, 0:nsel(t)], start=True, stop=True)
                    w0, w1 = wtiles(t)[0] * P, nsel(t)
                    nc.tensor.matmul(ps_w[:, t % 2, 0:w1 - w0], qt, Z[:, B_KW, w0:w1], start=True, stop=True).then_inc(scored, 1)

                scores(0)
                for t in range(TILES):
                    if t + 1 < TILES:
                        scores(t + 1)
                    pe.wait_ge(weighted, h * TILES + (t + 1))
                    s = t % 2
                    for k in range(t + 1):
                        nc.tensor.transpose(ps_t[:, 0, k * P:(k + 1) * P], sc[:, s, k * P:(k + 1) * P], n.ident)
                    for k in range(len(wtiles(t))):
                        nc.tensor.transpose(ps_t[:, 1, k * P:(k + 1) * P], sc[:, s, 512 + k * P:512 + (k + 1) * P], n.ident)
                    nc.tensor.transpose(ps_t[0:NCMP, 1, 384:512], pcg[:, s, :], n.ident).then_inc(turned, 1)
                    pe.wait_ge(pt_saved, h * TILES + (t + 1))
                    po = ps_o[:, s, 0:P]
                    nc.tensor.matmul(po, cvp[:, g, :], pt[0:NCMP, 7, :], start=True, stop=False)
                    for k in range(t + 1):
                        nc.tensor.matmul(po, rows[:, R_VS, k, :], pt[:, k, :], start=False, stop=False)
                    for j, k in enumerate(wtiles(t)):
                        last = nc.tensor.matmul(po, rows[:, R_VW, k, :], pt[:, 4 + j, :], start=False, stop=(k == t))
                    last.then_inc(summed, 1)

        @block.vector
        def _(dve):
            dve.wait_ge(loaded, 16)
            with dve.Fori(0, HG) as h:
                p = pc[:, bass.ds(h, 1), :, :].rearrange("p o t c -> p (o t) c")
                spread = lambda x: x.unsqueeze(2).to_broadcast([P, TILES, NCMP])
                table = lambda name: parts[name].rearrange("p (t c) -> p t c", c=NCMP)
                dve.wait_ge(c_scored, h + 1)
                nc.vector.tensor_tensor(p, ps_o[:, 0, 0:64].rearrange("p (t c) -> p t c", c=NCMP), table("cbias"), ALU.add)
                dve.drain()
                nc.vector.tensor_reduce(cm[:, :], p, AX.X, ALU.max)
                dve.drain()
                nc.vector.tensor_tensor(p, p, spread(cm[:, :]), ALU.subtract).then_inc(c_biased, 1)
                dve.wait_ge(c_exped, h + 1)
                nc.vector.tensor_tensor(half[:, :, 0:8], p[:, :, 0:8], p[:, :, 8:16], ALU.add)
                dve.drain()
                for w in (4, 2, 1):
                    nc.vector.tensor_tensor(half[:, :, 0:w], half[:, :, 0:w], half[:, :, w:2 * w], ALU.add)
                    dve.drain()
                nc.vector.reciprocal(cr[:, :], half[:, :, 0])
                dve.drain()
                nc.vector.tensor_tensor(p, p, spread(cr[:, :]), ALU.mult)
                dve.drain()
                nc.vector.tensor_tensor(p, p, table("cmask"), ALU.mult).then_inc(c_done, 1)
                dve.drain()
            nc.vector.tensor_reduce(pcs[:, :], pc[:, :, :, :].rearrange("p h t c -> p (t c) h"), AX.X, ALU.add)
            dve.drain()
            nc.vector.tensor_reduce(imp[:, :, :].rearrange("p t b -> p (t b)"),
                                    pcs[:, :].rearrange("p (b r) -> p b r", r=2), AX.X, ALU.add)
            dve.drain()
            nc.vector.tensor_tensor(imp[:, :, :].rearrange("p t b -> p (t b)"), imp[:, :, :].rearrange("p t b -> p (t b)"),
                                    parts["vmask"], ALU.mult)
            dve.drain()
            nc.vector.tensor_tensor(imp[:, :, :].rearrange("p t b -> p (t b)"), imp[:, :, :].rearrange("p t b -> p (t b)"),
                                    parts["vadd"], ALU.add)
            dve.drain()
            for t in range(TILES):
                pick_blocks(nc, dve, imp[:, t, :], v8[:, :], i8[:, :], if4[:, :], hit[:, :, :], sel[:, :], parts["iota"][:, 0:8], 8)
                nc.vector.tensor_scalar(sel[:, :], sel[:, :], -NEG, NEG, ALU.mult, ALU.add)
                dve.drain()
                nc.vector.tensor_tensor(bias[:, t, :].rearrange("p (b k) -> p b k", k=64),
                                        sel[:, :].unsqueeze(2).to_broadcast([P, 8, 64]),
                                        parts["causal"][:, 384 - t * P:896 - t * P].rearrange("p (b k) -> p b k", k=64), ALU.add)
                dve.drain()
            dve.sem_inc(mask_done, 1)
            with dve.Fori(0, HG) as h:
                def bias_scores(t):
                    s = t % 2
                    dve.wait_ge(scored, h * TILES + (t + 1))
                    w = len(wtiles(t)) * P
                    nc.vector.tensor_tensor(sc[:, s, 0:nsel(t)], ps_s[:, s, 0:nsel(t)], bias[:, t, 0:nsel(t)], ALU.add)
                    nc.vector.tensor_tensor(sc[:, s, 512:512 + w], ps_w[:, s, 0:w], parts["win"][:, 384 - w:384], ALU.add)
                    dve.drain()
                    nc.vector.tensor_reduce(mx[:, s, 0:1], sc[:, s, 0:nsel(t)], AX.X, ALU.max, negate=True)
                    nc.vector.tensor_reduce(mx[:, s, 1:2], sc[:, s, 512:512 + w], AX.X, ALU.max, negate=True).then_inc(biased, 1)

                def weigh(t):
                    s = t % 2
                    w = len(wtiles(t)) * P
                    gate = lambda br: gt[:, t, bass.ds(h * 3 + (3 * HG * g + br), 1)]
                    nc.vector.tensor_scalar(pcg[:, s, :], pc[:, bass.ds(h, 1), t, :].rearrange("p o c -> p (o c)"), gate(0), None, ALU.mult)
                    dve.wait_ge(exped, h * TILES + (t + 1))
                    nc.vector.reciprocal(rs[:, s, 0:2], rs[:, s, 0:2])
                    dve.drain()
                    nc.vector.tensor_tensor(rs[:, s, 0:2], rs[:, s, 0:2], gt[:, t, bass.ds(h * 3 + (3 * HG * g + 1), 2)], ALU.mult)
                    dve.drain()
                    nc.vector.tensor_scalar(sc[:, s, 0:nsel(t)], sc[:, s, 0:nsel(t)], rs[:, s, 0:1], None, ALU.mult)
                    nc.vector.tensor_scalar(sc[:, s, 512:512 + w], sc[:, s, 512:512 + w], rs[:, s, 1:2], None, ALU.mult).then_inc(weighted, 1)

                def save_out(t):
                    dve.wait_ge(summed, h * TILES + (t + 1))
                    nc.vector.tensor_copy(oT[:, bass.ds(h + (8 + g * HG), 1), t * P:(t + 1) * P].rearrange("p o t -> p (o t)"),
                                          ps_o[:, t % 2, 0:P])

                bias_scores(0)
                for t in range(TILES):
                    weigh(t)
                    if t + 1 < TILES:
                        bias_scores(t + 1)
                    if t > 0:
                        save_out(t - 1)
                save_out(TILES - 1)
                dve.drain()


def stage_cached_scores(nc, tag, n, q, units, dblocks, npg, loads, load, st):
    rows = q.shape[2]
    per = rows // NS // units
    nt = units * dblocks
    SLOTS = 4
    with ExitStack() as es:
        sb = lambda name, shape: es.enter_context(nc.sbuf_tensor(f"{tag}_{name}", shape, F32))
        sem = lambda name: new_sem(nc, es, f"{tag}_{name}")
        keys = sb("keys", [P, SLOTS, npg, nt * P])
        kt = sb("kt", [P, nt, npg * P])
        width = nt // 2 * npg * P
        ps_t = es.enter_context(nc.psum_tensor(tag + "_pst", [P, 2, max(512, width)], F32))
        ps_s = es.enter_context(nc.psum_tensor(tag + "_pss", [P, npg, rows], F32))
        turned, copied, scored = sem("turned"), sem("copied"), sem("scored")
        loaded = [sem(f"loaded{i}") for i in range(SLOTS)]
        block = es.enter_context(stage_block(nc))

        @block.sync
        def _(sp):
            for s in range(SLOTS):
                load(sp, keys[:, s, :, :], s, loaded[s])
            with sp.Fori(0, NS // SLOTS - 1) as i:
                for s in range(SLOTS):
                    sp.wait_ge(turned, i * (2 * SLOTS) + (2 * s + 2))
                    load(sp, keys[:, s, :, :], i * SLOTS + (s + SLOTS), loaded[s])

        @block.tensor
        def _(pe):
            with pe.Fori(0, NS // SLOTS) as i:
                for s in range(SLOTS):
                    pe.wait_ge(loaded[s], i * (16 * loads) + 16 * loads)
                    for part in range(2):
                        for u in range(part * nt // 2, (part + 1) * nt // 2):
                            for pg in range(npg):
                                at = (u % (nt // 2) * npg + pg) * P
                                last = nc.tensor.transpose(ps_t[:, part, at:at + P], keys[:, s, pg, u * P:(u + 1) * P], n.ident)
                        last.then_inc(turned, 1)
                    for part in range(2):
                        pe.wait_ge(copied, i * (2 * SLOTS) + (2 * s + part + 1))
                        for u in range(part * units // 2, (part + 1) * units // 2):
                            col = i * (SLOTS * units * per) + (s * units + u) * per
                            for pg in range(npg):
                                for d in range(dblocks):
                                    last = nc.tensor.matmul(ps_s[:, pg, bass.ds(col, per)],
                                                            kt[:, u * dblocks + d, pg * P:(pg + 1) * P],
                                                            q[:, d, bass.ds(col, per)], start=(d == 0), stop=(d == dblocks - 1))
                    last.then_inc(scored, 1)

        @block.scalar
        def _(act):
            with act.Fori(0, NS) as b:
                for part in range(2):
                    act.wait_ge(turned, b * 2 + (part + 1))
                    heads = slice(part * nt // 2, (part + 1) * nt // 2)
                    nc.scalar.copy(kt[:, heads, :], ps_t[:, part, 0:width].rearrange("p (u k) -> p u k", k=npg * P)
                                   ).then_inc(copied, 1)

        @block.vector
        def _(dve):
            dve.wait_ge(scored, NS)
            nc.vector.tensor_copy(st[:, :, :], ps_s[:, :, :])


def stage_row_softmax(nc, tag, n, rows, st, npg, pt, direct=None, bias=None, block_bias=None, new_score=None,
                      gate=None, keep=None, new_weight=None):
    keys = npg * P
    total = keys + (1 if new_score is not None else 0)
    with ExitStack() as es:
        sb = lambda name, shape: es.enter_context(nc.sbuf_tensor(f"{tag}_{name}", shape, F32))
        sem = lambda name: new_sem(nc, es, f"{tag}_{name}")
        s_ = sb("s", [rows, total])
        sm = sb("sm", [rows, 3])
        ps = es.enter_context(nc.psum_tensor(tag + "_ps", [P, 512], F32))
        ps_t = es.enter_context(nc.psum_tensor(tag + "_pst", [P, npg, rows], F32))
        scored, biased, exped, weighted, turned = sem("scored"), sem("biased"), sem("exped"), sem("weighted"), sem("turned")
        block = es.enter_context(stage_block(nc))

        @block.tensor
        def _(pe):
            if direct is not None:
                last = nc.tensor.matmul(ps[0:rows, 0:keys], direct[0], direct[1], start=True, stop=True)
            else:
                for pg in range(npg):
                    last = nc.tensor.transpose(ps[0:rows, pg * P:(pg + 1) * P], st[:, pg, :], n.ident)
            last.then_inc(scored, 1)
            pe.wait_ge(weighted, 1)
            for pg in range(npg):
                last = nc.tensor.transpose(ps_t[:, pg, :], s_[:, pg * P:(pg + 1) * P], n.ident[0:rows, 0:rows])
            last.then_inc(turned, 1)

        @block.scalar
        def _(act):
            act.wait_ge(biased, 1)
            nc.scalar.activation(s_[:, :], s_[:, :], ACT.Exp, bias=sm[:, 0:1], accum_out=sm[:, 1:2]).then_inc(exped, 1)
            act.wait_ge(turned, 1)
            nc.scalar.copy(pt[:, :, :], ps_t[:, :, :])

        @block.vector
        def _(dve):
            dve.wait_ge(scored, 1)
            if bias is not None:
                nc.vector.tensor_tensor(s_[:, 0:keys], ps[0:rows, 0:keys], bias, ALU.add)
            elif block_bias is not None:
                nb = keys // 64
                nc.vector.tensor_tensor(s_[:, 0:keys].rearrange("p (b k) -> p b k", k=64),
                                        ps[0:rows, 0:keys].rearrange("p (b k) -> p b k", k=64),
                                        block_bias[:, 0:nb].unsqueeze(2).to_broadcast([rows, nb, 64]), ALU.add)
            else:
                nc.vector.tensor_copy(s_[:, 0:keys], ps[0:rows, 0:keys])
            if new_score is not None:
                if block_bias is not None:
                    nc.vector.tensor_tensor(s_[:, keys:total], new_score, block_bias[:, keys // 64:keys // 64 + 1], ALU.add)
                else:
                    nc.vector.tensor_copy(s_[:, keys:total], new_score)
            dve.drain()
            nc.vector.tensor_reduce(sm[:, 0:1], s_[:, :], AX.X, ALU.max, negate=True).then_inc(biased, 1)
            dve.wait_ge(exped, 1)
            nc.vector.reciprocal(sm[:, 2:3], sm[:, 1:2])
            dve.drain()
            if keep is not None:
                nc.vector.tensor_scalar(keep, s_[:, 0:keys], sm[:, 2:3], None, ALU.mult)
            if gate is not None:
                nc.vector.tensor_scalar(s_[:, :], s_[:, :], sm[:, 2:3], gate, ALU.mult, ALU.mult).then_inc(weighted, 1)
            else:
                nc.vector.tensor_scalar(s_[:, :], s_[:, :], sm[:, 2:3], None, ALU.mult).then_inc(weighted, 1)
            if new_weight is not None:
                dve.drain()
                nc.vector.tensor_copy(new_weight, s_[:, keys:total])


def stage_cached_values(nc, tag, n, pt, units, dblocks, npg, loads, load, acc, add):
    rows = pt.shape[2]
    per = rows // NS // units
    nt = units * dblocks
    SLOTS = 4
    with ExitStack() as es:
        sem = lambda name: new_sem(nc, es, f"{tag}_{name}")
        vals = es.enter_context(nc.sbuf_tensor(tag + "_vals", [P, SLOTS, npg, nt * P], F32))
        ps = es.enter_context(nc.psum_tensor(tag + "_ps", [P, dblocks, rows], F32))
        summed = sem("summed")
        loaded = [sem(f"loaded{i}") for i in range(SLOTS)]
        block = es.enter_context(stage_block(nc))

        @block.sync
        def _(sp):
            for s in range(SLOTS):
                load(sp, vals[:, s, :, :], s, loaded[s])
            with sp.Fori(0, NS // SLOTS - 1) as i:
                for s in range(SLOTS):
                    sp.wait_ge(summed, i * SLOTS + (s + 1))
                    load(sp, vals[:, s, :, :], i * SLOTS + (s + SLOTS), loaded[s])

        @block.tensor
        def _(pe):
            with pe.Fori(0, NS // SLOTS) as i:
                for s in range(SLOTS):
                    pe.wait_ge(loaded[s], i * (16 * loads) + 16 * loads)
                    for u in range(units):
                        col = i * (SLOTS * units * per) + (s * units + u) * per
                        for d in range(dblocks):
                            c = (u * dblocks + d) * P
                            for pg in range(npg):
                                last = nc.tensor.matmul(ps[:, d, bass.ds(col, per)], vals[:, s, pg, c:c + P],
                                                        pt[:, pg, bass.ds(col, per)], start=(pg == 0), stop=(pg == npg - 1))
                    last.then_inc(summed, 1)

        @block.vector
        def _(dve):
            dve.wait_ge(summed, NS)
            if add:
                nc.vector.tensor_tensor(acc, acc, ps[:, :, :], ALU.add)
            else:
                nc.vector.tensor_copy(acc, ps[:, :, :])


def stage_new_scores(nc, tag, n, q, Z, con_mine, out):
    with ExitStack() as es:
        sem = lambda name: new_sem(nc, es, f"{tag}_{name}")
        nk = es.enter_context(nc.sbuf_tensor(tag + "_nk", [P, 2, NG, NS], F32))
        tmp = es.enter_context(nc.sbuf_tensor(tag + "_tmp", [ROWS, 2, NG * NS], F32))
        ps = es.enter_context(nc.psum_tensor(tag + "_ps", [P, 2, NG * NS], F32))
        copied, scored = sem("copied"), sem("scored")
        block = es.enter_context(stage_block(nc))

        @block.scalar
        def _(act):
            nc.scalar.copy(nk[:, 0, :, :], Z[:, 12:14, SEQ:T])
            nc.scalar.copy(nk[:, 1, :, :], Z[:, 16:18, SEQ:T]).then_inc(copied, 1)

        @block.tensor
        def _(pe):
            pe.wait_ge(copied, 1)
            for j in range(2):
                last = nc.tensor.matmul(ps[0:ROWS, j, :], q[:, 0, :], nk[:, j, :, :].rearrange("p g b -> p (g b)"),
                                        start=True, stop=True)
            last.then_inc(scored, 1)

        @block.vector
        def _(dve):
            dve.wait_ge(scored, 1)
            nc.vector.tensor_tensor(tmp[:, :, :], ps[0:ROWS, :, :], con_mine.unsqueeze(1).to_broadcast([ROWS, 2, NG * NS]), ALU.mult)
            dve.drain()
            nc.vector.tensor_reduce(out, tmp[:, :, :], AX.X, ALU.add)


def stage_pick_sample(nc, tag, n, pk, con, bsel):
    same, vm, va, iota = con[:, 256:320], con[:, 336:345], con[:, 345:354], con[:, 354:363]
    with ExitStack() as es:
        sb = lambda name, shape, dt=F32: es.enter_context(nc.sbuf_tensor(f"{tag}_{name}", shape, dt))
        sem = lambda name: new_sem(nc, es, f"{tag}_{name}")
        own, pb_, score = sb("own", [ROWS, NCMP]), sb("pb", [ROWS, 8]), sb("score", [ROWS, 9])
        v8, i8, if4, hit = sb("v8", [ROWS, 8]), sb("i8", [ROWS, 8], U32), sb("if4", [ROWS, 4]), sb("hit", [ROWS, 9, 4])
        ps = es.enter_context(nc.psum_tensor(tag + "_ps", [P, NCMP], F32))
        reduced, summed = sem("reduced"), sem("summed")
        block = es.enter_context(stage_block(nc))

        @block.tensor
        def _(pe):
            pe.wait_ge(reduced, 1)
            nc.tensor.matmul(ps[0:ROWS, :], same, own[:, :], start=True, stop=True).then_inc(summed, 1)

        @block.vector
        def _(dve):
            nc.vector.tensor_reduce(own[:, :], pk.rearrange("p (u c) -> p c u", c=NCMP), AX.X, ALU.add).then_inc(reduced, 1)
            dve.wait_ge(summed, 1)
            nc.vector.tensor_reduce(pb_[:, :], ps[0:ROWS, :].rearrange("p (b r) -> p b r", r=2), AX.X, ALU.add)
            dve.drain()
            nc.vector.tensor_tensor(score[:, 0:8], pb_[:, :], vm[:, 0:8], ALU.mult)
            nc.vector.tensor_copy(score[:, 8:9], va[:, 8:9])
            dve.drain()
            nc.vector.tensor_tensor(score[:, 0:8], score[:, 0:8], va[:, 0:8], ALU.add)
            dve.drain()
            pick_blocks(nc, dve, score[:, :], v8[:, :], i8[:, :], if4[:, :], hit[:, :, :], bsel, iota, 9)
            nc.vector.tensor_scalar(bsel, bsel, -NEG, NEG, ALU.mult, ALU.add)


def stage_sample_sum(nc, tag, n, ptc, cvs, srows, mine, new_w, acc, oT):
    with ExitStack() as es:
        sem = lambda name: new_sem(nc, es, f"{tag}_{name}")
        m = es.enter_context(nc.sbuf_tensor(tag + "_m", [ROWS, 2, NG * NS], F32))
        mt = es.enter_context(nc.sbuf_tensor(tag + "_mt", [NS, 2 * NG, ROWS], F32))
        ps_t = es.enter_context(nc.psum_tensor(tag + "_pst", [P, 2 * NG, ROWS], F32))
        ps = es.enter_context(nc.psum_tensor(tag + "_ps", [P, ROWS], F32))
        spread, turned, copied, summed = sem("spread"), sem("turned"), sem("copied"), sem("summed")
        block = es.enter_context(stage_block(nc))

        @block.vector
        def _(dve):
            for j in range(2):
                last = nc.vector.tensor_scalar(m[:, j, :], mine, new_w[:, j:j + 1], None, ALU.mult)
            last.then_inc(spread, 1)
            dve.wait_ge(turned, 1)
            nc.vector.tensor_copy(mt[:, :, :], ps_t[0:NS, :, :]).then_inc(copied, 1)
            dve.wait_ge(summed, 1)
            nc.vector.tensor_tensor(acc, acc, ps[:, :].unsqueeze(1), ALU.add)
            dve.drain()
            nc.vector.tensor_copy(oT[:, 8:16, SEQ:T].rearrange("p h b -> p b h"),
                                  acc.rearrange("p o (b h) -> p (o b) h", h=NH))

        @block.tensor
        def _(pe):
            pe.wait_ge(spread, 1)
            for j in range(2):
                for g in range(NG):
                    last = nc.tensor.transpose(ps_t[0:NS, 2 * j + g, :], m[:, j, g * NS:(g + 1) * NS], n.ident[0:ROWS, 0:ROWS])
            last.then_inc(turned, 1)
            pe.wait_ge(copied, 1)
            for a in range(2):
                nc.tensor.matmul(ps[:, :], cvs[:, a, :], ptc[:, a, :], start=(a == 0), stop=False)
            for j in range(2):
                for g in range(NG):
                    last = nc.tensor.matmul(ps[:, :], srows[:, (6 if j == 0 else 10) + g, :], mt[:, 2 * j + g, :],
                                            start=False, stop=(j == 1 and g == 1))
            last.then_inc(summed, 1)


def stage_sample_queries(nc, tag, n, Z, q, heads, dblocks, scale, con=None):
    with ExitStack() as es:
        loaded = new_sem(nc, es, tag + "_loaded")
        block = es.enter_context(stage_block(nc))

        @block.sync
        def _(sp):
            if con is not None:
                sp.dma_start(con[:, :], n.c["smp"]).then_inc(loaded, 16)
                sp.wait_ge(loaded, 16)

        @block.vector
        def _(dve):
            for d in range(dblocks):
                nc.vector.tensor_scalar(q[:, d, :].rearrange("p (b h) -> p h b", h=heads),
                                        Z[:, d:heads * dblocks:dblocks, SEQ:T], scale, None, ALU.mult)


def sample_nsa(nc, n, Z, ck, cvs, srows, grow, oT):

    def paged(pool):
        def load(sp, dst, b, done):
            for pg in range(PAGES):
                at = b * PAGES + pg
                number = sp.value_load(n.table[0:1, bass.ds(at, 1)], min_val=0, max_val=N_POOL - 1)
                sp.dma_start(dst[:, pg, :], pool[bass.ds(number, 1), :, :, :].rearrange("o t g d -> t (o g d)")).then_inc(done, 16)
        return load

    def window(cache):
        def load(sp, dst, b, done):
            sp.dma_start(dst, cache[bass.ds(b, 1), :, :, :].rearrange("o (t p) g d -> p (o t) (g d)", p=P)).then_inc(done, 16)
        return load

    with ExitStack() as es:
        sb = lambda name, shape: es.enter_context(nc.sbuf_tensor("sn_" + name, shape, F32))
        q = sb("q", [P, 1, ROWS])
        con = sb("con", [ROWS, 363])
        acc = sb("acc", [P, 1, ROWS])
        new_s, new_w, bsel = sb("new_s", [ROWS, 2]), sb("new_w", [ROWS, 2]), sb("bsel", [ROWS, 9])
        ptc, pk = sb("ptc", [P, 2, ROWS]), sb("pk", [ROWS, 256])
        st, pt = sb("st", [P, PAGES, ROWS]), sb("pt", [P, PAGES, ROWS])
        mine = con[:, 320:336]
        stage_sample_queries(nc, "sq", n, Z, q, NH, 1, P ** -0.5, con)
        stage_new_scores(nc, "sn", n, q, Z, mine, new_s[:, :])
        stage_row_softmax(nc, "sc", n, ROWS, None, 2, ptc, direct=(q[:, 0, :], ck[:, 32:288]), bias=con[:, 0:256],
                          gate=grow[:, 0:1], keep=pk[:, :])
        stage_pick_sample(nc, "sk", n, pk[:, :], con, bsel[:, :])
        stage_cached_scores(nc, "ss", n, q, NG, 1, PAGES, PAGES, paged(n.i["cache_sel_k"][0]), st)
        stage_row_softmax(nc, "sf", n, ROWS, st, PAGES, pt, block_bias=bsel, new_score=new_s[:, 0:1],
                          gate=grow[:, 1:2], new_weight=new_w[:, 0:1])
        stage_cached_values(nc, "sv", n, pt, NG, 1, PAGES, PAGES, paged(n.i["cache_sel_v"][0]), acc[:, :, :], False)
        stage_cached_scores(nc, "ws", n, q, NG, 1, 2, 1, window(n.i["cache_win_k"][0]), st[:, 0:2, :])
        stage_row_softmax(nc, "wf", n, ROWS, st, 2, pt[:, 0:2, :], new_score=new_s[:, 1:2], gate=grow[:, 2:3],
                          new_weight=new_w[:, 1:2])
        stage_cached_values(nc, "wv", n, pt[:, 0:2, :], NG, 1, 2, 1, window(n.i["cache_win_v"][0]), acc[:, :, :], True)
        stage_sample_sum(nc, "sx", n, ptc, cvs, srows, mine, new_w, acc[:, :, :], oT)


def stage_memory_rows(nc, tag, n, M, b0, rows, out):
    with ExitStack() as es:
        sem = lambda name: new_sem(nc, es, f"{tag}_{name}")
        ps = es.enter_context(nc.psum_tensor(tag + "_ps", [P, 2, MH * MD], F32))
        turned, copied, stored = sem("turned"), sem("copied"), sem("stored")
        block = es.enter_context(stage_block(nc))

        @block.tensor
        def _(pe):
            for t in range(2):
                for k in range(8):
                    last = nc.tensor.transpose(ps[:, t, k * P:(k + 1) * P], M[:, b0 + k, t * P:(t + 1) * P], n.ident)
            last.then_inc(turned, 1)

        @block.vector
        def _(dve):
            dve.wait_ge(turned, 1)
            nc.vector.tensor_copy(rows[:, :, :], ps[:, :, :]).then_inc(copied, 1)

        @block.sync
        def _(sp):
            sp.wait_ge(copied, 1)
            sp.dma_start(out.rearrange("(t p) h d -> p t (h d)", p=P), rows[:, :, :]).then_inc(stored, 16)
            sp.wait_ge(stored, 16)


def stage_memory_attend(nc, tag, n, Z, M, vrows, oT):
    with ExitStack() as es:
        sb = lambda name, shape: es.enter_context(nc.sbuf_tensor(f"{tag}_{name}", shape, F32))
        pb = lambda name, shape: es.enter_context(nc.psum_tensor(f"{tag}_{name}", shape, F32))
        sem = lambda name: new_sem(nc, es, f"{tag}_{name}")
        qs = sb("qs", [P, 2, SEQ])
        pr = sb("pr", [P, 2, NM])
        sm = sb("sm", [P, 2, 3])
        pt = sb("pt", [P, 2, P])
        vh = sb("vh", [P, 2, MD])
        ps_s, ps_t, ps_o = pb("pss", [P, 2, 512]), pb("pst", [P, 512]), pb("pso", [P, 2, 512])
        staged, scored, maxed, exped, weighted, turned, pt_saved, summed = (
            sem("staged"), sem("scored"), sem("maxed"), sem("exped"), sem("weighted"), sem("turned"), sem("pt_saved"), sem("summed"))
        block = es.enter_context(stage_block(nc))

        @block.scalar
        def _(act):
            with act.Fori(0, MH) as h:
                nc.scalar.copy(vh[:, :, :], vrows[:, :, bass.ds(h * MD, MD)])
                nc.scalar.activation(qs[:, :, :], Z[:, bass.ds(h * 2, 2), 0:SEQ], ACT.Copy, scale=MD ** -0.5).then_inc(staged, 1)

                def softmax(t):
                    act.wait_ge(maxed, h * TILES + (t + 1))
                    nc.scalar.activation(pr[:, t % 2, :], ps_s[:, t % 2, 0:NM], ACT.Exp, bias=sm[:, t % 2, 0:1],
                                         accum_out=sm[:, t % 2, 1:2]).then_inc(exped, 1)

                softmax(0)
                for t in range(TILES):
                    act.wait_ge(turned, h * TILES + (t + 1))
                    nc.scalar.copy(pt[:, :, :], ps_t[:, 0:NM].rearrange("p (k q) -> p k q", q=P)).then_inc(pt_saved, 1)
                    if t + 1 < TILES:
                        softmax(t + 1)
                act.wait_ge(summed, h * TILES + TILES)

        @block.tensor
        def _(pe):
            with pe.Fori(0, MH) as h:
                pe.wait_ge(staged, h + 1)

                def scores(t):
                    for d in range(2):
                        last = nc.tensor.matmul(ps_s[:, t % 2, 0:NM], qs[:, d, t * P:(t + 1) * P],
                                                M[:, bass.ds(h * 2 + d, 1), :].rearrange("p o m -> p (o m)"),
                                                start=(d == 0), stop=(d == 1))
                    last.then_inc(scored, 1)

                scores(0)
                for t in range(TILES):
                    if t + 1 < TILES:
                        scores(t + 1)
                    pe.wait_ge(weighted, h * TILES + (t + 1))
                    for k in range(2):
                        last = nc.tensor.transpose(ps_t[:, k * P:(k + 1) * P], pr[:, t % 2, k * P:(k + 1) * P], n.ident)
                    last.then_inc(turned, 1)
                    pe.wait_ge(pt_saved, h * TILES + (t + 1))
                    for e in range(2):
                        for k in range(2):
                            last = nc.tensor.matmul(ps_o[:, t % 2, e * P:(e + 1) * P], vh[:, k, e * P:(e + 1) * P],
                                                    pt[:, k, :], start=(k == 0), stop=(k == 1))
                    last.then_inc(summed, 1)

        @block.vector
        def _(dve):
            with dve.Fori(0, MH) as h:
                def top(t):
                    dve.wait_ge(scored, h * TILES + (t + 1))
                    nc.vector.tensor_reduce(sm[:, t % 2, 0:1], ps_s[:, t % 2, 0:NM], AX.X, ALU.max, negate=True).then_inc(maxed, 1)

                def save_out(t):
                    dve.wait_ge(summed, h * TILES + (t + 1))
                    nc.vector.tensor_copy(oT[:, bass.ds(h * 2 + 16, 2), t * P:(t + 1) * P],
                                          ps_o[:, t % 2, 0:2 * P].rearrange("p (e q) -> p e q", e=2))

                top(0)
                for t in range(TILES):
                    dve.wait_ge(exped, h * TILES + (t + 1))
                    nc.vector.reciprocal(sm[:, t % 2, 2:3], sm[:, t % 2, 1:2])
                    dve.drain()
                    nc.vector.tensor_scalar(pr[:, t % 2, :], pr[:, t % 2, :], sm[:, t % 2, 2:3], None, ALU.mult).then_inc(weighted, 1)
                    if t + 1 < TILES:
                        top(t + 1)
                    if t > 0:
                        save_out(t - 1)
                save_out(TILES - 1)
                dve.drain()


def stage_copy_rows(nc, tag, dst, src):
    with nc.Block() as block:
        @block.vector
        def _(dve):
            nc.vector.tensor_copy(dst, src)


def sample_memory(nc, n, Z, oT):
    rows = NS * MH

    def cached(cache):
        def load(sp, dst, b, done):
            sp.dma_start(dst, cache[bass.ds(b, 1), :, :, :].rearrange("o (t p) h d -> p (o t) (h d)", p=P)).then_inc(done, 16)
        return load

    with ExitStack() as es:
        sb = lambda name, shape: es.enter_context(nc.sbuf_tensor("sm_" + name, shape, F32))
        q, st, pt, acc = sb("q", [P, 2, rows]), sb("st", [P, 2, rows]), sb("pt", [P, 2, rows]), sb("acc", [P, 2, rows])
        stage_sample_queries(nc, "mq", n, Z, q, MH, 2, MD ** -0.5)
        stage_cached_scores(nc, "ms", n, q, MH, 2, 2, 1, cached(n.i["cache_mem_k"][0]), st)
        stage_row_softmax(nc, "mf", n, rows, st, 2, pt)
        stage_cached_values(nc, "mv", n, pt, MH, 2, 2, 1, cached(n.i["cache_mem_v"][0]), acc[:, :, :], False)
        for d in range(2):
            stage_copy_rows(nc, f"mc{d}", oT[:, 16 + d:24:2, SEQ:T].rearrange("p h b -> p b h"),
                            acc[:, d, :].rearrange("p (b h) -> p b h", h=MH))


def stage_merge(nc, tag, n, hT, oT, w_in, w_branch, mT):
    U = 6
    with ExitStack() as es:
        sb = lambda name, shape: es.enter_context(nc.sbuf_tensor(f"{tag}_{name}", shape, F32))
        sem = lambda name: new_sem(nc, es, f"{tag}_{name}")
        wt = sb("w", [P, 2, 24, P])
        sg, up = sb("sg", [P, 2, T]), sb("up", [P, T])
        ps_g = es.enter_context(nc.psum_tensor(tag + "_psg", [P, 2, 2, 512], F32))
        ps_u = es.enter_context(nc.psum_tensor(tag + "_psu", [P, 2, 2, 512], F32))
        loaded = [sem(f"loaded{i}") for i in range(2)]
        summed, gated, merged = sem("summed"), sem("gated"), sem("merged")
        block = es.enter_context(stage_block(nc))

        @block.sync
        def _(sp):
            def load(slot, j, c):
                col = j * P
                sp.dma_start(wt[:, slot, 0:16, :], w_in[:, bass.ds(col + (C_MG + c * D), P)].rearrange("(k p) n -> p k n", p=P)
                             ).then_inc(loaded[slot], 16)
                sp.dma_start(wt[:, slot, 16:24, :], w_branch[c][:, bass.ds(col, P)].rearrange("(k p) n -> p k n", p=P)
                             ).then_inc(loaded[slot], 16)

            load(0, 0, 0)
            load(1, 0, 1)
            with sp.Fori(0, KD // 2 - 1) as i:
                for u in range(U):
                    sp.wait_ge(summed, i * U + (u + 1))
                    load(u % 2, i * 2 + (u + 2) // 3, (u + 2) % 3)
            for u in range(U - 2):
                sp.wait_ge(summed, (KD // 2 - 1) * U + u + 1)
                load(u % 2, KD - 2 + (u + 2) // 3, (u + 2) % 3)

        @block.tensor
        def _(pe):
            with pe.Fori(0, KD // 2) as i:
                for u in range(U):
                    s, c = u % 2, u % 3
                    pe.wait_ge(loaded[s], i * 96 + (u // 2 + 1) * 32)
                    pe.wait_ge(merged, i * U + (u + 1))
                    for k in range(16):
                        for h in range(2):
                            nc.tensor.matmul(ps_g[:, s, h, 0:HALF], wt[:, s, k, :], hT[:, k, h * HALF:(h + 1) * HALF],
                                             start=(k == 0), stop=(k == 15))
                    for k in range(8):
                        for h in range(2):
                            last = nc.tensor.matmul(ps_u[:, s, h, 0:HALF], wt[:, s, 16 + k, :],
                                                    oT[:, c * 8 + k, h * HALF:(h + 1) * HALF],
                                                    start=(k == 0), stop=(k == 7))
                    last.then_inc(summed, 1)

        @block.scalar
        def _(act):
            with act.Fori(0, KD // 2) as i:
                for u in range(U):
                    act.wait_ge(summed, i * U + (u + 1))
                    act.wait_ge(merged, i * U + (u + 1))
                    nc.scalar.activation(halves(sg[:, u % 2, :]), ps_g[:, u % 2, :, 0:HALF], ACT.Sigmoid).then_inc(gated, 1)

        @block.vector
        def _(dve):
            dve.sem_inc(merged, 2)
            with dve.Fori(0, KD // 2) as i:
                for u in range(U):
                    m = mT[:, bass.ds(i * 2 + u // 3, 1), :].rearrange("p o t -> p (o t)")
                    dve.wait_ge(gated, i * U + (u + 1))
                    dst = m if u % 3 == 0 else up[:, :]
                    last = nc.vector.tensor_tensor(halves(dst), halves(sg[:, u % 2, :]), ps_u[:, u % 2, :, 0:HALF], ALU.mult)
                    if u % 3:
                        dve.drain()
                        last = nc.vector.tensor_tensor(m, m, up[:, :], ALU.add)
                    last.then_inc(merged, 1)
                    dve.drain()


def stage_residual(nc, tag, n, aT, tiles, x1, dram):
    with ExitStack() as es:
        sem = lambda name: new_sem(nc, es, f"{tag}_{name}")
        ps = es.enter_context(nc.psum_tensor(tag + "_ps", [P, 2, D], F32))
        loaded, turned, added, stored = sem("loaded"), sem("turned"), sem("added"), sem("stored")
        block = es.enter_context(stage_block(nc))

        @block.sync
        def _(sp):
            for t, (src, rows, _c) in enumerate(tiles):
                sp.dma_start(x1[0:rows, t, :], src).then_inc(loaded, 16)
            for t, (_s, rows, col) in enumerate(tiles):
                sp.wait_ge(added, t + 1)
                sp.dma_start(dram[col:col + rows, :], x1[0:rows, t, :]).then_inc(stored, 16)
            sp.wait_ge(stored, 16 * len(tiles))

        @block.tensor
        def _(pe):
            for t, (_s, rows, col) in enumerate(tiles):
                if t >= 2:
                    pe.wait_ge(added, t - 1)
                for k in range(KD):
                    last = nc.tensor.transpose(ps[0:rows, t % 2, k * P:(k + 1) * P], aT[:, k, col:col + rows], n.ident)
                last.then_inc(turned, 1)

        @block.vector
        def _(dve):
            dve.wait_ge(loaded, 16 * len(tiles))
            for t, (_s, rows, _c) in enumerate(tiles):
                dve.wait_ge(turned, t + 1)
                nc.vector.tensor_tensor(x1[0:rows, t, :], x1[0:rows, t, :], ps[0:rows, t % 2, :], ALU.add).then_inc(added, 1)


def stage_subkeys(nc, tag, n, subkeys, sk):
    with ExitStack() as es:
        sem = lambda name: new_sem(nc, es, f"{tag}_{name}")
        nat = es.enter_context(nc.sbuf_tensor(tag + "_nat", [PK, PH, 2, 64], F32))
        ps = es.enter_context(nc.psum_tensor(tag + "_ps", [P, PH, PK], F32))
        loaded, turned = sem("loaded"), sem("turned")
        block = es.enter_context(stage_block(nc))

        @block.sync
        def _(sp):
            for h in range(PH):
                sp.dma_start(nat[:, h, :, :], subkeys[h].rearrange("a e k -> e a k")).then_inc(loaded, 16)

        @block.tensor
        def _(pe):
            pe.wait_ge(loaded, 16 * PH)
            for h in range(PH):
                last = nc.tensor.transpose(ps[:, h, :], nat[:, h, :, :].rearrange("e a k -> e (a k)"), n.ident)
            last.then_inc(turned, 1)

        @block.vector
        def _(dve):
            dve.wait_ge(turned, 1)
            nc.vector.tensor_copy(sk[:, :, :], ps[:, :, :])


def stage_experts(nc, tag, n, u, v, qT, sk, h2, x1, x1_dram, y_prompt, y_sample):
    R = 8
    RUNS = PICKS // R
    PARTS = 4
    G = 2 * PH
    LOW = -3e38
    with ExitStack() as es:
        sb = lambda name, shape, dt=F32: es.enter_context(nc.sbuf_tensor(f"{tag}_{name}", shape, dt))
        sem = lambda name: new_sem(nc, es, f"{tag}_{name}")
        eid, gate = sb("eid", [P, TILES + 1, PICKS], I32), sb("gate", [P, TILES + 1, PICKS])
        eids, gates = sb("eids", [P, NS], I32), sb("gates", [P, NS])
        iota = sb("iota", [P, TOPK])
        qs = sb("qs", [P, PH, P])
        s0 = x1[:, TILES, :].rearrange("p (g k) -> p g k", k=PK)
        s1 = sb("s1", [P, G, PK])
        val, idx, idf = sb("val", [P, PH, 2, TOPK]), sb("idx", [P, PH, 2, TOPK], U32), sb("idf", [P, PH, 2, TOPK])
        top, pos = sb("top", [P, PH, TOPK]), sb("pos", [P, PH, TOPK], U32)
        part, parf = sb("part", [P, 2, PICKS], U32), sb("parf", [P, 2, PICKS])
        e01, ef = sb("e01", [P, 2, PICKS]), sb("ef", [P, PICKS])
        sm = sb("sm", [P, PH])
        ring = sb("ring", [P, R, D])
        slot_ids = sb("slot_ids", [P, R], I32)
        onehot = sb("onehot", [NS, NS * P])
        dot8 = sb("dot8", [P, R])
        dots, dotb = sb("dots", [P, TILES, PICKS]), sb("dotb", [P, NS])
        diag = sb("diag", [P, NS * NS])
        ps = es.enter_context(nc.psum_tensor(tag + "_ps", [P, 2, D], F32))
        ps_s = ps[:, 0, :].rearrange("p (g k) -> p g k", k=PK)
        ps_t = ps[:, 1, 0:2 * NS].rearrange("p (a b) -> p a b", b=NS)
        iota_loaded, staged, scored, shifted, exped, routed, turned, sample_routed = (
            sem("iota_loaded"), sem("staged"), sem("scored"), sem("shifted"), sem("exped"), sem("routed"), sem("turned"),
            sem("sample_routed"))
        landed = [sem(f"landed{i}") for i in range(R)]
        onehot_loaded, x1_loaded, idx_ready, started, used, spread, dotted, gelued, weighted, summed, added, stored = (
            sem("onehot_loaded"), sem("x1_loaded"), sem("idx_ready"), sem("started"), sem("used"), sem("spread"),
            sem("dotted"), sem("gelued"), sem("weighted"), sem("summed"), sem("added"), sem("stored"))
        block = es.enter_context(stage_block(nc))
        HALF_USES = TILES * RUNS + 1

        @block.gpsimd
        def _(pool):
            def gather(table, ids, s, number):
                pool.wait_ge(used, number + 1)
                nc.gpsimd.tensor_copy(slot_ids[:, s:s + 1], ids).then_inc(idx_ready, 1)
                pool.wait_ge(idx_ready, number + 1)
                pool.sem_inc(started, 1)
                nc.gpsimd.indirect_dma_start(ring[:, s, :], None, table, bass.IndirectOffsetOnAxis(slot_ids[:, s:s + 1], 0)
                                             ).then_inc(landed[s], 16)

            for a, table in enumerate((u, v)):
                first = a * HALF_USES * R
                with pool.Fori(0, TILES) as t:
                    if a == 0:
                        pool.wait_ge(routed, t + 1)
                        pool.sem_inc(started, 1)
                    with pool.Fori(0, RUNS) as i:
                        for s in range(R):
                            gather(table, eid[:, bass.ds(t, 1), bass.ds(i * R + s, 1)].rearrange("p o k -> p (o k)"), s,
                                   t * (RUNS * R) + i * R + (first + s))
                if a == 0:
                    pool.wait_ge(sample_routed, 1)
                for s in range(R):
                    gather(table, eids[:, s:s + 1], s, first + TILES * RUNS * R + s)

        @block.tensor
        def _(pe):
            def score(t, rows):
                pe.wait_ge(staged, t + 1)
                for h in range(PH):
                    for a in range(2):
                        last = nc.tensor.matmul(ps_s[0:rows, a * PH + h, :], qs[64 * a:64 * a + 64, h, 0:rows],
                                                sk[64 * a:64 * a + 64, h, :], start=True, stop=True)
                last.then_inc(scored, 1)

            with pe.Fori(0, TILES) as t:
                score(t, P)
            score(TILES, NS)
            pe.wait_ge(routed, TILES + 1)
            nc.tensor.transpose(ps_t[:, 0, :], ef[0:NS, :], n.ident[0:NS, 0:NS])
            nc.tensor.transpose(ps_t[:, 1, :], gate[0:NS, TILES, :], n.ident[0:NS, 0:NS]).then_inc(turned, 1)
            pe.wait_ge(onehot_loaded, 16)
            pe.wait_ge(sample_routed, 1)
            for b in range(NS):
                if b >= 2:
                    pe.wait_ge(dotted, b - 1)
                for c in range(4):
                    last = nc.tensor.matmul(ps[:, b % 2, c * 512:(c + 1) * 512], onehot[:, b * P:(b + 1) * P],
                                            h2[0:NS, TILES, c * 512:(c + 1) * 512], start=True, stop=True)
                last.then_inc(spread, 1)
            pe.wait_ge(weighted, 1)
            for b in range(NS):
                pe.wait_ge(landed[b], 2 * HALF_USES * 16)
                for c in range(4):
                    last = nc.tensor.matmul(ps[0:NS, 0, c * 512:(c + 1) * 512], diag[:, b * NS:(b + 1) * NS],
                                            ring[:, b, c * 512:(c + 1) * 512], start=(b == 0), stop=(b == NS - 1))
            last.then_inc(summed, 1)

        @block.scalar
        def _(act):
            nc.scalar.copy(qs[:, :, :], qT[:, :, 0:P]).then_inc(staged, 1)
            with act.Fori(0, TILES - 1) as t:
                act.wait_ge(shifted, t + 1)
                g = gate[:, bass.ds(t, 1), :].rearrange("p o k -> p (o k)")
                nc.scalar.activation(g, g, ACT.Exp).then_inc(exped, 1)
                nc.scalar.copy(qs[:, :, :], qT[:, :, bass.ds(t * P + P, P)]).then_inc(staged, 1)
            act.wait_ge(shifted, TILES)
            nc.scalar.activation(gate[:, TILES - 1, :], gate[:, TILES - 1, :], ACT.Exp).then_inc(exped, 1)
            nc.scalar.copy(qs[:, :, 0:NS], qT[:, :, SEQ:T]).then_inc(staged, 1)
            act.wait_ge(shifted, TILES + 1)
            nc.scalar.activation(gate[0:NS, TILES, :], gate[0:NS, TILES, :], ACT.Exp).then_inc(exped, 1)
            act.wait_ge(dotted, NS)
            nc.scalar.activation(dots[:, :, :], dots[:, :, :], ACT.Gelu)
            nc.scalar.activation(dotb[:, :], dotb[:, :], ACT.Gelu).then_inc(gelued, 1)

        @block.vector
        def _(dve):
            def top16(scores, spare, v, i):
                for src, lo in ((scores, 0), (spare, 8)):
                    for j in range(len(v)):
                        nc.vector.max(v[j][:, lo:lo + 8], src[j])
                    dve.drain()
                    for j in range(len(v)):
                        nc.vector.max_index(i[j][:, lo:lo + 8], v[j][:, lo:lo + 8], src[j])
                        if lo == 0:
                            nc.vector.match_replace(spare[j], v[j][:, 0:8], src[j], LOW)
                    dve.drain()

            def route(p, t, rows, g, out):
                r = slice(0, rows)
                cand = s0[r].rearrange("p g k -> p (g k)").rearrange("p (h a b) -> p h a b", h=PH, a=TOPK)
                gh = g.rearrange("p (h k) -> p h k", h=PH)
                if p < 2:
                    if p == 0:
                        dve.wait_ge(scored, t + 1)
                        nc.vector.tensor_copy(s0[r], ps_s[r])
                        dve.drain()
                    js = range(p * PH, (p + 1) * PH)
                    top16([s0[r, j % 2 * PH + j // 2, :] for j in js], [s1[r, j, :] for j in js],
                          [val[r, j // 2, j % 2, :] for j in js], [idx[r, j // 2, j % 2, :] for j in js])
                elif p == 2:
                    nc.vector.tensor_copy(idf[r], idx[r])
                    nc.vector.tensor_tensor(cand, val[r, :, 0, :].unsqueeze(3).to_broadcast([rows, PH, TOPK, TOPK]),
                                            val[r, :, 1, :].unsqueeze(2).to_broadcast([rows, PH, TOPK, TOPK]), ALU.add)
                    dve.drain()
                    c1 = s0[r].rearrange("p g k -> p (g k)").rearrange("p (h c) -> p h c", h=PH)
                    c2 = s1[r].rearrange("p g k -> p (g k)").rearrange("p (h c) -> p h c", h=PH)
                    top16([c1[:, h, :] for h in range(PH)], [c2[:, h, :] for h in range(PH)],
                          [top[r, h, :] for h in range(PH)], [pos[r, h, :] for h in range(PH)])
                    nc.vector.tensor_tensor(gh, top[r], top[r, :, 0:1].to_broadcast([rows, PH, TOPK]),
                                            ALU.subtract).then_inc(shifted, 1)
                else:
                    flat = pos[r].rearrange("p h k -> p (h k)")
                    nc.vector.tensor_scalar(part[r, 0, :], flat, 4, None, ALU.logical_shift_right)
                    nc.vector.tensor_scalar(part[r, 1, :], flat, 15, None, ALU.bitwise_and)
                    dve.drain()
                    nc.vector.tensor_copy(parf[r], part[r])
                    dve.drain()
                    for a in range(2):
                        hot = s0[r].rearrange("p g k -> p (g k)").rearrange("p (h k c) -> p h k c", h=PH, k=TOPK)
                        hot3 = s0[r].rearrange("p g k -> p (g k)").rearrange("p (k c) -> p k c", c=TOPK)
                        nc.vector.tensor_tensor(hot3, parf[r, a, :].unsqueeze(2).to_broadcast([rows, PICKS, TOPK]),
                                                iota[r].unsqueeze(1).to_broadcast([rows, PICKS, TOPK]), ALU.is_equal)
                        dve.drain()
                        nc.vector.tensor_tensor(hot, hot, idf[r, :, a, :].unsqueeze(2).to_broadcast([rows, PH, TOPK, TOPK]),
                                                ALU.mult)
                        dve.drain()
                        nc.vector.tensor_reduce(e01[r, a, :], hot3, AX.X, ALU.add)
                        dve.drain()
                    nc.vector.scalar_tensor_tensor(ef[r], e01[r, 0, :], float(PK), e01[r, 1, :], ALU.mult, ALU.add)
                    dve.drain()
                    dve.wait_ge(exped, t + 1)
                    nc.vector.tensor_scalar(out, ef[r], 0.0, None, ALU.add)
                    dve.drain()
                    nc.vector.tensor_reduce(sm[r], gh, AX.X, ALU.add)
                    dve.drain()
                    nc.vector.reciprocal(sm[r], sm[r])
                    dve.drain()
                    nc.vector.tensor_tensor(gh, gh, sm[r].unsqueeze(2).to_broadcast([rows, PH, TOPK]), ALU.mult
                                            ).then_inc(routed, 1)
                    dve.drain()

            def dot(p, t):
                with dve.Fori(0, RUNS // PARTS) as i:
                    run0 = p * (RUNS // PARTS)
                    for s in range(R):
                        dve.wait_ge(landed[s], t * (RUNS * 16) + i * 16 + (run0 + 1) * 16)
                        nc.vector.scalar_tensor_tensor(ring[:, s, :], ring[:, s, :], 1.0, h2[:, bass.ds(t, 1), :].rearrange("p o d -> p (o d)"),
                                                       ALU.mult, ALU.mult, accum_out=dot8[:, s:s + 1]).then_inc(used, 1)
                    dve.drain()
                    d8 = dots[:, bass.ds(t, 1), bass.ds(i * R + run0 * R, R)].rearrange("p o k -> p (o k)")
                    nc.vector.tensor_copy(d8, dot8[:, :])
                    dve.drain()

            last_tile = TILES - 1
            dve.wait_ge(iota_loaded, 16)
            for p in range(PARTS):
                route(p, 0, P, gate[:, 0, :], eid[:, 0, :])
            dve.sem_inc(used, R)
            with dve.Fori(0, TILES - 1) as t:
                for p in range(PARTS):
                    route(p, t + 1, P, gate[:, bass.ds(t + 1, 1), :].rearrange("p o k -> p (o k)"),
                          eid[:, bass.ds(t + 1, 1), :].rearrange("p o k -> p (o k)"))
                    dot(p, t)
            for p in range(PARTS):
                route(p, TILES, NS, gate[0:NS, TILES, :], eid[0:NS, TILES, :])
                if p == PARTS - 1:
                    dve.wait_ge(turned, 1)
                    nc.vector.tensor_copy(eids[:, :], ps_t[:, 0, :])
                    nc.vector.tensor_copy(gates[:, :], ps_t[:, 1, :])
                    dve.drain()
                    dve.sem_inc(sample_routed, 1)
                dot(p, last_tile)
            for b in range(NS):
                dve.wait_ge(landed[b], HALF_USES * 16)
                dve.wait_ge(spread, b + 1)
                nc.vector.scalar_tensor_tensor(ring[:, b, :], ring[:, b, :], 1.0, ps[:, b % 2, :], ALU.mult, ALU.mult,
                                               accum_out=dotb[:, b:b + 1]).then_inc(dotted, 1)
                dve.drain()
                dve.sem_inc(used, 1)
            nc.vector.memset(diag[:, :], 0.0)
            dve.drain()
            dve.wait_ge(gelued, 1)
            nc.vector.tensor_tensor(dots[:, :, :], dots[:, :, :], gate[:, 0:TILES, :], ALU.mult)
            nc.vector.tensor_tensor(diag[:, 0:NS * NS:NS + 1], dotb[:, :], gates[:, :], ALU.mult).then_inc(weighted, 1)
            dve.drain()
            dve.wait_ge(x1_loaded, 16 * (TILES + 1))
            with dve.Fori(0, TILES) as t:
                x = x1[:, bass.ds(t, 1), :].rearrange("p o d -> p (o d)")
                with dve.Fori(0, RUNS) as i:
                    for s in range(R):
                        dve.wait_ge(landed[s], t * (RUNS * 16) + i * 16 + (HALF_USES + 1) * 16)
                        nc.vector.scalar_tensor_tensor(
                            x, ring[:, s, :], dots[:, bass.ds(t, 1), bass.ds(i * R + s, 1)].rearrange("p o k -> p (o k)"),
                            x, ALU.mult, ALU.add).then_inc(used, 1)
                        dve.drain()
                dve.sem_inc(added, 1)
            dve.wait_ge(summed, 1)
            nc.vector.tensor_tensor(x1[0:NS, TILES, :], x1[0:NS, TILES, :], ps[0:NS, 0, :], ALU.add).then_inc(added, 1)

        @block.sync
        def _(sp):
            sp.dma_start(iota[:, :], n.c["peer"]).then_inc(iota_loaded, 16)
            sp.dma_start(onehot[:, :], n.c["onehot"]).then_inc(onehot_loaded, 16)
            for t in range(TILES):
                sp.dma_start(x1[:, t, :], x1_dram[t * P:(t + 1) * P, :]).then_inc(x1_loaded, 16)
            sp.wait_ge(routed, TILES + 1)
            sp.dma_start(x1[0:NS, TILES, :], x1_dram[SEQ:T, :]).then_inc(x1_loaded, 16)
            for t in range(TILES):
                sp.wait_ge(added, t + 1)
                sp.dma_start(y_prompt[t * P:(t + 1) * P, :], x1[:, t, :]).then_inc(stored, 16)
            sp.wait_ge(added, TILES + 1)
            sp.dma_start(y_sample, x1[0:NS, TILES, :]).then_inc(stored, 16)
            sp.wait_ge(stored, 16 * (TILES + 1))


OUTPUTS = [("y_prompt", (1, SEQ, D)), ("y_sample", (NS, 1, D)),
           ("p_cmp_k", (1, 1, SEQ, NG, P)), ("p_cmp_v", (1, 1, SEQ, NG, P)), ("p_sel_k", (1, 1, SEQ, NG, P)),
           ("p_sel_v", (1, 1, SEQ, NG, P)), ("p_win_k", (1, 1, WIN, NG, P)), ("p_win_v", (1, 1, WIN, NG, P)),
           ("p_ret", (1, 1, RH, P, RDV)), ("p_mem_k", (1, 1, NM, MH, MD)), ("p_mem_v", (1, 1, NM, MH, MD)),
           ("s_cmp_k", (1, NS, 1, NG, P)), ("s_cmp_v", (1, NS, 1, NG, P)), ("s_sel_k", (1, NS, 1, NG, P)),
           ("s_sel_v", (1, NS, 1, NG, P)), ("s_win_k", (1, NS, WIN, NG, P)), ("s_win_v", (1, NS, WIN, NG, P)),
           ("s_ret", (1, NS, RH, P, RDV))]


def trunk(nc, i, c, o):
    n = Net()
    nc._stage_sems = []
    n.c, n.i, n.o = c, i, o
    with ExitStack() as es:
        n.base = es.enter_context(nc.sbuf_tensor("base", [P, 2 * P], F32))
        n.ident, n.ones = n.base[:, 0:P], n.base[:, P:2 * P]
        nc._eps_tile = es.enter_context(nc.sbuf_tensor("eps", [P, 1], F32))
        n.table = es.enter_context(nc.sbuf_tensor("table", [1, NS * PAGES], I32))
        scratch = nc.dram_tensor("gate_rows", (NS, 3 * NH), F32, kind="Internal").ap()
        x1d = nc.dram_tensor("x_after_attention", (T, D), F32, kind="Internal").ap()
        stage_load_consts(nc, n)
        front = es.enter_context(ExitStack())
        hT = front.enter_context(nc.sbuf_tensor("hT", [P, KD, T], F32))
        oT = front.enter_context(nc.sbuf_tensor("oT", [P, 24, T], F32))
        w_in = i["w_in"][0]
        xp = i["x_prompt"][0]
        xs = i["x_sample"].rearrange("b o d -> (b o) d")
        tiles = [(xp[t * P:(t + 1) * P, :], P, t * P) for t in range(TILES)] + [(xs, NS, SEQ)]
        stage_norm(nc, "na", tiles, i["norm_attn"][0], hT, n.ident)
        with nc.sbuf_tensor("Zr", [P, 24, T], F32) as Z:
            stage_project(nc, "pr", w_in, C_RQ, 24, hT, Z, 0, finish=Finish(
                "rope", [(1, [(0, 1, False, (0, 0))]), (4, [(1, 1, True, (0, 0))]), (7, [(5, 1, False, (0, 0))])],
                n.ones, table=c["rope_ret"]))
            stage_retention(nc, "rt", n, Z, oT, o["p_ret"][0, 0])
            stage_retention_sample(nc, "rs", n, Z, oT, i["state_ret"][0], o["s_ret"][0])
            stage_retention_gate(nc, "rg", n, Z, oT, i["ret_gn"][0])
        with ExitStack() as nsa:
            sb = lambda name, shape, dt=F32: nsa.enter_context(nc.sbuf_tensor(name, shape, dt))
            rows, srows = sb("rows", [P, 12, TILES, P]), sb("srows", [NS, 12, P])
            gt, gts, grow = sb("gt", [P, TILES, 3 * NH]), sb("gts", [NS, 3 * NH]), sb("grow", [ROWS, 3])
            ck, cv = sb("ck", [P, 288]), sb("cv", [P, 288])
            cvp, cvs = sb("cvp", [NCMP, NG, P]), sb("cvs", [P, 2, P])
            Z = sb("Zn", [P, 20, T])
            stage_gates(nc, "ga", n, hT, w_in, gt, gts, scratch, grow)
            kn = i["nsa_k_norm"][0]
            stage_project(nc, "pn", w_in, C_NQ, 20, hT, Z, 0, finish=Finish(
                "norm_rope", [(1, [(0, 1, False, (0, 0))]), (4, [(1, 1, True, (0, 0))]),
                              (2, [(5, 2, True, (1, 1)), (6, 2, False, (0, 0))]), (1, [(9, 1, True, (3, 0))])],
                n.ones, gains=[i["nsa_q_norm"][0], kn[0], kn[1], kn[2]], table=c["rope_nsa"]))
            stage_rows(nc, "ro", Z, 8, 12, n.ident, rows, srows)
            stage_compress(nc, "ck", n, Z, 8, i["cache_cmp_k"][0], i["cmp_pos_k"][0], i["cmp_w_k"][0], ck)
            stage_compress(nc, "cv", n, Z, 10, i["cache_cmp_v"][0], i["cmp_pos_v"][0], i["cmp_w_v"][0], cv)
            stage_cv_rows(nc, "cr", n, cv, cvp, cvs)
            for g in range(NG):
                stage_nsa_group(nc, f"ng{g}", n, g, Z, rows, srows, ck, cvp, gt, oT)
            sample_nsa(nc, n, Z, ck, cvs, srows, grow, oT)
        with ExitStack() as mem:
            sb = lambda name, shape, dt=F32: mem.enter_context(nc.sbuf_tensor(name, shape, dt))
            mp = i["mem_prompt"][0]
            Z = sb("Zm", [P, 8, T])
            halved = lambda gain: [gain[0:P], gain[P:MD]]
            stage_project(nc, "pm", w_in, C_MQ, 8, hT, Z, 0, finish=Finish(
                "norm", [(1, [(0, 1, False, (0, 0))]), (3, [(1, 1, True, (0, 0))])], n.ones,
                gains=halved(i["mem_q_norm"][0]), tail=True))
            M = sb("M", [P, 16, NM])
            with nc.sbuf_tensor("hm", [P, KD, NM], F32) as hm:
                stage_norm(nc, "nm", [(mp[t * P:(t + 1) * P, :], P, t * P) for t in range(2)], i["norm_mem"][0], hm, n.ident)
                stage_project(nc, "pk", i["w_mem_kv"][0], 0, 16, hm, M, 0, cols=NM, finish=Finish(
                    "norm", [(1, [(0, 1, False, (0, 0))]), (4, [(1, 1, True, (0, 0))]), (3, [(5, 1, False, (0, 0))])],
                    n.ones, gains=halved(i["mem_k_norm"][0])))
            krows, vrows = sb("krows", [P, 2, MH * MD]), sb("vrows", [P, 2, MH * MD])
            stage_memory_rows(nc, "m1", n, M, 0, krows, o["p_mem_k"][0, 0])
            stage_memory_rows(nc, "m2", n, M, 8, vrows, o["p_mem_v"][0, 0])
            stage_memory_attend(nc, "ma", n, Z, M, vrows, oT)
            sample_memory(nc, n, Z, oT)

        mT = front.enter_context(nc.sbuf_tensor("mT", [P, KD, T], F32))
        stage_merge(nc, "mg", n, hT, oT, w_in, i["w_branch"][0], mT)
        stage_project(nc, "po", i["w_out"][0], 0, KD, mT, hT, 0)
        with nc.sbuf_tensor("xa", [P, TILES + 1, D], F32) as xa:
            stage_residual(nc, "re", n, hT, tiles, xa, x1d)
        front.close()
        x1, h2 = [es.enter_context(nc.sbuf_tensor(name, [P, TILES + 1, D], F32)) for name in ("x1", "h2")]
        qT = es.enter_context(nc.sbuf_tensor("qT", [P, PH, T], F32))
        sk = es.enter_context(nc.sbuf_tensor("sk", [P, PH, PK], F32))
        with nc.sbuf_tensor("h2T", [P, KD, T], F32) as h2T:
            x1tiles = [(x1d[t * P:t * P + rows, :], rows, t * P) for t, (_s, rows, _c) in enumerate(tiles)]
            stage_norm(nc, "nf", x1tiles, i["norm_ffn"][0], h2T, n.ident, keep=h2)
            stage_project(nc, "pq", i["peer_wq"][0], 0, PH, h2T, qT, 0)
        stage_subkeys(nc, "su", n, i["peer_subkeys"][0], sk)
        stage_experts(nc, "ex", n, i["peer_u"][0], i["peer_v"][0], qT, sk, h2, x1, x1d, o["y_prompt"][0],
                      o["y_sample"].rearrange("b o d -> (b o) d"))


def kernel(**inputs):
    import concourse.bacc as bacc
    from concourse.bass_utils import run_bass_kernel_spmd

    nc = bacc.Bacc("TRN2", target_bir_lowering=False, num_devices=1)
    arrays, ins, consts, outs = {}, {}, {}, {}
    for name, a in inputs.items():
        a = np.ascontiguousarray(a)
        arrays["in_" + name] = a
        ins[name] = nc.dram_tensor("in_" + name, a.shape, mybir.dt.from_np(a.dtype), kind="ExternalInput").ap()
    for name, a in host_constants().items():
        arrays["const_" + name] = a
        consts[name] = nc.dram_tensor("const_" + name, a.shape, F32, kind="ExternalInput").ap()
    for name, shape in OUTPUTS:
        outs[name] = nc.dram_tensor("out_" + name, shape, F32, kind="ExternalOutput").ap()
    trunk(nc, ins, consts, outs)
    r = run_bass_kernel_spmd(nc, [arrays], core_ids=[0])
    return tuple(r.results[0]["out_" + name] for name, _ in OUTPUTS)
```
